# Optimizing a Trainium2 kernel written in Bass

```python
import jax, jax.numpy as jnp
from jax import lax
import numpy as np
import math

D_MODEL = 1024
BATCH = 1
SEQ = 256
DEPTH = 2

D_CONV = D_MODEL // 2
D_POOL = D_MODEL // 2
CONV_K = 31
POOL_WINDOWS = (2, 4, 8, 16)
N_POOL_GROUPS = len(POOL_WINDOWS)
POOL_GROUP = D_POOL // N_POOL_GROUPS
POOL_OUT_GROUP = D_MODEL // N_POOL_GROUPS
N_BRANCHES = 2
D_IN = 2 * D_CONV + D_POOL + N_BRANCHES * D_MODEL

N_EXPERT_GROUPS = 4
EXPERTS_PER_GROUP = 8
N_EXPERTS = N_EXPERT_GROUPS * EXPERTS_PER_GROUP
TOP_K = 2
D_EXPERT = D_MODEL // 4

N_MOD = 6
EPS = 1e-6


def rms_norm(x, g):
    xf = x.astype(jnp.float32)
    y = xf * lax.rsqrt(jnp.mean(xf * xf, axis=-1, keepdims=True) + EPS)
    return (y * g.astype(jnp.float32)).astype(x.dtype)

def layer_norm(x, g, b):
    xf = x.astype(jnp.float32)
    mu = jnp.mean(xf, axis=-1, keepdims=True)
    var = jnp.mean(jnp.square(xf - mu), axis=-1, keepdims=True)
    y = (xf - mu) * lax.rsqrt(var + EPS)
    return (y * g.astype(jnp.float32) + b.astype(jnp.float32)).astype(x.dtype)

def modulate(h, shift, scale):
    return h * (1 + scale[:, None, :]) + shift[:, None, :]

def conformer_conv_branch(u, conv_w, conv_b, ln_g, ln_b, w_pw, b_pw):
    a, g = jnp.split(u, 2, axis=-1)
    v = a * jax.nn.sigmoid(g)
    v = lax.conv_general_dilated(
        v, conv_w[:, None, :], window_strides=(1,), padding=[(CONV_K - 1, 0)],
        dimension_numbers=("NWC", "WIO", "NWC"), feature_group_count=D_CONV) + conv_b
    v = jax.nn.silu(layer_norm(v, ln_g, ln_b))
    return v @ w_pw + b_pw

def causal_window_mean(u, w):
    s_len = u.shape[1]
    cs = jnp.cumsum(u.astype(jnp.float32), axis=1)
    shifted = jnp.pad(cs, ((0, 0), (w, 0), (0, 0)))[:, :s_len]
    count = jnp.minimum(jnp.arange(1, s_len + 1), w).astype(jnp.float32)
    return ((cs - shifted) / count[None, :, None]).astype(u.dtype)

def pool_branch(u, pool_w, pool_scale):
    b, s, _ = u.shape
    ug = u.reshape(b, s, N_POOL_GROUPS, POOL_GROUP)
    pooled = jnp.stack([causal_window_mean(ug[:, :, gi], w)
                        for gi, w in enumerate(POOL_WINDOWS)], axis=2) - ug
    y = jnp.einsum("bsgc,gco->bsgo", pooled, pool_w).reshape(b, s, D_MODEL)
    return y * pool_scale

def hierarchical_moe(h, w_rg, b_rg, w_re, b_re, w_g, w_u, w_d):
    b, s, d = h.shape
    t = h.reshape(b * s, d)
    n_tok = t.shape[0]
    group_probs = jax.nn.softmax((t @ w_rg + b_rg).astype(jnp.float32), axis=-1)
    p_group, g_idx = lax.top_k(group_probs, 1)
    exp_logits = (t @ w_re + b_re).astype(jnp.float32).reshape(n_tok, N_EXPERT_GROUPS, EXPERTS_PER_GROUP)
    in_group = jnp.take_along_axis(exp_logits, g_idx[:, :, None], axis=1)[:, 0]
    p_exp, e_idx = lax.top_k(jax.nn.softmax(in_group, axis=-1), TOP_K)
    weights = p_group * p_exp / jnp.sum(p_exp, axis=-1, keepdims=True)
    expert_id = g_idx * EXPERTS_PER_GROUP + e_idx
    combine = jnp.sum(jax.nn.one_hot(expert_id, N_EXPERTS, dtype=jnp.float32) * weights[..., None],
                      axis=1).astype(h.dtype)
    out = jnp.zeros_like(t)
    for gi in range(N_EXPERT_GROUPS):
        sl = slice(gi * EXPERTS_PER_GROUP, (gi + 1) * EXPERTS_PER_GROUP)
        act = jax.nn.silu(jnp.einsum("td,edh->teh", t, w_g[sl])) * jnp.einsum("td,edh->teh", t, w_u[sl])
        out = out + jnp.einsum("teh,ehd->td", act * combine[:, sl, None], w_d[sl])
    return out.reshape(b, s, d)

def first_inputs(seed: int = 0) -> dict:
    key = jax.random.key(seed)
    ks = jax.random.split(key, 24)
    f32 = jnp.float32
    nrm = lambda k, shape, scale: (jax.random.normal(k, shape, f32) * scale)
    return {
        "x": nrm(ks[0], (BATCH, SEQ, D_MODEL), 1.0),
        "c": nrm(ks[1], (BATCH, D_MODEL), 1.0),
        "mixer_norm_g": 1.0 + nrm(ks[2], (DEPTH, D_MODEL), 0.05),
        "w_ada": nrm(ks[3], (DEPTH, D_MODEL, N_MOD * D_MODEL), 0.5 * D_MODEL ** -0.5),
        "b_ada": nrm(ks[4], (DEPTH, N_MOD * D_MODEL), 0.02),
        "w_in": nrm(ks[5], (DEPTH, D_MODEL, D_IN), D_MODEL ** -0.5),
        "conv_w": nrm(ks[6], (DEPTH, CONV_K, D_CONV), CONV_K ** -0.5),
        "conv_b": nrm(ks[7], (DEPTH, D_CONV), 0.02),
        "conv_ln_g": 1.0 + nrm(ks[8], (DEPTH, D_CONV), 0.05),
        "conv_ln_b": nrm(ks[9], (DEPTH, D_CONV), 0.02),
        "w_conv_out": nrm(ks[10], (DEPTH, D_CONV, D_MODEL), D_CONV ** -0.5),
        "b_conv_out": nrm(ks[11], (DEPTH, D_MODEL), 0.02),
        "pool_w": nrm(ks[12], (DEPTH, N_POOL_GROUPS, POOL_GROUP, POOL_OUT_GROUP), POOL_GROUP ** -0.5),
        "pool_scale": 1.0 + nrm(ks[13], (DEPTH, D_MODEL), 0.1),
        "w_out": nrm(ks[14], (DEPTH, D_MODEL, D_MODEL), D_MODEL ** -0.5),
        "ffn_norm_g": 1.0 + nrm(ks[15], (DEPTH, D_MODEL), 0.05),
        "w_router_group": nrm(ks[16], (DEPTH, D_MODEL, N_EXPERT_GROUPS), D_MODEL ** -0.5),
        "b_router_group": nrm(ks[17], (DEPTH, N_EXPERT_GROUPS), 0.01),
        "w_router_expert": nrm(ks[18], (DEPTH, D_MODEL, N_EXPERTS), D_MODEL ** -0.5),
        "b_router_expert": nrm(ks[19], (DEPTH, N_EXPERTS), 0.01),
        "w_expert_gate": nrm(ks[20], (DEPTH, N_EXPERTS, D_MODEL, D_EXPERT), D_MODEL ** -0.5),
        "w_expert_up": nrm(ks[21], (DEPTH, N_EXPERTS, D_MODEL, D_EXPERT), D_MODEL ** -0.5),
        "w_expert_down": nrm(ks[22], (DEPTH, N_EXPERTS, D_EXPERT, D_MODEL), D_EXPERT ** -0.5),
        "final_norm_g": 1.0 + nrm(ks[23], (D_MODEL,), 0.05),
    }

def first_block(x, c, mixer_norm_g, w_ada, b_ada, w_in, conv_w, conv_b, conv_ln_g, conv_ln_b,
              w_conv_out, b_conv_out, pool_w, pool_scale, w_out, ffn_norm_g,
              w_router_group, b_router_group, w_router_expert, b_router_expert,
              w_expert_gate, w_expert_up, w_expert_down, final_norm_g):
    c_act = jax.nn.silu(c)
    for l in range(DEPTH):
        mod = c_act @ w_ada[l] + b_ada[l]
        sh1, sc1, g1, sh2, sc2, g2 = jnp.split(mod, N_MOD, axis=-1)
        h = modulate(rms_norm(x, mixer_norm_g[l]), sh1, sc1)
        proj = h @ w_in[l]
        u_conv = proj[..., :2 * D_CONV]
        u_pool = proj[..., 2 * D_CONV:2 * D_CONV + D_POOL]
        gate_a, gate_b = jnp.split(jax.nn.sigmoid(proj[..., 2 * D_CONV + D_POOL:]), N_BRANCHES, axis=-1)
        y_a = conformer_conv_branch(u_conv, conv_w[l], conv_b[l], conv_ln_g[l], conv_ln_b[l],
                                    w_conv_out[l], b_conv_out[l])
        y_b = pool_branch(u_pool, pool_w[l], pool_scale[l])
        mixed = gate_a * y_a + gate_b * y_b
        x = x + g1[:, None, :] * (mixed @ w_out[l])
        h2 = modulate(rms_norm(x, ffn_norm_g[l]), sh2, sc2)
        x = x + g2[:, None, :] * hierarchical_moe(h2, w_router_group[l], b_router_group[l],
                                                  w_router_expert[l], b_router_expert[l],
                                                  w_expert_gate[l], w_expert_up[l], w_expert_down[l])
    return rms_norm(x, final_norm_g)


HEAD_DIM = 64
DIFF_HEADS = 4
DIFF_VDIM = 2 * HEAD_DIM
SB_HEADS = 8
DIFF_WIDTH = DIFF_HEADS * DIFF_VDIM
SB_WIDTH = SB_HEADS * HEAD_DIM
MIX_WIDTH = DIFF_WIDTH + SB_WIDTH
DIFF_QK = DIFF_HEADS * 2 * HEAD_DIM
SB_QK = SB_HEADS * HEAD_DIM
IN_WIDTH = 2 * DIFF_QK + DIFF_WIDTH + 2 * SB_QK + SB_WIDTH
Q_BLOCK = 128

PEER_HEADS = 8
N_KEYS = 128
N_EXPERTS_2 = N_KEYS * N_KEYS
PEER_TOPK = 16
HALF_Q = 128
QUERY_DIM = 2 * HALF_Q
TOKEN_CHUNK = 128

DEEPNORM_ALPHA = (2.0 * DEPTH) ** 0.25
DEEPNORM_BETA = (8.0 * DEPTH) ** -0.25
LN_EPS = 1e-5
RMS_EPS = 1e-5


def layer_norm_2(h, g, b):
    hf = h.astype(jnp.float32)
    mu = jnp.mean(hf, axis=-1, keepdims=True)
    var = jnp.mean(jnp.square(hf - mu), axis=-1, keepdims=True)
    y = (hf - mu) * lax.rsqrt(var + LN_EPS) * g.astype(jnp.float32) + b.astype(jnp.float32)
    return y.astype(h.dtype)

def alibi_slopes():
    return jnp.asarray([2.0 ** (-8.0 * (i + 1) / DIFF_HEADS) for i in range(DIFF_HEADS)], jnp.float32)

def token_mixer(h, w_in, lq1, lk1, lq2, lk2, subln_g, w_o, layer):
    B, S, _ = h.shape
    proj = h @ w_in
    s1 = DIFF_QK
    s2 = s1 + DIFF_QK
    s3 = s2 + DIFF_WIDTH
    s4 = s3 + SB_QK
    s5 = s4 + SB_QK
    dq, dk, dv, sq, sk, sv = jnp.split(proj, [s1, s2, s3, s4, s5], axis=-1)
    dq = dq.reshape(B, S, DIFF_HEADS, 2, HEAD_DIM).transpose(0, 2, 3, 1, 4)
    dk = dk.reshape(B, S, DIFF_HEADS, 2, HEAD_DIM).transpose(0, 2, 3, 1, 4)
    dv = dv.reshape(B, S, DIFF_HEADS, DIFF_VDIM).transpose(0, 2, 1, 3)
    sq = sq.reshape(B, S, SB_HEADS, HEAD_DIM).transpose(0, 2, 1, 3)
    sk = sk.reshape(B, S, SB_HEADS, HEAD_DIM).transpose(0, 2, 1, 3)
    sv = sv.reshape(B, S, SB_HEADS, HEAD_DIM).transpose(0, 2, 1, 3)

    lambda_init = 0.8 - 0.6 * math.exp(-0.3 * layer)
    lam = (jnp.exp(jnp.sum(lq1.astype(jnp.float32) * lk1.astype(jnp.float32)))
           - jnp.exp(jnp.sum(lq2.astype(jnp.float32) * lk2.astype(jnp.float32)))
           + lambda_init)
    slopes = alibi_slopes()[None, :, None, None, None]
    scale = HEAD_DIM ** -0.5

    diff_out, sb_out = [], []
    for blk in range(S // Q_BLOCK):
        q0 = blk * Q_BLOCK
        kv_len = q0 + Q_BLOCK
        t_pos = q0 + jnp.arange(Q_BLOCK)
        s_pos = jnp.arange(kv_len)
        dist = (t_pos[:, None] - s_pos[None, :]).astype(jnp.float32)

        sc = jnp.einsum('bhmqd,bhmkd->bhmqk', dq[:, :, :, q0:kv_len], dk[:, :, :, :kv_len]).astype(jnp.float32) * scale
        sc = jnp.where(dist >= 0, sc - slopes * dist, -jnp.inf)
        p = jax.nn.softmax(sc, axis=-1)
        attn = p[:, :, 0] - lam * p[:, :, 1]
        diff_out.append(jnp.einsum('bhqk,bhkd->bhqd', attn.astype(dv.dtype), dv[:, :, :kv_len]))

        z = jnp.einsum('bgqd,bgkd->bgqk', sq[:, :, q0:kv_len], sk[:, :, :kv_len]).astype(jnp.float32) * scale
        strict = dist > 0
        log_fail = jnp.where(strict, jax.nn.log_sigmoid(-z), 0.0)
        log_later = lax.cumsum(log_fail, axis=3, reverse=True) - log_fail
        w = jnp.where(strict, jnp.exp(jax.nn.log_sigmoid(z) + log_later), 0.0)
        sb_out.append(jnp.einsum('bgqk,bgkd->bgqd', w.astype(sv.dtype), sv[:, :, :kv_len]))

    diff = jnp.concatenate(diff_out, axis=2).astype(jnp.float32)
    diff = diff * lax.rsqrt(jnp.mean(jnp.square(diff), axis=-1, keepdims=True) + RMS_EPS)
    diff = diff * subln_g.astype(jnp.float32) * (1.0 - lambda_init)
    diff = diff.astype(h.dtype).transpose(0, 2, 1, 3).reshape(B, S, DIFF_WIDTH)
    sb = jnp.concatenate(sb_out, axis=2).transpose(0, 2, 1, 3).reshape(B, S, SB_WIDTH)
    mixed = jnp.concatenate([diff, sb.astype(h.dtype)], axis=-1)
    return mixed @ w_o

def peer_ffn(h, w_query, sub_keys, expert_u, expert_v):
    B, S, D = h.shape
    T = B * S
    xt = h.reshape(T, D)
    q = (xt @ w_query).reshape(T, PEER_HEADS, 2, HALF_Q).astype(jnp.float32)
    scores = jnp.einsum('thpc,hpnc->thpn', q, sub_keys.astype(jnp.float32))
    top_s, top_i = lax.top_k(scores, PEER_TOPK)
    cand_s = top_s[:, :, 0, :, None] + top_s[:, :, 1, None, :]
    cand_i = top_i[:, :, 0, :, None] * N_KEYS + top_i[:, :, 1, None, :]
    cand_s = cand_s.reshape(T, PEER_HEADS, PEER_TOPK * PEER_TOPK)
    cand_i = cand_i.reshape(T, PEER_HEADS, PEER_TOPK * PEER_TOPK)
    best_s, best_pos = lax.top_k(cand_s, PEER_TOPK)
    idx = jnp.take_along_axis(cand_i, best_pos, axis=-1)
    gate = jax.nn.softmax(best_s, axis=-1)
    n_sel = PEER_HEADS * PEER_TOPK
    n_chunks = T // TOKEN_CHUNK

    def expert_chunk(args):
        xc, ic, gc = args
        u = expert_u[ic]
        act = jax.nn.gelu(jnp.einsum('cd,ced->ce', xc, u).astype(jnp.float32), approximate=False)
        v = expert_v[ic]
        return jnp.einsum('ce,ced->cd', (gc * act).astype(v.dtype), v)

    y = lax.map(expert_chunk, (xt.reshape(n_chunks, TOKEN_CHUNK, D),
                               idx.reshape(n_chunks, TOKEN_CHUNK, n_sel),
                               gate.reshape(n_chunks, TOKEN_CHUNK, n_sel)))
    return y.reshape(B, S, D).astype(h.dtype)

def second_inputs(seed: int = 0) -> dict:
    key = jax.random.key(seed)
    ks = jax.random.split(key, 16)
    f32 = jnp.float32
    beta = DEEPNORM_BETA
    col_scale = np.concatenate([np.ones(2 * DIFF_QK), np.full(DIFF_WIDTH, beta),
                                np.ones(2 * SB_QK), np.full(SB_WIDTH, beta)]).astype(np.float32)
    x = jax.random.normal(ks[0], (BATCH, SEQ, D_MODEL), f32)
    w_in = jax.random.normal(ks[1], (DEPTH, D_MODEL, IN_WIDTH), f32) * (D_MODEL ** -0.5) * jnp.asarray(col_scale)
    lam_q1 = 0.1 * jax.random.normal(ks[2], (DEPTH, HEAD_DIM), f32)
    lam_k1 = 0.1 * jax.random.normal(ks[3], (DEPTH, HEAD_DIM), f32)
    lam_q2 = 0.1 * jax.random.normal(ks[4], (DEPTH, HEAD_DIM), f32)
    lam_k2 = 0.1 * jax.random.normal(ks[5], (DEPTH, HEAD_DIM), f32)
    subln_g = 1.0 + 0.02 * jax.random.normal(ks[6], (DEPTH, DIFF_VDIM), f32)
    w_o = jax.random.normal(ks[7], (DEPTH, MIX_WIDTH, D_MODEL), f32) * (MIX_WIDTH ** -0.5) * beta
    ln1_g = 1.0 + 0.02 * jax.random.normal(ks[8], (DEPTH, D_MODEL), f32)
    ln1_b = 0.02 * jax.random.normal(ks[9], (DEPTH, D_MODEL), f32)
    w_query = jax.random.normal(ks[10], (DEPTH, D_MODEL, PEER_HEADS * QUERY_DIM), f32) * (D_MODEL ** -0.5)
    sub_keys = jax.random.normal(ks[11], (DEPTH, PEER_HEADS, 2, N_KEYS, HALF_Q), f32) * (HALF_Q ** -0.5)
    expert_u = jax.random.normal(ks[12], (DEPTH, N_EXPERTS_2, D_MODEL), f32) * (D_MODEL ** -0.5) * beta
    expert_v = jax.random.normal(ks[13], (DEPTH, N_EXPERTS_2, D_MODEL), f32) * beta
    ln2_g = 1.0 + 0.02 * jax.random.normal(ks[14], (DEPTH, D_MODEL), f32)
    ln2_b = 0.02 * jax.random.normal(ks[15], (DEPTH, D_MODEL), f32)
    return {"x": x, "w_in": w_in, "lam_q1": lam_q1, "lam_k1": lam_k1, "lam_q2": lam_q2,
            "lam_k2": lam_k2, "subln_g": subln_g, "w_o": w_o, "ln1_g": ln1_g, "ln1_b": ln1_b,
            "w_query": w_query, "sub_keys": sub_keys, "expert_u": expert_u, "expert_v": expert_v,
            "ln2_g": ln2_g, "ln2_b": ln2_b}

def second_block(x, w_in, lam_q1, lam_k1, lam_q2, lam_k2, subln_g, w_o, ln1_g, ln1_b,
              w_query, sub_keys, expert_u, expert_v, ln2_g, ln2_b):
    h = x
    for l in range(DEPTH):
        mix = token_mixer(h, w_in[l], lam_q1[l], lam_k1[l], lam_q2[l], lam_k2[l], subln_g[l], w_o[l], l)
        h = layer_norm_2(DEEPNORM_ALPHA * h + mix, ln1_g[l], ln1_b[l])
        ffn = peer_ffn(h, w_query[l], sub_keys[l], expert_u[l], expert_v[l])
        h = layer_norm_2(DEEPNORM_ALPHA * h + ffn, ln2_g[l], ln2_b[l])
    return h


def setup_inputs(seed=0):
    out = dict(first_inputs(seed))
    for name, value in second_inputs(seed + 1).items():
        if name != "x":
            out[name + "_2"] = value
    return out


def reference(
    x, c, mixer_norm_g, w_ada, b_ada, w_in, conv_w, conv_b, conv_ln_g, conv_ln_b, w_conv_out,
    b_conv_out, pool_w, pool_scale, w_out, ffn_norm_g, w_router_group, b_router_group,
    w_router_expert, b_router_expert, w_expert_gate, w_expert_up, w_expert_down, final_norm_g,
    w_in_2, lam_q1_2, lam_k1_2, lam_q2_2, lam_k2_2, subln_g_2, w_o_2, ln1_g_2, ln1_b_2,
    w_query_2, sub_keys_2, expert_u_2, expert_v_2, ln2_g_2, ln2_b_2,
):
    x = first_block(
        x, c, mixer_norm_g, w_ada, b_ada, w_in, conv_w, conv_b, conv_ln_g, conv_ln_b,
        w_conv_out, b_conv_out, pool_w, pool_scale, w_out, ffn_norm_g, w_router_group,
        b_router_group, w_router_expert, b_router_expert, w_expert_gate, w_expert_up,
        w_expert_down, final_norm_g,
    )
    return second_block(
        x, w_in_2, lam_q1_2, lam_k1_2, lam_q2_2, lam_k2_2, subln_g_2, w_o_2, ln1_g_2, ln1_b_2,
        w_query_2, sub_keys_2, expert_u_2, expert_v_2, ln2_g_2, ln2_b_2,
    )


_drawn_inputs = setup_inputs


def setup_inputs(seed=0):
    import zlib

    import numpy as np

    out = dict(_drawn_inputs(seed))
    spreads = {}
    factors = {'conv_b': 3.312,
     'conv_ln_g': 2.701,
     'conv_ln_b': 4.582,
     'b_conv_out': 3.813,
     'b_router_group': 4.485,
     'b_router_expert': 4.693,
     'subln_g_2': 5.442}
    for name, (base, spread) in spreads.items():
        noise = np.random.default_rng([zlib.crc32(name.encode()), seed]).standard_normal(out[name].shape)
        drawn = base * np.exp(spread * noise) if base else spread * noise
        out[name] = __import__('jax').numpy.asarray(drawn.astype(out[name].dtype))
    for name, factor in factors.items():
        out[name] = (out[name] * factor).astype(out[name].dtype)
    return out
```

```python
import math
from contextlib import ExitStack

import concourse.bass as bass
import numpy as np
from concourse import mybir

F32 = mybir.dt.float32
BF16 = mybir.dt.bfloat16
U32 = mybir.dt.uint32
ALU = mybir.AluOpType
ACT = mybir.ActivationFunctionType
AX = mybir.AxisListType

P = 128
D = 1024
T = 256
L = 2
KC = D // P
TH = T // P
CK = 31
DCONV = 512
CC = DCONV // P
NG, EPG = 4, 8
NE = NG * EPG
NR = NG + NE
EPS1, EPS2 = 1e-6, 1e-5
HD = 64
DH, SH = 4, 8
PH, PTOP, NK = 8, 16, 128
HP = PH * 2
NSEL = PH * PTOP
ALPHA = (2.0 * L) ** 0.25
NEG = -1.0e30

SLOTS = 3
TILE = 2048
ADA_T, IN_T, POOL_T, CONV_T, OUT_T = 24, 14, 1, 2, 4
J_IN = ADA_T
J_POOL = J_IN + IN_T
J_CONV = J_POOL + POOL_T
J_OUT = J_CONV + CONV_T
J_MOE = J_OUT + OUT_T
TILES1 = J_MOE + 3 * NE
IN2_T, WO_T, WQ_T, KEY_T, U_T = 12, 4, 8, 1, NK // 2
J_WO = IN2_T
J_WQ = J_WO + WO_T
J_KEY = J_WQ + WQ_T
J_U = J_KEY + KEY_T
J_V = J_U + U_T
TILES2 = J_V + U_T
TILES = L * (TILES1 + TILES2)
assert TILES1 % SLOTS == 0 and TILES2 % SLOTS == 0

LB = 3
UN_POOL, UN_CONV, UN_OUT, UN_ROUT = 14, 18, 22, 26
UNITS1 = 27
UN_WO, UN_WQ, UN_SC, UN_U = 12, 16, 24, 32
UNITS2 = UN_U + U_T
BASE2 = L * UNITS1
PARTS1, PARTS2 = 6, 7
assert UNITS1 % LB == 0 and UNITS2 % LB == 0


def columns(parts):
    at, out = 0, {}
    for name, n in parts:
        out[name] = (at, at + n)
        at += n
    return out, at


COL1, NCOL1 = columns([("norm_g", KC), ("b_ada", 6 * KC), ("conv_w", CC * CK), ("conv_b", CC),
                       ("ln_g", CC), ("ln_b", CC), ("b_out", KC), ("pool_scale", KC), ("ffn_g", KC),
                       ("router_w", KC * NR), ("router_b", NR)])
COL2, NCOL2 = columns([("subln_g", 1), ("keep", 1), ("lambda_init", 1), ("ln1_g", KC), ("ln1_b", KC),
                       ("ln2_g", KC), ("ln2_b", KC), ("lam_q", 2 * HD), ("lam_k", 2 * HD)])
COLC, NCOLC = columns([("final_g", KC), ("c", KC)])


def program(nc, wstream, x_in, params1, params2, consts, inv_count, out):
    ctx = ExitStack()
    with ctx:
        def sb(name, shape, dt=F32):
            return ctx.enter_context(nc.sbuf_tensor(name, shape, dt))

        def sem(name):
            return ctx.enter_context(nc.semaphore(name))

        slot = [sb(f"slot{i}", [P, TILE]) for i in range(SLOTS)]
        arena = sb("arena", [P, NK, T])
        xT = sb("xT", [P, KC, T])
        iota = sb("iota", [P, P])
        ident = sb("ident", [P, P])
        ones = sb("ones", [P, P])
        later = sb("later", [P, P])
        zeros = sb("zeros", [P, 512], BF16)
        par1 = sb("par1", [P, NCOL1])
        par2 = sb("par2", [P, NCOL2])
        cst = sb("cst", [P, NCOLC])
        c_act = sb("c_act", [P, KC])
        mod = sb("mod", [P, 6 * KC])
        gain = sb("gain", [P, 2 * KC])
        picks = sb("picks", [P, 3, TH, NSEL])
        picksT = sb("picksT", [P, 3, T])
        hotA = sb("hotA", [P, 2, 4, P])
        hotB = sb("hotB", [P, 2, 4, P])
        lamb = sb("lamb", [P, 16])
        rsm = sb("rsm", [P, 16])

        def par(t, cols, name):
            a, b = cols[name]
            return t[:, a:b]

        def area(at, n):
            return arena[:, at:at + n, :]

        def flat(at, n):
            return arena[:, at:at + n, :].rearrange("p a b -> p (a b)")

        SQ, H = area(0, 8), area(8, 8)
        UA, SG = area(16, 4), area(20, 4)
        GA, GB = area(24, 8), area(32, 8)
        YA, YB, MIX = area(40, 8), area(48, 8), area(56, 8)
        VPAD = flat(64, 5)[:, 0:CC * (T + CK - 1)].rearrange("p (c t) -> p c t", c=CC)
        UP, CV = area(69, 4), area(73, 4)
        PPAD = [flat(77 + 5 * i, 5)[:, 0:CC * (T + 16)].rearrange("p (c t) -> p c t", c=CC) for i in range(4)]
        PLD, INVC, TMP1 = area(97, 4), area(101, 4), area(105, 8)
        MEAN, VAR, RSTD = area(113, 1), area(114, 1), area(115, 1)
        CVN, CVS = area(116, 4), area(120, 4)
        RT = flat(73, 4)
        SGM, EACT, GU = area(77, 2), area(79, 2), area(81, 2)
        DIAG = flat(83, 1).rearrange("p (h t) -> p h t", h=TH)
        CMB = flat(84, 1)[:, 0:TH * NE].rearrange("p (h e) -> p h e", h=TH)

        DQ, DK, SQT, SKT = area(0, 4), area(4, 4), area(8, 4), area(12, 4)
        DV = flat(16, 4).rearrange("p (h n) -> p h n", h=TH)
        SV = flat(20, 4).rearrange("p (h n) -> p h n", h=TH)
        ALIBI = area(24, 8).rearrange("p (h b) t -> p h b t", h=DH)
        SCO = [area(32 + 2 * i, 2) for i in range(2)]
        EXO = [area(36 + 2 * i, 2) for i in range(2)]
        ATT = [area(40 + i, 1) for i in range(2)]
        ATT_T = area(42, 8).rearrange("p (h b) t -> p h b t", h=DH)
        DIFF, DSQ, DRS = area(50, 4), area(54, 4), area(58, 4)
        MIXT = area(62, 8)
        SW = 384
        ZS, NA, L1, LF, WW = (flat(70 + 6 * i, 6).rearrange("p (g t) -> p g t", g=4) for i in range(5))
        MASK = flat(100, 2)[:, 0:SW]
        YC, SQ2, TMP2 = area(0, 8), area(8, 8), area(16, 8)
        MEAN2, VAR2, RSTD2 = area(24, 1), area(25, 1), area(26, 1)
        QT = area(28, 16)
        SC = [flat(112 + 8 * h, 8).rearrange("p (s n) -> p s n", s=HP) for h in range(TH)]
        WORK = flat(64, 8).rearrange("p (s n) -> p s n", s=HP)
        CAND, CWORK = area(72, 8), area(80, 8)
        EQ = area(88, 8).rearrange("p (h j) (k a) -> p h j k a", h=PH, k=16)
        EQS = flat(88, 8).rearrange("p (s a) -> p s a", a=16)
        EQH = flat(88, 8).rearrange("p (h j a) -> p h j a", h=PH, j=16)
        TOPV = flat(96, 1).rearrange("p (s j) -> p s j", s=HP)
        TOPI = flat(97, 1).bitcast(U32).rearrange("p (s j) -> p s j", s=HP)
        TOPF = flat(98, 1).rearrange("p (h q j) -> p h q j", h=PH, q=2)
        BV = flat(99, 1)[:, 0:NSEL].rearrange("p (h j) -> p h j", h=PH)
        BP = flat(100, 1)[:, 0:NSEL].bitcast(U32)
        BPH = BP.rearrange("p (h j) -> p h j", h=PH)
        BA = flat(101, 1)[:, 0:NSEL].bitcast(U32)
        BB = flat(102, 1)[:, 0:NSEL].bitcast(U32)
        BF = flat(103, 1).rearrange("p (q s) -> p q s", q=2)
        BE = flat(104, 1)[:, 0:NSEL].rearrange("p (h j) -> p h j", h=PH)
        BS = flat(105, 1)[:, 0:PH]

        acc = ctx.enter_context(nc.psum_tensor("acc", [P, 4, 512], F32))
        lin = [ctx.enter_context(nc.psum_tensor(f"lin{i}", [P, 512], F32)) for i in range(LB)]
        stat = ctx.enter_context(nc.psum_tensor("stat", [P, 512], F32))
        accT = acc[:, :, :].rearrange("p b (c t) -> p (b c) t", c=2)
        G_PS, U_PS, C_PS = lin[0], lin[1], lin[2]

        w_loaded = [sem(f"w_loaded{i}") for i in range(SLOTS)]
        tile_done = sem("tile_done")
        small_loaded = sem("small_loaded")
        x_loaded = sem("x_loaded")
        par1_loaded, par2_loaded = sem("par1_loaded"), sem("par2_loaded")
        inv_loaded = sem("inv_loaded")
        consts_made = sem("consts_made")
        zeros_made = sem("zeros_made")
        pads_made = sem("pads_made")
        c_ready = sem("c_ready")
        part_done = sem("part_done")
        lin_free = sem("lin_free")
        stat_in, stat_out = sem("stat_in"), sem("stat_out")
        var_ready, std_ready = sem("var_ready"), sem("std_ready")
        h_ready = sem("h_ready")
        pooled_ready, mixed_ready = sem("pooled_ready"), sem("mixed_ready")
        cvn_ready, cvs_ready = sem("cvn_ready"), sem("cvs_ready")
        h2_ready = sem("h2_ready")
        rl_ready, re_ready = sem("rl_ready"), sem("re_ready")
        up_done = sem("up_done")
        silu_done, diag_ready, eact_ready = sem("silu_done"), sem("diag_ready"), sem("eact_ready")
        moe_done, moe_out = sem("moe_done"), sem("moe_out")
        layer_end1, layer_end2 = sem("layer_end1"), sem("layer_end2")
        x2_ready = sem("x2_ready")
        alibi_made = sem("alibi_made")
        lam_in, lam_exp = sem("lam_in"), sem("lam_exp")
        sc_done, smax_ready, e_ready = sem("sc_done"), sem("smax_ready"), sem("e_ready")
        att_ready, tr_done, tr_out = sem("att_ready"), sem("tr_done"), sem("tr_out")
        dpv_done, dpv_out, dsq_ready, dss_done = sem("dpv_done"), sem("dpv_out"), sem("dsq_ready"), sem("dss_done")
        dvar_ready, dstd_ready = sem("dvar_ready"), sem("dstd_ready")
        z_done, na_ready, l1_ready, lf_ready = sem("z_done"), sem("na_ready"), sem("l1_ready"), sem("lf_ready")
        lat_done, wl_ready, we_ready, ww_ready = sem("lat_done"), sem("wl_ready"), sem("we_ready"), sem("ww_ready")
        spv_done, spv_out = sem("spv_done"), sem("spv_out")
        mixt_ready, x3_ready = sem("mixt_ready"), sem("x3_ready")
        bl_ready, be_ready = sem("bl_ready"), sem("be_ready")
        routed = sem("routed")
        ptr_done, ptr_out = sem("ptr_done"), sem("ptr_out")
        hot_ready, g_done, gated = sem("hot_ready"), sem("g_done"), sem("gated")
        v_done, v_out = sem("v_done"), sem("v_out")
        final_ready, stored = sem("final_ready"), sem("stored")

        block = ctx.enter_context(nc.Block())

        @block.sync
        def _(sp):
            sp.dma_start(cst[:, :], consts[:, :]).then_inc(small_loaded, 16)
            with sp.Fori(0, TILES // SLOTS) as i:
                for s in range(SLOTS):
                    sp.wait_ge(tile_done, i * SLOTS + s + 1)
                    sp.dma_start(slot[s][:, :], wstream[i * SLOTS + s]).then_inc(w_loaded[s], 16)

        @block.gpsimd
        def _(pool):
            pool.dma_start(xT[:, :, :], x_in[:, :, :]).then_inc(x_loaded, 16)
            pool.dma_start(INVC, inv_count[:, :, :]).then_inc(inv_loaded, 16)
            nc.gpsimd.iota(iota[:, :], [[1, P]], base=0, channel_multiplier=0,
                           allow_small_or_imprecise_dtypes=True)
            nc.gpsimd.memset(ones[:, :], 1.0)
            pool.drain()
            nc.gpsimd.affine_select(out=ident[:, :], in_=ones[:, :], compare_op=ALU.is_equal, fill=0.0,
                                    base=0, pattern=[[-1, P]], channel_multiplier=1)
            nc.gpsimd.affine_select(out=later[:, :], in_=ones[:, :], compare_op=ALU.is_gt, fill=0.0,
                                    base=0, pattern=[[-1, P]], channel_multiplier=1)
            pool.drain().then_inc(consts_made, 1)
            with pool.Fori(0, L) as l:
                pool.wait_ge(layer_end1, l + 1)
                pool.dma_start(par1[:, :], params1[l]).then_inc(par1_loaded, 16)
                nc.gpsimd.memset(VPAD[:, :, 0:CK - 1], 0.0)
                for q in PPAD:
                    nc.gpsimd.memset(q[:, :, 0:16], 0.0)
                pool.drain().then_inc(pads_made, 1)
            pool.wait_ge(layer_end1, L + 1)
            with pool.Fori(0, L) as l:
                pool.wait_ge(layer_end2, l + 1)
                pool.dma_start(par2[:, :], params2[l]).then_inc(par2_loaded, 16)
                for b in range(TH):
                    for h in range(DH):
                        nc.gpsimd.iota(ALIBI[:, h, b, :], [[-1, T]], base=b * P, channel_multiplier=1,
                                       allow_small_or_imprecise_dtypes=True)
                pool.drain()
                for h in range(DH):
                    slope = 2.0 ** (-8.0 * (h + 1) / DH)
                    nc.gpsimd.tensor_scalar(ALIBI[:, h, :, :], ALIBI[:, h, :, :], -slope, None, ALU.mult)
                pool.drain()
                for b in range(TH):
                    for h in range(DH):
                        nc.gpsimd.affine_select(out=ALIBI[:, h, b, :], in_=ALIBI[:, h, b, :],
                                                compare_op=ALU.is_ge, fill=NEG, base=b * P,
                                                pattern=[[-1, T]], channel_multiplier=1)
                nc.gpsimd.memset(MASK, 1.0)
                pool.drain()
                for a in (0, 2 * P):
                    nc.gpsimd.affine_select(out=MASK[:, a:a + P], in_=MASK[:, a:a + P], compare_op=ALU.is_gt,
                                            fill=0.0, base=0, pattern=[[1, P]], channel_multiplier=-1)
                pool.drain().then_inc(alibi_made, 1)

        @block.tensor
        def _(pe):
            mm = nc.tensor.matmul

            def loaded(count, j):
                pe.wait_ge(w_loaded[j % SLOTS], (count + j // SLOTS + 1) * 16)
                return slot[j % SLOTS]

            def column_sum(value, src, n):
                pe.wait_ge(stat_in, value)
                for k in range(n):
                    last = mm(stat[:, 0:T], ones[:, :], src[:, k, :], start=(k == 0), stop=(k == n - 1))
                last.then_inc(stat_out, 1)

            def linear(w, rhs, unit, base_unit):
                pe.wait_ge(lin_free, base_unit + unit + 1)
                bank = lin[unit % LB]
                wv = w[:, :].rearrange("p (k n) -> p k n", k=KC)
                for n in range(2):
                    for k in range(KC):
                        last = mm(bank[:, n * T:(n + 1) * T], wv[:, k, n * P:(n + 1) * P], rhs[:, k, :],
                                  start=(k == 0), stop=(k == KC - 1))
                last.then_inc(tile_done, 1)

            pe.sem_inc(tile_done, SLOTS)
            pe.wait_ge(consts_made, 1)
            pe.wait_ge(zeros_made, 1)
            pe.wait_ge(c_ready, 1)

            def open_acc():
                for b in range(4):
                    mm(acc[:, b, :], zeros[:, 0:P], zeros[:, :], start=True, stop=False)

            def close_acc(done):
                for b in range(4):
                    last = mm(acc[:, b, :], zeros[:, 0:P], zeros[:, :], start=False, stop=True)
                last.then_inc(done, 1)

            with pe.Fori(0, L) as l:
                rings = l * (TILES1 // SLOTS)
                units = l * UNITS1
                column_sum(l * 4 + 1, SQ, KC)
                with pe.Fori(0, ADA_T // SLOTS) as i:
                    for s in range(SLOTS):
                        w = loaded(rings + i, s)[:, :].rearrange("p (k n) -> p k n", k=KC)
                        for n in range(2):
                            for k in range(KC):
                                last = mm(acc[:, 0, bass.ds(i * (2 * SLOTS) + (2 * s + n), 1)],
                                          w[:, k, n * P:(n + 1) * P], c_act[:, k:k + 1],
                                          start=(k == 0), stop=(k == KC - 1))
                        last.then_inc(tile_done, 1)
                pe.wait_ge(h_ready, l + 1)
                for j in range(IN_T):
                    linear(loaded(rings, J_IN + j), H, j, units)
                pe.wait_ge(pooled_ready, l + 1)
                w = loaded(rings, J_POOL)
                for g in range(CC):
                    pe.wait_ge(lin_free, units + UN_POOL + g + 1)
                    bank = lin[(UN_POOL + g) % LB]
                    for n in range(2):
                        last = mm(bank[:, n * T:(n + 1) * T], w[:, (2 * g + n) * P:(2 * g + n + 1) * P],
                                  PLD[:, g, :], start=True, stop=True)
                    last.then_inc(tile_done if g == CC - 1 else part_done, 1)
                column_sum(l * 4 + 2, CV, CC)
                column_sum(l * 4 + 3, SQ, CC)
                pe.wait_ge(cvs_ready, l + 1)
                for j in range(CONV_T):
                    w = loaded(rings, J_CONV + j)[:, :].rearrange("p (k n) -> p k n", k=CC)
                    for half in range(2):
                        u = UN_CONV + 2 * j + half
                        pe.wait_ge(lin_free, units + u + 1)
                        for n in range(2):
                            for k in range(CC):
                                m = (2 * half + n) * P
                                last = mm(lin[u % LB][:, n * T:(n + 1) * T], w[:, k, m:m + P], CVS[:, k, :],
                                          start=(k == 0), stop=(k == CC - 1))
                        last.then_inc(tile_done if half else part_done, 1)
                pe.wait_ge(mixed_ready, l + 1)
                for j in range(OUT_T):
                    linear(loaded(rings, J_OUT + j), MIX, UN_OUT + j, units)
                column_sum(l * 4 + 4, SQ, KC)
                pe.wait_ge(h2_ready, l + 1)
                pe.wait_ge(lin_free, units + UN_ROUT + 1)
                rw = par(par1, COL1, "router_w").rearrange("p (k n) -> p k n", k=KC)
                for th in range(TH):
                    for k in range(KC):
                        last = mm(lin[UN_ROUT % LB][:, th * NR:(th + 1) * NR], H[:, k, th * P:(th + 1) * P],
                                  rw[:, k, :], start=(k == 0), stop=(k == KC - 1))
                last.then_inc(part_done, 1)
                pe.wait_ge(lin_free, units + UNITS1 + LB)
                open_acc()

                def expert_in(j, count, e, bank, free):
                    w = loaded(count, j)[:, :].rearrange("p (k n) -> p k n", k=KC)
                    pe.wait_ge(free, e + 1)
                    for n in range(2):
                        for k in range(KC):
                            last = mm(bank[:, n * T:(n + 1) * T], w[:, k, n * P:(n + 1) * P], H[:, k, :],
                                      start=(k == 0), stop=(k == KC - 1))
                    last.then_inc(tile_done, 1)

                def spread_weights(e):
                    pe.wait_ge(diag_ready, e + 1)
                    for th in range(TH):
                        last = mm(C_PS[:, th * P:(th + 1) * P], ones[:, :], DIAG[:, th, :], start=True, stop=True)
                    last.then_inc(up_done, 1)

                def expert_down(j, count, e):
                    w = loaded(count, j)[:, :].rearrange("p (k n) -> p k n", k=2)
                    pe.wait_ge(eact_ready, e + 2)
                    for n in range(KC):
                        for k in range(2):
                            last = mm(accT[:, n, :], w[:, k, n * P:(n + 1) * P], EACT[:, k, :],
                                      start=False, stop=False)
                    last.then_inc(tile_done, 1)

                e0 = l * NE
                expert_in(J_MOE, rings, e0, G_PS, silu_done)
                expert_in(J_MOE + 1, rings, e0, U_PS, eact_ready)
                spread_weights(e0)
                with pe.Fori(0, NE - 1) as i:
                    expert_in(J_MOE + 2, rings + i, e0 + i + 1, G_PS, silu_done)
                    expert_down(J_MOE + 3, rings + i, e0 + i)
                    expert_in(J_MOE + 4, rings + i, e0 + i + 1, U_PS, eact_ready)
                    spread_weights(e0 + i + 1)
                expert_down(J_MOE + 3 * NE - 1, rings, e0 + NE - 1)
                close_acc(moe_done)

            column_sum(L * 4 + 1, SQ, KC)

            with pe.Fori(0, L) as l:
                rings = l * (TILES2 // SLOTS) + L * TILES1 // SLOTS
                units = l * UNITS2 + BASE2
                stat0 = l * 4 + (L * 4 + 1)
                pe.wait_ge(x2_ready, l + 1)
                for j in range(IN2_T):
                    w = loaded(rings, j)
                    if j in (4, 5, 10, 11):
                        pe.wait_ge(lin_free, units + j + 1)
                        wv = w[:, :].rearrange("p (k n) -> p k n", k=KC)
                        for th in range(TH):
                            for k in range(KC):
                                last = mm(lin[j % LB][:, th * T:(th + 1) * T], xT[:, k, th * P:(th + 1) * P],
                                          wv[:, k, :], start=(k == 0), stop=(k == KC - 1))
                        last.then_inc(tile_done, 1)
                    else:
                        linear(w, xT, j, units)

                def scores(d):
                    b, h = divmod(d, DH)
                    if d >= 2:
                        pe.wait_ge(smax_ready, l * 8 + d - 1)
                    for m in range(2):
                        r = slice(m * HD, (m + 1) * HD)
                        last = mm(acc[:, 2 * (d % 2) + m, 0:(b + 1) * P], DQ[r, h, b * P:(b + 1) * P],
                                  DK[r, h, 0:(b + 1) * P], start=True, stop=True)
                    last.then_inc(sc_done, 1)

                pe.wait_ge(lin_free, units + IN2_T + LB)
                scores(0)
                scores(1)
                for d in range(8):
                    b, h = divmod(d, DH)
                    pe.wait_ge(att_ready, l * 8 + d + 1)
                    if d >= 2:
                        pe.wait_ge(tr_out, l * 8 + d - 1)
                    for kb in range(b + 1):
                        last = nc.tensor.transpose(lin[d % 2][:, kb * P:(kb + 1) * P],
                                                   ATT[d % 2][:, 0, kb * P:(kb + 1) * P], ident[:, :])
                    last.then_inc(tr_done, 1)
                    if d + 2 < 8:
                        scores(d + 2)
                pe.wait_ge(tr_out, l * 8 + 8)
                for h in range(DH):
                    o = accT[:, h, :]
                    mm(o, DV[:, 0, h * P:(h + 1) * P], ATT_T[:, h, 0, :], start=True, stop=False)
                    last = mm(accT[:, h, P:T], DV[:, 1, h * P:(h + 1) * P], ATT_T[:, h, 1, P:T],
                              start=False, stop=True)
                last.then_inc(dpv_done, 1)
                pe.wait_ge(dsq_ready, l + 1)
                for q in range(2):
                    last = mm(acc[:, 2 + q, :], ones[:, :], DSQ[:, 2 * q:2 * q + 2, :], start=True, stop=True)
                last.then_inc(dss_done, 1)
                for w4 in range(2):
                    if w4 == 0:
                        pe.wait_ge(dvar_ready, l + 1)
                    for g in range(4):
                        hh = 4 * w4 + g
                        r, c = slice((hh % 2) * HD, (hh % 2 + 1) * HD), hh // 2
                        mm(acc[:, g, 0:T], SKT[r, c, 0:P], SQT[r, c, :], start=True, stop=True)
                        last = mm(acc[:, g, T:SW], SKT[r, c, P:T], SQT[r, c, P:T], start=True, stop=True)
                    last.then_inc(z_done, 1)
                    pe.wait_ge(lf_ready, l * 2 + w4 + 1)
                    for g in range(4):
                        mm(acc[:, g, 0:T], later[:, :], LF[:, g, 0:T], start=True, stop=False)
                        mm(acc[:, g, P:T], ones[:, :], LF[:, g, T:SW], start=False, stop=True)
                        last = mm(acc[:, g, T:SW], later[:, :], LF[:, g, T:SW], start=True, stop=True)
                    last.then_inc(lat_done, 1)
                    pe.wait_ge(ww_ready, l * 2 + w4 + 1)
                    for g in range(4):
                        hh = 4 * w4 + g
                        r, c = slice((hh % 2) * HD, (hh % 2 + 1) * HD), g // 2
                        mm(stat[r, c * T:(c + 1) * T], SV[:, 0, hh * HD:(hh + 1) * HD], WW[:, g, 0:T],
                           start=True, stop=False)
                        last = mm(stat[r, c * T + P:(c + 1) * T], SV[:, 1, hh * HD:(hh + 1) * HD],
                                  WW[:, g, T:SW], start=False, stop=True)
                    last.then_inc(spv_done, 1)
                    if w4 == 0:
                        pe.wait_ge(spv_out, l * 2 + 1)
                pe.wait_ge(mixt_ready, l + 1)
                pe.wait_ge(spv_out, l * 2 + 2)
                for j in range(WO_T):
                    linear(loaded(rings, J_WO + j), MIXT, UN_WO + j, units)
                column_sum(stat0 + 1, YC, KC)
                column_sum(stat0 + 2, SQ2, KC)
                pe.wait_ge(x3_ready, l + 1)
                for j in range(WQ_T):
                    linear(loaded(rings, J_WQ + j), xT, UN_WQ + j, units)
                pe.wait_ge(lin_free, units + UN_SC + LB)
                w = loaded(rings, J_KEY)[:, :].rearrange("p (s n) -> p s n", s=HP)
                for s in range(8):
                    th, q = divmod(s, 4)
                    pe.wait_ge(lin_free, units + UN_SC + s + 1)
                    for a in range(4):
                        hp = 4 * q + a
                        last = mm(lin[(UN_SC + s) % LB][:, a * P:(a + 1) * P], QT[:, hp, th * P:(th + 1) * P],
                                  w[:, hp, :], start=True, stop=True)
                    last.then_inc(tile_done if s == 7 else part_done, 1)

                def u_tile(j, i, unit_base):
                    w = loaded(rings + i, J_U + j)[:, :].rearrange("p (a k n) -> p a k n", a=2, k=KC)
                    pe.wait_ge(lin_free, unit_base + UN_U + j + 1)
                    bank = lin[(UN_U + j) % LB]
                    for a in range(2):
                        for k in range(KC):
                            last = mm(bank[:, a * T:(a + 1) * T], w[:, a, k, :], xT[:, k, :],
                                      start=(k == 0), stop=(k == KC - 1))
                    last.then_inc(tile_done, 1)

                with pe.Fori(0, U_T // SLOTS) as i:
                    for s in range(SLOTS):
                        u_tile(s, i, units + i * SLOTS)
                u_tile(U_T - 1, 0, units)
                pe.wait_ge(routed, l + 1)
                for q in range(3):
                    for th in range(TH):
                        a = q * TH + th
                        last = nc.tensor.transpose(acc[:, 2 + a // 4, (a % 4) * P:(a % 4 + 1) * P],
                                                   picks[:, q, th, :], ident[:, :])
                last.then_inc(ptr_done, 1)
                with pe.Fori(0, T // 8) as i:
                    for s in range(2):
                        pe.wait_ge(hot_ready, l * (T // 4) + i * 2 + s + 1)
                        for t in range(4):
                            last = mm(acc[:, s, t * P:(t + 1) * P], hotA[:, s, t, :], hotB[:, s, t, :],
                                      start=True, stop=True)
                        last.then_inc(g_done, 1)
                pe.wait_ge(gated, l + 1)
                open_acc()

                def v_tile(j, i, col):
                    w = loaded(rings + i, J_V + j)[:, :].rearrange("p (a n) -> p a n", a=2)
                    for a in range(2):
                        for n in range(KC):
                            last = mm(accT[:, n, :], w[:, a, n * P:(n + 1) * P],
                                      arena[:, bass.ds(col + a, 1), :], start=False, stop=False)
                    last.then_inc(tile_done, 1)

                with pe.Fori(0, U_T // SLOTS) as i:
                    for s in range(SLOTS):
                        v_tile(s, i, i * (2 * SLOTS) + 2 * s)
                v_tile(U_T - 1, 0, 2 * (U_T - 1))
                close_acc(v_done)
                column_sum(stat0 + 3, YC, KC)
                column_sum(stat0 + 4, SQ2, KC)

        @block.scalar
        def _(act):
            A = nc.scalar.activation

            def tile_through(count, j):
                act.wait_ge(tile_done, count + j + (SLOTS + 1))

            def unit1(l, u):
                part = {14: 1, 15: 2, 16: 3, UN_CONV: 4, UN_CONV + 2: 5, UN_ROUT: 6}
                if u in part:
                    act.wait_ge(part_done, l * PARTS1 + part[u])
                elif u < UN_POOL:
                    tile_through(l * TILES1, J_IN + u)
                elif u < UN_CONV:
                    tile_through(l * TILES1, J_POOL)
                elif u < UN_OUT:
                    tile_through(l * TILES1, J_CONV + (u - UN_CONV) // 2)
                else:
                    tile_through(l * TILES1, J_OUT + u - UN_OUT)
                return lin[u % LB]

            def unit2(l, u):
                count = l * TILES2 + L * TILES1
                if UN_SC <= u < UN_SC + 7:
                    act.wait_ge(part_done, l * PARTS2 + (L * PARTS1 + u - UN_SC + 1))
                elif u < UN_WO:
                    tile_through(count, u)
                elif u < UN_WQ:
                    tile_through(count, J_WO + u - UN_WO)
                elif u < UN_SC:
                    tile_through(count, J_WQ + u - UN_WQ)
                else:
                    tile_through(count, J_KEY)
                return lin[u % LB]

            def root(value, src, dst):
                act.wait_ge(var_ready, value)
                A(dst, src, ACT.Sqrt).then_inc(std_ready, 1)

            act.sem_inc(lin_free, LB)
            act.sem_inc(silu_done, 1)
            act.wait_ge(small_loaded, 16)
            A(c_act[:, :], par(cst, COLC, "c"), ACT.Silu).then_inc(c_ready, 1)

            with act.Fori(0, L) as l:
                units = l * UNITS1
                root(l * 3 + 1, VAR, RSTD)
                dsts = [UA[:, 0:2], SG[:, 0:2], UA[:, 2:4], SG[:, 2:4], UP[:, 0:2], UP[:, 2:4]]
                dsts += [GA[:, 2 * q:2 * q + 2] for q in range(4)] + [GB[:, 2 * q:2 * q + 2] for q in range(4)]
                for j, dst in enumerate(dsts):
                    func = ACT.Copy if j in (0, 2, 4, 5) else ACT.Sigmoid
                    A(dst, unit1(l, j)[:, :].rearrange("p (c t) -> p c t", c=2), func).then_inc(lin_free, 1)
                ps = par(par1, COL1, "pool_scale")
                for j in range(4):
                    bank = unit1(l, UN_POOL + j)
                    for n in range(2):
                        last = A(YB[:, 2 * j + n], bank[:, n * T:(n + 1) * T], ACT.Identity,
                                 scale=ps[:, 2 * j + n:2 * j + n + 1])
                    last.then_inc(lin_free, 1)
                root(l * 3 + 2, VAR, RSTD)
                act.wait_ge(cvn_ready, l + 1)
                g, b = par(par1, COL1, "ln_g"), par(par1, COL1, "ln_b")
                for k in range(CC):
                    last = A(CVS[:, k], CVN[:, k], ACT.Silu, scale=g[:, k:k + 1], bias=b[:, k:k + 1])
                last.then_inc(cvs_ready, 1)
                bo = par(par1, COL1, "b_out")
                for j in range(4):
                    bank = unit1(l, UN_CONV + j)
                    for n in range(2):
                        last = A(YA[:, 2 * j + n], bank[:, n * T:(n + 1) * T], ACT.Identity,
                                 bias=bo[:, 2 * j + n:2 * j + n + 1])
                    last.then_inc(lin_free, 1)
                for j in range(4):
                    bank = unit1(l, UN_OUT + j)
                    for n in range(2):
                        m = 2 * KC + 2 * j + n
                        last = A(TMP1[:, 2 * j + n], bank[:, n * T:(n + 1) * T], ACT.Identity,
                                 scale=mod[:, m:m + 1])
                    last.then_inc(lin_free, 1)
                root(l * 3 + 3, VAR, RSTD)
                A(RT[:, 0:TH * NR], unit1(l, UN_ROUT)[:, 0:TH * NR], ACT.Copy).then_inc(lin_free, 1)
                act.wait_ge(rl_ready, l * 2 + 1)
                A(RT[:, 100:108], RT[:, 100:108], ACT.Exp).then_inc(re_ready, 1)
                act.wait_ge(rl_ready, l * 2 + 2)
                A(RT[:, 200:216], RT[:, 200:216], ACT.Exp).then_inc(re_ready, 1)

                def expert_silu(e):
                    act.wait_ge(eact_ready, l * NE + e + 1)
                    A(SGM, G_PS[:, :].rearrange("p (c t) -> p c t", c=2), ACT.Silu).then_inc(silu_done, 1)

                tile_through(l * TILES1, J_MOE)
                expert_silu(0)
                with act.Fori(1, NE) as e:
                    tile_through(l * TILES1 + e * 3, J_MOE - 1)
                    expert_silu(e)
                act.wait_ge(moe_done, l + 1)
                for n in range(KC):
                    last = A(TMP1[:, n], accT[:, n, :], ACT.Identity, scale=mod[:, 5 * KC + n:5 * KC + n + 1])
                last.then_inc(moe_out, 1)

            root(L * 3 + 1, VAR, RSTD)

            with act.Fori(0, L) as l:
                units = l * UNITS2 + BASE2
                act.wait_ge(lam_in, l + 1)
                A(lamb[:, 2:4], lamb[:, 0:2], ACT.Exp).then_inc(lam_exp, 1)
                for j in range(IN2_T):
                    bank = unit2(l, j)[:, :].rearrange("p (c t) -> p c t", c=2)
                    which, half = divmod(j, 2)
                    if which in (2, 5):
                        dst = (DV if which == 2 else SV)[:, :, half * T:(half + 1) * T]
                    else:
                        dst = {0: DQ, 1: DK, 3: SQT, 4: SKT}[which][:, 2 * half:2 * half + 2]
                    A(dst, bank, ACT.Copy).then_inc(lin_free, 1)

                def soft(d):
                    b = d // DH
                    act.wait_ge(smax_ready, l * 8 + d + 1)
                    for m in range(2):
                        last = A(EXO[d % 2][:, m, 0:(b + 1) * P], SCO[d % 2][:, m, 0:(b + 1) * P], ACT.Exp,
                                 bias=rsm[:, 4 * (d % 2) + m:4 * (d % 2) + m + 1],
                                 accum_out=rsm[:, 4 * (d % 2) + 2 + m:4 * (d % 2) + 3 + m])
                    last.then_inc(e_ready, 1)

                def move(d):
                    b, h = divmod(d, DH)
                    act.wait_ge(tr_done, l * 8 + d + 1)
                    A(ATT_T[:, h, 0:b + 1, b * P:(b + 1) * P],
                      lin[d % 2][:, 0:(b + 1) * P].rearrange("p (k q) -> p k q", k=b + 1),
                      ACT.Copy).then_inc(tr_out, 1)

                soft(0)
                for d in range(8):
                    if d + 1 < 8:
                        soft(d + 1)
                    move(d)
                act.wait_ge(dpv_done, l + 1)
                A(DIFF, accT[:, 0:4, :], ACT.Copy).then_inc(dpv_out, 1)
                act.wait_ge(dvar_ready, l + 1)
                A(DRS, DRS, ACT.Sqrt).then_inc(dstd_ready, 1)
                for w4 in range(2):
                    v = l * 2 + w4 + 1
                    act.wait_ge(na_ready, v)
                    A(NA, NA, ACT.Exp)
                    act.drain()
                    A(L1, NA, ACT.Ln, bias=1.0).then_inc(l1_ready, 1)
                    act.wait_ge(wl_ready, v)
                    A(NA, ZS, ACT.Exp).then_inc(we_ready, 1)
                    act.wait_ge(spv_done, v)
                    A(MIXT[:, 4 + 2 * w4:6 + 2 * w4], stat[:, :].rearrange("p (c t) -> p c t", c=2),
                      ACT.Copy).then_inc(spv_out, 1)
                for j in range(WO_T):
                    A(TMP2[:, 2 * j:2 * j + 2], unit2(l, UN_WO + j)[:, :].rearrange("p (c t) -> p c t", c=2),
                      ACT.Copy).then_inc(lin_free, 1)
                root(L * 3 + 1 + l * 2 + 1, VAR2, RSTD2)
                for j in range(WQ_T):
                    A(QT[:, 2 * j:2 * j + 2], unit2(l, UN_WQ + j)[:, :].rearrange("p (c t) -> p c t", c=2),
                      ACT.Copy).then_inc(lin_free, 1)
                for s in range(8):
                    th, q = divmod(s, 4)
                    A(SC[th][:, 4 * q:4 * q + 4, :],
                      unit2(l, UN_SC + s)[:, :].rearrange("p (a n) -> p a n", a=4),
                      ACT.Copy).then_inc(lin_free, 1)

                def gelu(j, value, col):
                    tile_through(value, J_U + j)
                    A(arena[:, bass.ds(col, 2), :], lin[(UN_U + j) % LB][:, :].rearrange("p (c t) -> p c t", c=2),
                      ACT.Gelu).then_inc(lin_free, 1)

                HEAD = 10
                with act.Fori(0, HEAD) as i:
                    for s in range(SLOTS):
                        gelu(s, l * TILES2 + (L * TILES1) + i * SLOTS, i * (2 * SLOTS) + 2 * s)
                for th in range(TH):
                    act.wait_ge(bl_ready, l * TH + th + 1)
                    A(BE, BE, ACT.Exp).then_inc(be_ready, 1)
                act.wait_ge(routed, l + 1)
                with act.Fori(HEAD, U_T // SLOTS) as i:
                    for s in range(SLOTS):
                        gelu(s, l * TILES2 + (L * TILES1) + i * SLOTS, i * (2 * SLOTS) + 2 * s)
                gelu(U_T - 1, l * TILES2 + (L * TILES1), 2 * (U_T - 1))
                act.wait_ge(ptr_done, l + 1)
                A(picksT[:, 0:2, :], acc[:, 2, :].rearrange("p (q t) -> p q t", q=2), ACT.Copy)
                A(picksT[:, 2, :], acc[:, 3, 0:T], ACT.Copy).then_inc(ptr_out, 1)
                act.wait_ge(v_done, l + 1)
                A(TMP2, accT, ACT.Copy).then_inc(v_out, 1)
                root(L * 3 + 1 + l * 2 + 2, VAR2, RSTD2)
            act.wait_ge(final_ready, 1)
            act.dma_start(out[:, :, :], xT[:, :, :]).then_inc(stored, 16)
            act.wait_ge(stored, 16)

        @block.vector
        def _(dve):
            V = nc.vector
            TT, TS, STT = V.tensor_tensor, V.tensor_scalar, V.scalar_tensor_tensor

            def over(ap, n):
                return ap.to_broadcast([P, n, T])

            def rstd(sum_value, root_value, src_bank, n, eps, var, dst):
                dve.wait_ge(stat_out, sum_value)
                TS(var[:, 0, :], src_bank, 1.0 / n, eps, ALU.mult, ALU.add).then_inc(var_ready, 1)
                dve.wait_ge(std_ready, root_value)
                V.reciprocal(dst[:, 0, :], dst[:, 0, :])
                dve.drain()

            def squares(src, dst):
                TT(dst, src, src, ALU.mult).then_inc(stat_in, 1)

            def modulated(dst, gains, shifts):
                TT(dst, xT[:, :, :], over(RSTD, KC), ALU.mult)
                dve.drain()
                for k in range(KC):
                    if shifts is None:
                        TS(xT[:, k, :], dst[:, k, :], gains[:, k:k + 1], None, ALU.mult)
                    else:
                        TS(dst[:, k, :], dst[:, k, :], gains[:, k:k + 1], shifts[:, k:k + 1], ALU.mult, ALU.add)

            dve.sem_inc(layer_end1, 1)
            dve.sem_inc(eact_ready, 1)
            V.memset(zeros[:, :], 0.0).then_inc(zeros_made, 1)
            dve.wait_ge(small_loaded, 16)
            dve.wait_ge(x_loaded, 16)
            dve.wait_ge(inv_loaded, 16)
            dve.wait_ge(consts_made, 1)

            with dve.Fori(0, L) as l:
                units = l * UNITS1

                def moved(u):
                    dve.wait_ge(lin_free, units + u + 1 + LB)

                squares(xT[:, :, :], SQ)
                rstd(l * 4 + 1, l * 3 + 1, stat[:, 0:T], D, EPS1, VAR, RSTD)
                dve.wait_ge(par1_loaded, l * 16 + 16)
                dve.wait_ge(tile_done, l * TILES1 + (ADA_T + SLOTS))
                TT(mod[:, :], acc[:, 0, 0:6 * KC], par(par1, COL1, "b_ada"), ALU.add)
                dve.drain()
                for q, name in ((0, "norm_g"), (1, "ffn_g")):
                    s = (3 * q + 1) * KC
                    STT(gain[:, q * KC:(q + 1) * KC], mod[:, s:s + KC], 1.0, par(par1, COL1, name), ALU.add, ALU.mult)
                dve.drain()
                modulated(H, gain[:, 0:KC], mod[:, 0:KC])
                dve.drain().then_inc(h_ready, 1)
                dve.wait_ge(pads_made, l + 1)
                moved(3)
                TT(VPAD[:, :, CK - 1:], UA, SG, ALU.mult)
                moved(5)
                V.tensor_copy(PPAD[0][:, :, 16:], UP)
                dve.drain()
                for s in range(4):
                    a, w = PPAD[s % 2 * 2], 1 << s
                    src = PPAD[s]
                    c = slice(s, CC)
                    dst = PPAD[s + 1][:, c, 16:] if s < 3 else PLD[:, c, :]
                    TT(dst, src[:, c, 16:], src[:, c, 16 - w:16 + T - w], ALU.add)
                    dve.drain()
                for s in range(3):
                    TT(PLD[:, s, :], PPAD[s + 1][:, s, 16:], INVC[:, s, :], ALU.mult)
                TT(PLD[:, 3, :], PLD[:, 3, :], INVC[:, 3, :], ALU.mult)
                dve.drain()
                TT(PLD, PLD, UP, ALU.subtract).then_inc(pooled_ready, 1)
                cw = par(par1, COL1, "conv_w").rearrange("p (c k) -> p c k", c=CC)
                cb = par(par1, COL1, "conv_b")
                for c in range(CC):
                    TS(CV[:, c, :], VPAD[:, c, 0:T], cw[:, c, 0:1], cb[:, c:c + 1], ALU.mult, ALU.add)
                dve.drain()
                with dve.Fori(1, CK) as k:
                    for c in range(CC):
                        STT(CV[:, c, :], VPAD[:, c, bass.ds(k, T)], cw[:, c, bass.ds(k, 1)], CV[:, c, :],
                            ALU.mult, ALU.add)
                    dve.drain()
                dve.drain().then_inc(stat_in, 1)
                dve.wait_ge(stat_out, l * 4 + 2)
                TS(MEAN[:, 0, :], stat[:, 0:T], 1.0 / DCONV, None, ALU.mult)
                dve.drain()
                TT(CVN, CV, over(MEAN, CC), ALU.subtract)
                dve.drain()
                squares(CVN, SQ[:, 0:CC, :])
                rstd(l * 4 + 3, l * 3 + 2, stat[:, 0:T], DCONV, EPS1, VAR, RSTD)
                TT(CVN, CVN, over(RSTD, CC), ALU.mult).then_inc(cvn_ready, 1)
                for u in range(4):
                    c = slice(2 * u, 2 * u + 2)
                    if u == 0:
                        moved(UN_POOL + 3)
                    TT(YB[:, c], YB[:, c], GB[:, c], ALU.mult)
                    moved(UN_CONV + u)
                    TT(YA[:, c], YA[:, c], GA[:, c], ALU.mult)
                    dve.drain()
                    TT(MIX[:, c], YA[:, c], YB[:, c], ALU.add)
                dve.drain().then_inc(mixed_ready, 1)
                for u in range(4):
                    moved(UN_OUT + u)
                    c = slice(2 * u, 2 * u + 2)
                    TT(xT[:, c, :], xT[:, c, :], TMP1[:, c], ALU.add)
                dve.drain()
                squares(xT[:, :, :], SQ)
                rstd(l * 4 + 4, l * 3 + 3, stat[:, 0:T], D, EPS1, VAR, RSTD)
                modulated(H, gain[:, KC:2 * KC], mod[:, 3 * KC:4 * KC])
                dve.drain().then_inc(h2_ready, 1)

                def r(a, *shape):
                    n = int(np.prod(shape))
                    v = RT[:, a:a + n]
                    if len(shape) == 2:
                        return v.rearrange("p (h n) -> p h n", h=shape[0])
                    if len(shape) == 3:
                        return v.rearrange("p (h g n) -> p h g n", h=shape[0], g=shape[1])
                    return v

                lg = r(0, TH, NR)
                eg, e8 = r(100, TH, NG), r(200, TH, EPG)
                gp8, g8, e8t = r(120, TH, 8), r(140, TH, 8), r(160, TH, 8)
                gi, ei = r(220, TH * 8).bitcast(U32), r(240, TH * 8).bitcast(U32)
                gmax, gsum = r(260, TH), r(264, TH)
                emax, esum, den = r(268, TH), r(272, TH), r(276, TH)
                gif, eif = r(280, TH, 8), r(300, TH, 8)
                og, sel8 = r(320, TH, NG), r(340, TH, EPG)
                prod = r(400, TH, NG, EPG)
                o1, o2, comb = r(500, TH, EPG), r(520, TH, EPG), r(540, TH, EPG)

                def wide(ap, n):
                    return ap.unsqueeze(2).to_broadcast([P, TH, n])

                moved(UN_ROUT)
                TT(lg, lg, par(par1, COL1, "router_b").unsqueeze(1).to_broadcast([P, TH, NR]), ALU.add)
                V.memset(gp8, -1.0)
                dve.drain()
                V.tensor_reduce(gmax, lg[:, :, 0:NG], AX.X, ALU.max)
                dve.drain()
                TT(eg, lg[:, :, 0:NG], wide(gmax, NG), ALU.subtract).then_inc(rl_ready, 1)
                dve.wait_ge(re_ready, l * 2 + 1)
                V.tensor_reduce(gsum, eg, AX.X, ALU.add)
                dve.drain()
                V.reciprocal(gsum, gsum)
                dve.drain()
                TT(gp8[:, :, 0:NG], eg, wide(gsum, NG), ALU.mult)
                dve.drain()
                for th in range(TH):
                    V.max(g8[:, th, :], gp8[:, th, :])
                dve.drain()
                for th in range(TH):
                    V.max_index(gi[:, th * 8:th * 8 + 8], g8[:, th, :], gp8[:, th, :])
                dve.drain()
                V.tensor_copy(gif, gi.rearrange("p (h n) -> p h n", h=TH))
                dve.drain()
                iot = iota[:, 0:8].unsqueeze(1).to_broadcast([P, TH, 8])
                TT(og, iot[:, :, 0:NG], gif[:, :, 0:1].to_broadcast([P, TH, NG]), ALU.is_equal)
                dve.drain()
                lge = lg[:, :, NG:NR].rearrange("p h (g n) -> p h g n", g=NG)
                TT(prod, lge, og.unsqueeze(3).to_broadcast([P, TH, NG, EPG]), ALU.mult)
                dve.drain()
                V.tensor_reduce(sel8, prod.rearrange("p h g n -> p h n g"), AX.X, ALU.add)
                dve.drain()
                V.tensor_reduce(emax, sel8, AX.X, ALU.max)
                dve.drain()
                TT(e8, sel8, wide(emax, EPG), ALU.subtract).then_inc(rl_ready, 1)
                dve.wait_ge(re_ready, l * 2 + 2)
                V.tensor_reduce(esum, e8, AX.X, ALU.add)
                dve.drain()
                V.reciprocal(esum, esum)
                dve.drain()
                TT(e8, e8, wide(esum, EPG), ALU.mult)
                dve.drain()
                for th in range(TH):
                    V.max(e8t[:, th, :], e8[:, th, :])
                dve.drain()
                for th in range(TH):
                    V.max_index(ei[:, th * 8:th * 8 + 8], e8t[:, th, :], e8[:, th, :])
                TT(den, e8t[:, :, 0], e8t[:, :, 1], ALU.add)
                dve.drain()
                V.tensor_copy(eif, ei.rearrange("p (h n) -> p h n", h=TH))
                V.reciprocal(den, den)
                dve.drain()
                TT(o1, iot, eif[:, :, 0:1].to_broadcast([P, TH, 8]), ALU.is_equal)
                TT(o2, iot, eif[:, :, 1:2].to_broadcast([P, TH, 8]), ALU.is_equal)
                TT(den, den, g8[:, :, 0], ALU.mult)
                dve.drain()
                TT(o1, o1, o2, ALU.add)
                TT(comb, e8, wide(den, EPG), ALU.mult)
                dve.drain()
                TT(comb, comb, o1, ALU.mult)
                dve.drain()
                cm = CMB.rearrange("p h (g n) -> p h g n", g=NG)
                for th in range(TH):
                    TT(cm[:, th], og[:, th].unsqueeze(2).to_broadcast([P, NG, EPG]),
                       comb[:, th].unsqueeze(1).to_broadcast([P, NG, EPG]), ALU.mult)
                dve.drain()
                with dve.Fori(0, NE) as e:
                    for th in range(TH):
                        last = TS(DIAG[:, th, :], ident[:, :], CMB[:, th, bass.ds(e, 1)], None, ALU.mult)
                    last.then_inc(diag_ready, 1)
                    dve.wait_ge(silu_done, l * NE + e + 2)
                    dve.wait_ge(up_done, l * NE + e + 1)
                    TT(GU, SGM, U_PS[:, :].rearrange("p (c t) -> p c t", c=2), ALU.mult)
                    dve.drain()
                    TT(EACT, GU, C_PS[:, 0:T].unsqueeze(1).to_broadcast([P, 2, T]), ALU.mult).then_inc(eact_ready, 1)
                dve.wait_ge(moe_out, l + 1)
                TT(xT[:, :, :], xT[:, :, :], TMP1, ALU.add)
                dve.drain().then_inc(layer_end1, 1)

            squares(xT[:, :, :], SQ)
            rstd(L * 4 + 1, L * 3 + 1, stat[:, 0:T], D, EPS1, VAR, RSTD)
            modulated(H, par(cst, COLC, "final_g"), None)
            dve.drain().then_inc(layer_end2, 1)
            dve.drain().then_inc(x2_ready, 1)

            def layer_norm(stat_value, root_value, tmp, g, b):
                STT(YC, xT[:, :, :], ALPHA, tmp, ALU.mult, ALU.add).then_inc(stat_in, 1)
                dve.wait_ge(stat_out, stat_value)
                TS(MEAN2[:, 0, :], stat[:, 0:T], 1.0 / D, None, ALU.mult)
                dve.drain()
                TT(YC, YC, over(MEAN2, KC), ALU.subtract)
                dve.drain()
                squares(YC, SQ2)
                rstd(stat_value + 1, root_value, stat[:, 0:T], D, EPS2, VAR2, RSTD2)
                TT(YC, YC, over(RSTD2, KC), ALU.mult)
                dve.drain()
                for k in range(KC):
                    TS(xT[:, k, :], YC[:, k, :], g[:, k:k + 1], b[:, k:k + 1], ALU.mult, ALU.add)
                dve.drain()

            with dve.Fori(0, L) as l:
                units = l * UNITS2 + BASE2
                stat0 = l * 4 + (L * 4 + 1)
                root0 = l * 2 + (L * 3 + 1)

                def moved2(u):
                    dve.wait_ge(lin_free, units + u + 1 + LB)

                dve.wait_ge(par2_loaded, l * 16 + 16)
                lq = par(par2, COL2, "lam_q")
                TT(rsm_wide(arena), lq, par(par2, COL2, "lam_k"), ALU.mult)
                dve.drain()
                V.tensor_reduce(lamb[:, 0:2], rsm_wide(arena).rearrange("p (q n) -> p q n", q=2), AX.X, ALU.add)\
                    .then_inc(lam_in, 1)
                dve.wait_ge(lam_exp, l + 1)
                TT(lamb[:, 4:5], lamb[:, 3:4], lamb[:, 2:3], ALU.subtract)
                dve.drain()
                TT(lamb[:, 5:6], lamb[:, 4:5], par(par2, COL2, "lambda_init"), ALU.subtract)
                dve.drain()
                dve.wait_ge(alibi_made, l + 1)

                def shifted(d):
                    b, h = divmod(d, DH)
                    kv = (b + 1) * P
                    s = SCO[d % 2]
                    dve.wait_ge(sc_done, l * 8 + d + 1)
                    STT(s[:, :, 0:kv], acc[:, 2 * (d % 2):2 * (d % 2) + 2, 0:kv], HD ** -0.5,
                        ALIBI[:, h, b, 0:kv].unsqueeze(1).to_broadcast([P, 2, kv]), ALU.mult, ALU.add)
                    dve.drain()
                    a = 4 * (d % 2)
                    V.tensor_reduce(rsm[:, a:a + 2], s[:, :, 0:kv], AX.X, ALU.max)
                    dve.drain()
                    TS(rsm[:, a:a + 2], rsm[:, a:a + 2], -1.0, None, ALU.mult).then_inc(smax_ready, 1)

                def combined(d):
                    b, h = divmod(d, DH)
                    kv = (b + 1) * P
                    a = 4 * (d % 2)
                    dve.wait_ge(e_ready, l * 8 + d + 1)
                    V.reciprocal(rsm[:, a + 2:a + 4], rsm[:, a + 2:a + 4])
                    dve.drain()
                    TT(rsm[:, a + 3:a + 4], rsm[:, a + 3:a + 4], lamb[:, 5:6], ALU.mult)
                    TS(EXO[d % 2][:, 0, 0:kv], EXO[d % 2][:, 0, 0:kv], rsm[:, a + 2:a + 3], None, ALU.mult)
                    dve.drain()
                    if d >= 2:
                        dve.wait_ge(tr_done, l * 8 + d - 1)
                    STT(ATT[d % 2][:, 0, 0:kv], EXO[d % 2][:, 1, 0:kv], rsm[:, a + 3:a + 4],
                        EXO[d % 2][:, 0, 0:kv], ALU.mult, ALU.add).then_inc(att_ready, 1)

                shifted(0)
                for d in range(8):
                    if d + 1 < 8:
                        shifted(d + 1)
                    combined(d)
                dve.wait_ge(dpv_out, l + 1)
                TT(DSQ, DIFF, DIFF, ALU.mult).then_inc(dsq_ready, 1)
                dve.wait_ge(dss_done, l + 1)
                TS(DRS, accT[:, 4:8, :], 1.0 / (2 * HD), EPS2, ALU.mult, ALU.add).then_inc(dvar_ready, 1)
                dve.wait_ge(dstd_ready, l + 1)
                V.reciprocal(DRS, DRS)
                dve.drain()
                TT(DIFF, DIFF, DRS, ALU.mult)
                dve.drain()
                TS(MIXT[:, 0:4], DIFF, par(par2, COL2, "subln_g"), par(par2, COL2, "keep"), ALU.mult, ALU.mult)\
                    .then_inc(mixt_ready, 1)
                mask4 = MASK.unsqueeze(1).to_broadcast([P, 4, SW])
                for w4 in range(2):
                    v = l * 2 + w4 + 1
                    dve.wait_ge(z_done, v)
                    TS(ZS, acc[:, :, 0:SW], HD ** -0.5, None, ALU.mult)
                    dve.drain()
                    STT(NA, ZS, -1.0, ZS, ALU.mult, ALU.min).then_inc(na_ready, 1)
                    dve.wait_ge(l1_ready, v)
                    STT(WW, ZS, 0.0, L1, ALU.min, ALU.subtract)
                    dve.drain()
                    TT(LF, WW, ZS, ALU.subtract)
                    dve.drain()
                    TT(LF, LF, mask4, ALU.mult).then_inc(lf_ready, 1)
                    dve.wait_ge(lat_done, v)
                    TT(ZS, WW, acc[:, :, 0:SW], ALU.add).then_inc(wl_ready, 1)
                    dve.wait_ge(we_ready, v)
                    TT(WW, NA, mask4, ALU.mult).then_inc(ww_ready, 1)
                moved2(UN_WO + 3)
                layer_norm(stat0 + 1, root0 + 1, TMP2, par(par2, COL2, "ln1_g"), par(par2, COL2, "ln1_b"))
                dve.drain().then_inc(x3_ready, 1)

                for th in range(TH):
                    moved2(UN_SC + 4 * th + 3)
                    S = SC[th]
                    V.memset(BS, 0.0)

                    def top16(vals, work, n, width, topv, topi):
                        for s in range(n):
                            V.max(topv[:, s, 0:8], vals[:, s, :])
                        dve.drain()
                        for s in range(n):
                            V.max_index(topi[:, s, 0:8], topv[:, s, 0:8], vals[:, s, :])
                            V.match_replace(work[:, s, :], topv[:, s, 0:8], vals[:, s, :], -3.0e38)
                        dve.drain()
                        for s in range(n):
                            V.max(topv[:, s, 8:16], work[:, s, :])
                        dve.drain()
                        for s in range(n):
                            V.max_index(topi[:, s, 8:16], topv[:, s, 8:16], work[:, s, :])
                        dve.drain()

                    top16(S, WORK, HP, NK, TOPV, TOPI)
                    V.tensor_copy(TOPF.rearrange("p h q j -> p (h q) j"), TOPI)
                    tv = TOPV.rearrange("p (h q) j -> p h q j", q=2)
                    for h in range(PH):
                        TT(CAND[:, h, :].rearrange("p (a b) -> p a b", a=16),
                           tv[:, h, 0, :].unsqueeze(2).to_broadcast([P, 16, 16]),
                           tv[:, h, 1, :].unsqueeze(1).to_broadcast([P, 16, 16]), ALU.add)
                    dve.drain()
                    top16(CAND, CWORK, PH, PTOP * PTOP, BV, BPH)
                    TT(BE, BV, BV[:, :, 0:1].to_broadcast([P, PH, PTOP]), ALU.subtract).then_inc(bl_ready, 1)
                    TS(BA, BP, 4, None, ALU.logical_shift_right)
                    TS(BB, BP, 15, None, ALU.bitwise_and)
                    dve.drain()
                    V.tensor_copy(BF[:, 0, :], BA)
                    V.tensor_copy(BF[:, 1, :], BB)
                    dve.drain()
                    for q in range(2):
                        TT(EQS, iota[:, 0:16].unsqueeze(1).to_broadcast([P, NSEL, 16]),
                           BF[:, q, :].unsqueeze(2).to_broadcast([P, NSEL, 16]), ALU.is_equal)
                        dve.drain()
                        for h in range(PH):
                            TT(EQH[:, h], EQH[:, h], TOPF[:, h, q, :].unsqueeze(1).to_broadcast([P, 16, 16]), ALU.mult)
                        dve.drain()
                        V.tensor_reduce(picks[:, q, th, :], EQS, AX.X, ALU.add)
                        dve.drain()
                    dve.wait_ge(be_ready, l * TH + th + 1)
                    V.tensor_reduce(BS, BE, AX.X, ALU.add)
                    dve.drain()
                    V.reciprocal(BS, BS)
                    dve.drain()
                    TT(picks[:, 2, th, :].rearrange("p (h j) -> p h j", h=PH), BE,
                       BS.unsqueeze(2).to_broadcast([P, PH, PTOP]), ALU.mult)
                    dve.drain()
                dve.drain().then_inc(routed, 1)

                dve.wait_ge(ptr_out, l + 1)
                dve.wait_ge(lin_free, units + UNITS2 + LB)
                V.memset(lamb[:, 8:9], 0.0)
                with dve.Fori(0, T // 8) as i:
                    for s in range(2):
                        for t in range(4):
                            at = bass.ds(i * 8 + (4 * s + t), 1)
                            TS(hotA[:, s, t, :], iota[:, :], picksT[:, 0, at], picksT[:, 2, at], ALU.is_equal, ALU.mult)
                            last = TS(hotB[:, s, t, :], iota[:, :], picksT[:, 1, at], None, ALU.is_equal)
                        last.then_inc(hot_ready, 1)
                    for s in range(2):
                        dve.wait_ge(g_done, l * (T // 4) + i * 2 + s + 1)
                        a = arena[:, :, bass.ds(i * 8 + 4 * s, 4)]
                        TT(a, a, acc[:, s, :].rearrange("p (t n) -> p n t", t=4), ALU.mult)
                dve.drain().then_inc(gated, 1)
                dve.wait_ge(v_out, l + 1)
                layer_norm(stat0 + 3, root0 + 2, TMP2, par(par2, COL2, "ln2_g"), par(par2, COL2, "ln2_b"))
                dve.drain().then_inc(layer_end2, 1)
                dve.drain().then_inc(x2_ready, 1)
            dve.drain().then_inc(final_ready, 1)


def rsm_wide(arena):
    return arena[:, 127, 0:2 * HD]


def kernel(**inputs):
    import concourse.bacc as _bacc
    from concourse.bass_utils import run_bass_kernel_spmd as _run

    f = {k: np.asarray(v) for k, v in inputs.items()}
    f32 = np.float32

    def cols(v):
        return v.reshape(-1, P).T

    def rows(v):
        return np.broadcast_to(v.reshape(1, -1), (P, v.size))

    def k_tiles(w, order=None):
        n = w.shape[1] // 256
        t = w.reshape(-1, P, n, 256).transpose(2, 1, 0, 3).reshape(n, P, -1)
        return t if order is None else t[order]

    stream = np.zeros((TILES, P, TILE), f32)
    at = 0

    def put(t):
        nonlocal at
        stream[at:at + t.shape[0], :, 0:t.shape[2]] = t
        at += t.shape[0]

    for l in range(L):
        put(k_tiles(f["w_ada"][l]))
        put(k_tiles(f["w_in"][l], [0, 2, 1, 3] + list(range(4, 14))))
        put(f["pool_w"][l].transpose(1, 0, 2).reshape(1, P, -1))
        put(f["w_conv_out"][l].reshape(CC, P, 2, 512).transpose(2, 1, 0, 3).reshape(2, P, -1))
        put(k_tiles(f["w_out"][l]))
        wg, wu, wd = f["w_expert_gate"][l], f["w_expert_up"][l], f["w_expert_down"][l]
        down = wd.reshape(NE, 2, P, D).transpose(0, 2, 1, 3).reshape(NE, P, -1)
        put(k_tiles(wg[0]))
        put(k_tiles(wu[0]))
        for e in range(NE - 1):
            put(k_tiles(wg[e + 1]))
            put(down[e:e + 1])
            put(k_tiles(wu[e + 1]))
        put(down[NE - 1:NE])
    for l in range(L):
        put(k_tiles(f["w_in_2"][l]))
        put(k_tiles(f["w_o_2"][l]))
        put(k_tiles(f["w_query_2"][l]))
        put(f["sub_keys_2"][l].transpose(3, 0, 1, 2).reshape(1, P, -1))
        u = f["expert_u_2"][l].reshape(P, U_T, 2, KC, P)
        put(u.transpose(1, 4, 2, 3, 0).reshape(U_T, P, -1))
        v = f["expert_v_2"][l].reshape(P, U_T, 2 * D)
        put(v.transpose(1, 0, 2))
    assert at == TILES

    par1 = np.stack([np.concatenate([
        cols(f["mixer_norm_g"][l]), cols(f["b_ada"][l]),
        f["conv_w"][l].T.reshape(CC, P, CK).transpose(1, 0, 2).reshape(P, -1), cols(f["conv_b"][l]),
        cols(f["conv_ln_g"][l]), cols(f["conv_ln_b"][l]), cols(f["b_conv_out"][l]), cols(f["pool_scale"][l]),
        cols(f["ffn_norm_g"][l]),
        np.concatenate([f["w_router_group"][l], f["w_router_expert"][l]], axis=1)
        .reshape(KC, P, NR).transpose(1, 0, 2).reshape(P, -1),
        rows(np.concatenate([f["b_router_group"][l], f["b_router_expert"][l]]))], axis=1) for l in range(L)])
    lambda_init = [0.8 - 0.6 * math.exp(-0.3 * l) for l in range(L)]
    par2 = np.stack([np.concatenate([
        cols(f["subln_g_2"][l]), np.full((P, 1), 1.0 - lambda_init[l], f32), np.full((P, 1), lambda_init[l], f32),
        cols(f["ln1_g_2"][l]), cols(f["ln1_b_2"][l]), cols(f["ln2_g_2"][l]), cols(f["ln2_b_2"][l]),
        rows(np.concatenate([f["lam_q1_2"][l], f["lam_q2_2"][l]])),
        rows(np.concatenate([f["lam_k1_2"][l], f["lam_k2_2"][l]]))], axis=1) for l in range(L)])
    consts = np.concatenate([cols(f["final_norm_g"]), cols(f["c"][0])], axis=1)
    inv = np.stack([1.0 / np.minimum(np.arange(1, T + 1), 2 << g) for g in range(CC)]).astype(f32)
    arrays = {
        "wstream": stream,
        "x_in": f["x"][0].T.reshape(KC, P, T).transpose(1, 0, 2),
        "params1": par1, "params2": par2, "consts": consts,
        "inv_count": np.broadcast_to(inv[None], (P, CC, T)),
    }
    nc = _bacc.Bacc("TRN2", target_bir_lowering=False, num_devices=1)
    aps = {}
    for name in arrays:
        arrays[name] = np.ascontiguousarray(arrays[name])
        aps[name] = nc.dram_tensor(name, arrays[name].shape, F32, kind="ExternalInput").ap()
    out = nc.dram_tensor("out", (P, KC, T), F32, kind="ExternalOutput").ap()
    program(nc, aps["wstream"], aps["x_in"], aps["params1"], aps["params2"], aps["consts"], aps["inv_count"], out)
    r = _run(nc, [arrays], core_ids=[0])
    return r.results[0]["out"].transpose(1, 0, 2).reshape(D, T).T.reshape(1, T, D)
```

```python
import math
from contextlib import ExitStack

import concourse.bass as bass
import numpy as np
from concourse import mybir

F32 = mybir.dt.float32
BF16 = mybir.dt.bfloat16
F32R = mybir.dt.float32r
U32 = mybir.dt.uint32
ALU = mybir.AluOpType
ACT = mybir.ActivationFunctionType
AX = mybir.AxisListType

P = 128
D = 1024
T = 256
L = 2
KC = D // P
TH = T // P
CK = 31
DCONV = 512
CC = DCONV // P
NG, EPG = 4, 8
NE = NG * EPG
NR = NG + NE
EPS1, EPS2 = 1e-6, 1e-5
HD = 64
DH, SH = 4, 8
PH, PTOP, NK = 8, 16, 128
HP = PH * 2
NSEL = PH * PTOP
ALPHA = (2.0 * L) ** 0.25
NEG = -1.0e30

SLOTS = 3
TILE = 2048
HALF = TILE // 2
IN_T, POOL_T, CONV_T, OUT_T = 14, 1, 2, 4
J_IN = 0
J_POOL = J_IN + IN_T
J_CONV = J_POOL + POOL_T
J_OUT = J_CONV + CONV_T
J_MOE = J_OUT + OUT_T
TILES1 = J_MOE + 3 * NE
IN2_T, WO_T, WQ_T, KEY_T, U_T = 12, 4, 8, 1, NK // 2
J_WO = IN2_T
J_WQ = J_WO + WO_T
J_KEY = J_WQ + WQ_T
J_U = J_KEY + KEY_T
J_V = J_U + U_T
TILES2 = J_V + U_T
TILES = L * (TILES1 + TILES2)
HALVES1, HALVES2 = 2 * 3 * NE, 2 * 2 * U_T
C_V = 2 * U_T

ADA_G = 4
ADA_GROUPS = L * 6 * D // 256 // ADA_G
ADA_BUFS = 3
assert TILES1 % SLOTS == 0 and TILES2 % SLOTS == 0

HEAD = 10
G4 = T // 4

LB = 3
UN_POOL, UN_CONV, UN_OUT, UN_ROUT = 14, 18, 22, 26
UNITS1 = 27
UN_WO, UN_WQ, UN_SC, UN_U = 12, 16, 24, 32
UNITS2 = UN_U + U_T
BASE2 = L * UNITS1
PARTS1, PARTS2 = 6, 7
assert UNITS1 % LB == 0 and UNITS2 % LB == 0


def columns(parts):
    at, out = 0, {}
    for name, n in parts:
        out[name] = (at, at + n)
        at += n
    return out, at


COL1, NCOL1 = columns([("norm_g", KC), ("b_ada", 6 * KC), ("conv_w", CC * CK), ("conv_b", CC),
                       ("ln_g", CC), ("ln_b", CC), ("b_out", KC), ("pool_scale", KC), ("ffn_g", KC),
                       ("router_w", KC * NR), ("router_b", NR)])
COL2, NCOL2 = columns([("subln_g", 1), ("keep", 1), ("lambda_init", 1), ("ln1_g", KC), ("ln1_b", KC),
                       ("ln2_g", KC), ("ln2_b", KC), ("lam_q", 2 * HD), ("lam_k", 2 * HD)])
COLC, NCOLC = columns([("final_g", KC), ("c", KC)])


def program(nc, w_ada, wstream, x_in, params1, params2, consts, inv_count, out):
    ctx = ExitStack()
    with ctx:
        def sb(name, shape, dt=F32):
            return ctx.enter_context(nc.sbuf_tensor(name, shape, dt))

        def sem(name):
            return ctx.enter_context(nc.semaphore(name))

        slot = [sb(f"slot{i}", [P, TILE]) for i in range(SLOTS)]
        w_hi = [sb(f"w_hi{i}", [P, HALF], F32R) for i in range(2)]
        w_lo = [sb(f"w_lo{i}", [P, HALF], F32R) for i in range(2)]
        arena = sb("arena", [P, NK, T])
        xT = sb("xT", [P, KC, T])
        iota = sb("iota", [P, P])
        ident = sb("ident", [P, P])
        ones = sb("ones", [P, P])
        later = sb("later", [P, P])
        zeros = sb("zeros", [P, P], BF16)
        par1 = sb("par", [P, max(NCOL1, NCOL2)])
        par2 = par1
        cst = sb("cst", [P, NCOLC])
        c_act = sb("c_act", [P, KC])
        mods = sb("mods", [P, L * 6 * KC])
        mod = sb("mod", [P, 6 * KC])
        gain = sb("gain", [P, 2 * KC])
        picksT = sb("picksT", [P, 3, T])
        eact = sb("eact", [P, 2, 2, T], F32R)
        lamb = sb("lamb", [P, 16])
        rsm = sb("rsm", [P, 16])

        REGION = nc.sbuf_usable_end // 32 * 32 - 4 * 2 * KC * T
        assert nc.sbuf_base <= REGION
        x_parts = nc.alloc_sbuf_tensor_at("x_parts", [P, 2, KC, T], F32R, offset=REGION)
        HOTS = 3
        hot = nc.alloc_sbuf_tensor_at("hot", [P, HOTS, 2, 4, P], F32, offset=REGION)
        gated_hot = nc.alloc_sbuf_tensor_at("gated_hot", [P, 2, 4, P], F32, offset=REGION + 4 * HOTS * 8 * P)
        x_hi, x_lo = x_parts[:, 0], x_parts[:, 1]
        act_hi = [x_parts[:, 0, b, :] for b in range(2)]
        act_lo = [x_parts[:, 1, b, :] for b in range(2)]

        def par(t, cols, name):
            a, b = cols[name]
            return t[:, a:b]

        def area(at, n):
            return arena[:, at:at + n, :]

        def flat(at, n):
            return arena[:, at:at + n, :].rearrange("p a b -> p (a b)")

        ADA_IN = [flat(32 * b, 32).rearrange("p (j k n) -> p j k n", j=ADA_G, k=KC) for b in range(ADA_BUFS)]
        ADA_SUM = [area(105 + ADA_G * b, ADA_G) for b in range(2)]
        SQ, H = area(0, 8), area(8, 8)
        UA, SG = area(16, 4), area(20, 4)
        GA, GB = area(24, 8), area(32, 8)
        YA, YB, MIX = area(40, 8), area(48, 8), area(56, 8)
        VPAD = flat(64, 5)[:, 0:CC * (T + CK - 1)].rearrange("p (c t) -> p c t", c=CC)
        UP, CV = area(69, 4), area(73, 4)
        PPAD = [flat(77 + 5 * i, 5)[:, 0:CC * (T + 16)].rearrange("p (c t) -> p c t", c=CC) for i in range(4)]
        PLD, INVC, TMP1 = area(97, 4), area(101, 4), area(105, 8)
        MEAN, VAR, RSTD = area(113, 1), area(114, 1), area(115, 1)
        CVN, CVS = area(116, 4), area(120, 4)
        RT = flat(73, 4)
        SGM, EACT, GU = area(77, 2), area(79, 2), area(81, 2)
        DIAG = flat(83, 1).rearrange("p (h t) -> p h t", h=TH)
        CMB = flat(84, 1)[:, 0:TH * NE].rearrange("p (h e) -> p h e", h=TH)

        DQ, DK, SQT, SKT = area(0, 4), area(4, 4), area(8, 4), area(12, 4)
        DV = flat(16, 4).rearrange("p (h n) -> p h n", h=TH)
        SV = flat(20, 4).rearrange("p (h n) -> p h n", h=TH)
        ALIBI = area(24, 8).rearrange("p (h b) t -> p h b t", h=DH)
        SCO = [area(32 + 2 * i, 2) for i in range(2)]
        EXO = [area(36 + 2 * i, 2) for i in range(2)]
        ATT = [area(40 + i, 1) for i in range(2)]
        ATT_T = area(42, 8).rearrange("p (h b) t -> p h b t", h=DH)
        DIFF, DSQ, DRS = area(50, 4), area(54, 4), area(58, 4)
        MIXT = area(62, 8)
        SW = 384
        ZS, NA, L1, LF, WW = (flat(70 + 6 * i, 6).rearrange("p (g t) -> p g t", g=4) for i in range(5))
        MASK = flat(100, 2)[:, 0:SW]
        YC, SQ2, TMP2 = area(0, 8), area(8, 8), area(16, 8)
        MEAN2, VAR2, RSTD2 = area(24, 1), area(25, 1), area(26, 1)
        QT = area(28, 16)
        SC = [flat(112 + 8 * h, 8).rearrange("p (s n) -> p s n", s=HP) for h in range(TH)]
        WORK = flat(64, 8).rearrange("p (s n) -> p s n", s=HP)
        CAND, CWORK = area(72, 8), area(80, 8)
        EQ = area(88, 8).rearrange("p (h j) (k a) -> p h j k a", h=PH, k=16)
        EQS = flat(88, 8).rearrange("p (s a) -> p s a", a=16)
        EQH = flat(88, 8).rearrange("p (h j a) -> p h j a", h=PH, j=16)
        TOPV = flat(96, 1).rearrange("p (s j) -> p s j", s=HP)
        TOPI = flat(97, 1).bitcast(U32).rearrange("p (s j) -> p s j", s=HP)
        TOPF = flat(98, 1).rearrange("p (h q j) -> p h q j", h=PH, q=2)
        BV = flat(99, 1)[:, 0:NSEL].rearrange("p (h j) -> p h j", h=PH)
        BP = flat(100, 1)[:, 0:NSEL].bitcast(U32)
        BPH = BP.rearrange("p (h j) -> p h j", h=PH)
        BA = flat(101, 1)[:, 0:NSEL].bitcast(U32)
        BB = flat(102, 1)[:, 0:NSEL].bitcast(U32)
        BF = flat(103, 1).rearrange("p (q s) -> p q s", q=2)
        BE = flat(104, 1).rearrange("p (t h j) -> p t h j", t=TH, h=PH)
        BS = flat(105, 1)[:, 0:TH * PH].rearrange("p (t h) -> p t h", t=TH)
        picks = flat(106, 3).rearrange("p (q t s) -> p q t s", q=3, t=TH)

        acc = ctx.enter_context(nc.psum_tensor("acc", [P, 4, 512], F32))
        lin = [ctx.enter_context(nc.psum_tensor(f"lin{i}", [P, 512], F32)) for i in range(LB)]
        stat = ctx.enter_context(nc.psum_tensor("stat", [P, 512], F32))
        accT = acc[:, :, :].rearrange("p b (c t) -> p (b c) t", c=2)
        G_PS, U_PS, C_PS = lin[0], lin[1], lin[2]

        w_loaded = [sem(f"w_loaded{i}") for i in range(SLOTS)]
        slot_free = [sem(f"slot_free{i}") for i in range(SLOTS)]
        hi_ready = sem("hi_ready")
        split_ready = sem("split_ready")
        half_done = sem("half_done")
        ada_loaded = [sem(f"ada_loaded{i}") for i in range(ADA_BUFS)]
        ada_free, part_sums, sums_used = sem("ada_free"), sem("part_sums"), sem("sums_used")
        small_loaded = sem("small_loaded")
        x_loaded = sem("x_loaded")
        par1_loaded, par2_loaded = sem("par1_loaded"), sem("par2_loaded")
        inv_loaded = sem("inv_loaded")
        consts_made = sem("consts_made")
        zeros_made = sem("zeros_made")
        pads_made = sem("pads_made")
        c_ready = sem("c_ready")
        part_done = sem("part_done")
        lin_free = sem("lin_free")
        stat_in, stat_out = sem("stat_in"), sem("stat_out")
        var_ready, std_ready = sem("var_ready"), sem("std_ready")
        h_ready = sem("h_ready")
        pooled_ready, mixed_ready = sem("pooled_ready"), sem("mixed_ready")
        cvn_ready, cvs_ready = sem("cvn_ready"), sem("cvs_ready")
        h2_ready = sem("h2_ready")
        h2_split, x3_split = sem("h2_split"), sem("x3_split")
        rl_ready, re_ready = sem("rl_ready"), sem("re_ready")
        up_done = sem("up_done")
        silu_done, diag_ready, eact_ready = sem("silu_done"), sem("diag_ready"), sem("eact_ready")
        moe_done, moe_out = sem("moe_done"), sem("moe_out")
        layer_end1, layer_end2 = sem("layer_end1"), sem("layer_end2")
        x2_ready = sem("x2_ready")
        alibi_made = sem("alibi_made")
        lam_in, lam_exp = sem("lam_in"), sem("lam_exp")
        sc_done, smax_ready, e_ready = sem("sc_done"), sem("smax_ready"), sem("e_ready")
        att_ready, tr_done, tr_out = sem("att_ready"), sem("tr_done"), sem("tr_out")
        dpv_done, dpv_out, dsq_ready, dss_done = sem("dpv_done"), sem("dpv_out"), sem("dsq_ready"), sem("dss_done")
        dvar_ready, dstd_ready = sem("dvar_ready"), sem("dstd_ready")
        z_done, na_ready, l1_ready, lf_ready = sem("z_done"), sem("na_ready"), sem("l1_ready"), sem("lf_ready")
        lat_done, wl_ready, we_ready, ww_ready = sem("lat_done"), sem("wl_ready"), sem("we_ready"), sem("ww_ready")
        spv_done, spv_out = sem("spv_done"), sem("spv_out")
        mixt_ready, x3_ready = sem("mixt_ready"), sem("x3_ready")
        bl_ready, be_ready = sem("bl_ready"), sem("be_ready")
        routed = sem("routed")
        ptr_done, ptr_out = sem("ptr_done"), sem("ptr_out")
        hot_ready, scaled_hot = sem("hot_ready"), sem("scaled_hot")
        g_done, gated = sem("g_done"), sem("gated")
        v_done, v_out = sem("v_done"), sem("v_out")
        final_ready, stored = sem("final_ready"), sem("stored")

        block = ctx.enter_context(nc.Block())

        @block.sync
        def _(sp):
            sp.dma_start(cst[:, :], consts[:, :]).then_inc(small_loaded, 16)
            with sp.Fori(0, ADA_GROUPS // ADA_BUFS) as i:
                for b in range(ADA_BUFS):
                    sp.wait_ge(ada_free, i * ADA_BUFS + b + 1)
                    for j in range(ADA_G):
                        sp.dma_start(flat(32 * b + KC * j, KC), w_ada[i * (ADA_BUFS * ADA_G) + (b * ADA_G + j)])\
                          .then_inc(ada_loaded[b], 16)
            with sp.Fori(0, TILES // SLOTS) as i:
                for s in range(SLOTS):
                    sp.wait_ge(slot_free[s], i + 1)
                    sp.dma_start(slot[s][:, :], wstream[i * SLOTS + s]).then_inc(w_loaded[s], 16)

        @block.gpsimd
        def _(pool):
            pool.dma_start(xT[:, :, :], x_in[:, :, :]).then_inc(x_loaded, 16)
            pool.dma_start(INVC, inv_count[:, :, :]).then_inc(inv_loaded, 16)
            nc.gpsimd.iota(iota[:, :], [[1, P]], base=0, channel_multiplier=0,
                           allow_small_or_imprecise_dtypes=True)
            nc.gpsimd.memset(ones[:, :], 1.0)
            pool.drain()
            nc.gpsimd.affine_select(out=ident[:, :], in_=ones[:, :], compare_op=ALU.is_equal, fill=0.0,
                                    base=0, pattern=[[-1, P]], channel_multiplier=1)
            nc.gpsimd.affine_select(out=later[:, :], in_=ones[:, :], compare_op=ALU.is_gt, fill=0.0,
                                    base=0, pattern=[[-1, P]], channel_multiplier=1)
            pool.drain().then_inc(consts_made, 1)
            with pool.Fori(0, L) as l:
                pool.wait_ge(layer_end1, l + 1)
                pool.dma_start(par1[:, 0:NCOL1], params1[l]).then_inc(par1_loaded, 16)
                nc.gpsimd.memset(VPAD[:, :, 0:CK - 1], 0.0)
                for q in PPAD:
                    nc.gpsimd.memset(q[:, :, 0:16], 0.0)
                pool.drain().then_inc(pads_made, 1)
            pool.wait_ge(layer_end1, L + 1)
            with pool.Fori(0, L) as l:
                pool.wait_ge(layer_end2, l + 1)
                pool.dma_start(par2[:, 0:NCOL2], params2[l]).then_inc(par2_loaded, 16)
                for b in range(TH):
                    for h in range(DH):
                        nc.gpsimd.iota(ALIBI[:, h, b, :], [[-1, T]], base=b * P, channel_multiplier=1,
                                       allow_small_or_imprecise_dtypes=True)
                pool.drain()
                for h in range(DH):
                    slope = 2.0 ** (-8.0 * (h + 1) / DH)
                    nc.gpsimd.tensor_scalar(ALIBI[:, h, :, :], ALIBI[:, h, :, :], -slope, None, ALU.mult)
                pool.drain()
                for b in range(TH):
                    for h in range(DH):
                        nc.gpsimd.affine_select(out=ALIBI[:, h, b, :], in_=ALIBI[:, h, b, :],
                                                compare_op=ALU.is_ge, fill=NEG, base=b * P,
                                                pattern=[[-1, T]], channel_multiplier=1)
                nc.gpsimd.memset(MASK, 1.0)
                pool.drain()
                for a in (0, 2 * P):
                    nc.gpsimd.affine_select(out=MASK[:, a:a + P], in_=MASK[:, a:a + P], compare_op=ALU.is_gt,
                                            fill=0.0, base=0, pattern=[[1, P]], channel_multiplier=-1)
                pool.drain().then_inc(alibi_made, 1)

        @block.tensor
        def _(pe):
            mm = nc.tensor.matmul

            def loaded(count, j):
                pe.wait_ge(w_loaded[j % SLOTS], (count + j // SLOTS + 1) * 16)
                return slot[j % SLOTS]

            def column_sum(value, src, n):
                pe.wait_ge(stat_in, value)
                for k in range(n):
                    last = mm(stat[:, 0:T], ones[:, :], src[:, k, :], start=(k == 0), stop=(k == n - 1))
                last.then_inc(stat_out, 1)

            def linear(count, j, rhs, unit, base_unit):
                w = loaded(count, j)
                pe.wait_ge(lin_free, base_unit + unit + 1)
                bank = lin[unit % LB]
                wv = w[:, :].rearrange("p (k n) -> p k n", k=KC)
                for n in range(2):
                    for k in range(KC):
                        last = mm(bank[:, n * T:(n + 1) * T], wv[:, k, n * P:(n + 1) * P], rhs[:, k, :],
                                  start=(k == 0), stop=(k == KC - 1))
                last.then_inc(slot_free[j % SLOTS], 1)

            for s in range(SLOTS):
                pe.sem_inc(slot_free[s], 1)
            pe.sem_inc(half_done, 2)
            pe.sem_inc(sums_used, 2)
            pe.sem_inc(g_done, 2)
            pe.wait_ge(consts_made, 1)
            pe.wait_ge(zeros_made, 1)
            pe.wait_ge(c_ready, 1)

            def open_acc():
                for b in range(4):
                    mm(acc[:, b, :], zeros[:, :], zeros[:, 0:1].to_broadcast([P, 512]), start=True, stop=False)

            def close_acc(done):
                for b in range(4):
                    last = mm(acc[:, b, :], zeros[:, :], zeros[:, 0:1].to_broadcast([P, 512]), start=False, stop=True)
                last.then_inc(done, 1)

            def products(out, hi, lo, x, start, stop):
                n = len(x)
                for i, (cols_, (xh, xl)) in enumerate(x):
                    mm(out, hi[:, cols_], xh, start=(start and i == 0), stop=False)
                    mm(out, hi[:, cols_], xl, start=False, stop=False)
                    last = mm(out, lo[:, cols_], xh, start=False, stop=(stop and i == n - 1))
                return last

            def half_ready(rings, c, j0, parity):
                j = j0 + c // 2
                if c % 2 == 0:
                    pe.wait_ge(split_ready, parity + c // 2 + 1)
                else:
                    pe.wait_ge(slot_free[j % SLOTS], rings + j // SLOTS + 2)
                return w_hi[c % 2], w_lo[c % 2]

            with pe.Fori(0, ADA_GROUPS // 2) as i:
                for b in range(2):
                    pe.wait_ge(part_sums, i * 2 + b + 1)
                    for n in range(2 * ADA_G):
                        last = mm(acc[:, 0, bass.ds((i * 2 + b) * (2 * ADA_G) + n, 1)],
                                  ADA_SUM[b][:, n // 2, (n % 2) * P:(n % 2 + 1) * P], ones[:, 0:1],
                                  start=True, stop=True)
                    last.then_inc(sums_used, 1)

            with pe.Fori(0, L) as l:
                rings = l * (TILES1 // SLOTS)
                units = l * UNITS1
                column_sum(l * 4 + 1, SQ, KC)
                pe.wait_ge(h_ready, l + 1)
                for j in range(IN_T):
                    linear(rings, J_IN + j, H, j, units)
                pe.wait_ge(pooled_ready, l + 1)
                w = loaded(rings, J_POOL)
                for g in range(CC):
                    pe.wait_ge(lin_free, units + UN_POOL + g + 1)
                    bank = lin[(UN_POOL + g) % LB]
                    for n in range(2):
                        last = mm(bank[:, n * T:(n + 1) * T], w[:, (2 * g + n) * P:(2 * g + n + 1) * P],
                                  PLD[:, g, :], start=True, stop=True)
                    last.then_inc(slot_free[J_POOL % SLOTS] if g == CC - 1 else part_done, 1)
                column_sum(l * 4 + 2, CV, CC)
                column_sum(l * 4 + 3, SQ, CC)
                pe.wait_ge(cvs_ready, l + 1)
                for j in range(CONV_T):
                    w = loaded(rings, J_CONV + j)[:, :].rearrange("p (k n) -> p k n", k=CC)
                    for half in range(2):
                        u = UN_CONV + 2 * j + half
                        pe.wait_ge(lin_free, units + u + 1)
                        for n in range(2):
                            for k in range(CC):
                                m = (2 * half + n) * P
                                last = mm(lin[u % LB][:, n * T:(n + 1) * T], w[:, k, m:m + P], CVS[:, k, :],
                                          start=(k == 0), stop=(k == CC - 1))
                        last.then_inc(slot_free[(J_CONV + j) % SLOTS] if half else part_done, 1)
                pe.wait_ge(mixed_ready, l + 1)
                for j in range(OUT_T):
                    linear(rings, J_OUT + j, MIX, UN_OUT + j, units)
                column_sum(l * 4 + 4, SQ, KC)
                pe.wait_ge(h2_ready, l + 1)
                pe.wait_ge(lin_free, units + UN_ROUT + 1)
                rw = par(par1, COL1, "router_w").rearrange("p (k n) -> p k n", k=KC)
                for th in range(TH):
                    for k in range(KC):
                        last = mm(lin[UN_ROUT % LB][:, th * NR:(th + 1) * NR], H[:, k, th * P:(th + 1) * P],
                                  rw[:, k, :], start=(k == 0), stop=(k == KC - 1))
                last.then_inc(part_done, 1)
                pe.wait_ge(lin_free, units + UNITS1 + LB)
                open_acc()

                parity = l * (HALVES1 // 2)
                e0 = l * NE
                pe.wait_ge(h2_split, l + 1)

                def expert_in(c, i, e, bank, free):
                    pe.wait_ge(free, e + 1)
                    for n in range(2):
                        hi, lo = half_ready(rings + i, c + n, J_MOE, parity + i * 3)
                        x = [(slice(k * P, (k + 1) * P), (x_hi[:, k, :], x_lo[:, k, :])) for k in range(KC)]
                        products(bank[:, n * T:(n + 1) * T], hi, lo, x, True, True).then_inc(half_done, 1)

                def spread_weights(e):
                    pe.wait_ge(diag_ready, e + 1)
                    for th in range(TH):
                        last = mm(C_PS[:, th * P:(th + 1) * P], ones[:, :], DIAG[:, th, :], start=True, stop=True)
                    last.then_inc(up_done, 1)

                def expert_down(c, i, e):
                    pe.wait_ge(eact_ready, e + 2)
                    for half in range(2):
                        hi, lo = half_ready(rings + i, c + half, J_MOE, parity + i * 3)
                        for n in range(4):
                            x = [(slice(k * 512 + n * P, k * 512 + (n + 1) * P), (eact[:, 0, k, :], eact[:, 1, k, :]))
                                 for k in range(2)]
                            last = products(accT[:, 4 * half + n, :], hi, lo, x, False, False)
                        last.then_inc(half_done, 1)

                expert_in(0, 0, e0, G_PS, silu_done)
                expert_in(2, 0, e0, U_PS, eact_ready)
                spread_weights(e0)
                with pe.Fori(0, NE - 1) as i:
                    expert_in(4, i, e0 + i + 1, G_PS, silu_done)
                    expert_down(6, i, e0 + i)
                    expert_in(8, i, e0 + i + 1, U_PS, eact_ready)
                    spread_weights(e0 + i + 1)
                expert_down(HALVES1 - 2, 0, e0 + NE - 1)
                close_acc(moe_done)

            column_sum(L * 4 + 1, SQ, KC)

            with pe.Fori(0, L) as l:
                rings = l * (TILES2 // SLOTS) + L * TILES1 // SLOTS
                units = l * UNITS2 + BASE2
                stat0 = l * 4 + (L * 4 + 1)
                pe.wait_ge(x2_ready, l + 1)
                for j in range(IN2_T):
                    if j in (4, 5, 10, 11):
                        w = loaded(rings, j)
                        pe.wait_ge(lin_free, units + j + 1)
                        wv = w[:, :].rearrange("p (k n) -> p k n", k=KC)
                        for th in range(TH):
                            for k in range(KC):
                                last = mm(lin[j % LB][:, th * T:(th + 1) * T], xT[:, k, th * P:(th + 1) * P],
                                          wv[:, k, :], start=(k == 0), stop=(k == KC - 1))
                        last.then_inc(slot_free[j % SLOTS], 1)
                    else:
                        linear(rings, j, xT, j, units)

                def scores(d):
                    b, h = divmod(d, DH)
                    if d >= 2:
                        pe.wait_ge(smax_ready, l * 8 + d - 1)
                    for m in range(2):
                        r = slice(m * HD, (m + 1) * HD)
                        last = mm(acc[:, 2 * (d % 2) + m, 0:(b + 1) * P], DQ[r, h, b * P:(b + 1) * P],
                                  DK[r, h, 0:(b + 1) * P], start=True, stop=True)
                    last.then_inc(sc_done, 1)

                pe.wait_ge(lin_free, units + IN2_T + LB)
                scores(0)
                scores(1)
                for d in range(8):
                    b, h = divmod(d, DH)
                    pe.wait_ge(att_ready, l * 8 + d + 1)
                    if d >= 2:
                        pe.wait_ge(tr_out, l * 8 + d - 1)
                    for kb in range(b + 1):
                        last = nc.tensor.transpose(lin[d % 2][:, kb * P:(kb + 1) * P],
                                                   ATT[d % 2][:, 0, kb * P:(kb + 1) * P], ident[:, :])
                    last.then_inc(tr_done, 1)
                    if d + 2 < 8:
                        scores(d + 2)
                pe.wait_ge(tr_out, l * 8 + 8)
                for h in range(DH):
                    o = accT[:, h, :]
                    mm(o, DV[:, 0, h * P:(h + 1) * P], ATT_T[:, h, 0, :], start=True, stop=False)
                    last = mm(accT[:, h, P:T], DV[:, 1, h * P:(h + 1) * P], ATT_T[:, h, 1, P:T],
                              start=False, stop=True)
                last.then_inc(dpv_done, 1)
                pe.wait_ge(dsq_ready, l + 1)
                for q in range(2):
                    last = mm(acc[:, 2 + q, :], ones[:, :], DSQ[:, 2 * q:2 * q + 2, :], start=True, stop=True)
                last.then_inc(dss_done, 1)
                for w4 in range(2):
                    if w4 == 0:
                        pe.wait_ge(dvar_ready, l + 1)
                    for g in range(4):
                        hh = 4 * w4 + g
                        r, c = slice((hh % 2) * HD, (hh % 2 + 1) * HD), hh // 2
                        mm(acc[:, g, 0:T], SKT[r, c, 0:P], SQT[r, c, :], start=True, stop=True)
                        last = mm(acc[:, g, T:SW], SKT[r, c, P:T], SQT[r, c, P:T], start=True, stop=True)
                    last.then_inc(z_done, 1)
                    pe.wait_ge(lf_ready, l * 2 + w4 + 1)
                    for g in range(4):
                        mm(acc[:, g, 0:T], later[:, :], LF[:, g, 0:T], start=True, stop=False)
                        mm(acc[:, g, P:T], ones[:, :], LF[:, g, T:SW], start=False, stop=True)
                        last = mm(acc[:, g, T:SW], later[:, :], LF[:, g, T:SW], start=True, stop=True)
                    last.then_inc(lat_done, 1)
                    pe.wait_ge(ww_ready, l * 2 + w4 + 1)
                    for g in range(4):
                        hh = 4 * w4 + g
                        r, c = slice((hh % 2) * HD, (hh % 2 + 1) * HD), g // 2
                        mm(stat[r, c * T:(c + 1) * T], SV[:, 0, hh * HD:(hh + 1) * HD], WW[:, g, 0:T],
                           start=True, stop=False)
                        last = mm(stat[r, c * T + P:(c + 1) * T], SV[:, 1, hh * HD:(hh + 1) * HD],
                                  WW[:, g, T:SW], start=False, stop=True)
                    last.then_inc(spv_done, 1)
                    if w4 == 0:
                        pe.wait_ge(spv_out, l * 2 + 1)
                pe.wait_ge(mixt_ready, l + 1)
                pe.wait_ge(spv_out, l * 2 + 2)
                for j in range(WO_T):
                    linear(rings, J_WO + j, MIXT, UN_WO + j, units)
                column_sum(stat0 + 1, YC, KC)
                column_sum(stat0 + 2, SQ2, KC)
                pe.wait_ge(x3_ready, l + 1)
                for j in range(WQ_T):
                    linear(rings, J_WQ + j, xT, UN_WQ + j, units)
                pe.wait_ge(lin_free, units + UN_SC + LB)
                pe.wait_ge(x3_split, l + 1)
                w = loaded(rings, J_KEY)[:, :].rearrange("p (s n) -> p s n", s=HP)
                for s in range(8):
                    th, q = divmod(s, 4)
                    pe.wait_ge(lin_free, units + UN_SC + s + 1)
                    for a in range(4):
                        hp = 4 * q + a
                        last = mm(lin[(UN_SC + s) % LB][:, a * P:(a + 1) * P], QT[:, hp, th * P:(th + 1) * P],
                                  w[:, hp, :], start=True, stop=True)
                    last.then_inc(slot_free[J_KEY % SLOTS] if s == 7 else part_done, 1)

                parity = l * (HALVES2 // 2) + L * (HALVES1 // 2)
                x = [(slice(k * P, (k + 1) * P), (x_hi[:, k, :], x_lo[:, k, :])) for k in range(KC)]

                def u_tile(j, i):
                    pe.wait_ge(lin_free, units + i * SLOTS + (UN_U + j + 1))
                    for a in range(2):
                        hi, lo = half_ready(rings + i, 2 * j + a, J_U, parity + i * SLOTS)
                        products(lin[(UN_U + j) % LB][:, a * T:(a + 1) * T], hi, lo, x, True, True)\
                            .then_inc(half_done, 1)

                with pe.Fori(0, HEAD) as i:
                    for s in range(SLOTS):
                        u_tile(s, i)
                pe.wait_ge(routed, l + 1)
                for q in range(3):
                    for th in range(TH):
                        a = q * TH + th
                        last = nc.tensor.transpose(acc[:, 2 + a // 4, (a % 4) * P:(a % 4 + 1) * P],
                                                   picks[:, q, th, :], ident[:, :])
                last.then_inc(ptr_done, 1)
                with pe.Fori(HEAD, U_T // SLOTS) as i:
                    for s in range(SLOTS):
                        u_tile(s, i)
                u_tile(U_T - 1, 0)

                def gate_group(g, i):
                    n = l * G4 + i * 6 + g
                    pe.wait_ge(scaled_hot, n + 1)
                    for t in range(4):
                        last = mm(acc[:, g % HOTS, t * P:(t + 1) * P], gated_hot[:, g % 2, t, :],
                                  hot[:, g % HOTS, 1, t, :], start=True, stop=True)
                    last.then_inc(g_done, 1)

                with pe.Fori(0, G4 // 6) as i:
                    for g in range(6):
                        gate_group(g, i)
                for g in range(G4 // 6 * 6, G4):
                    gate_group(g, 0)
                pe.wait_ge(gated, l + 1)
                open_acc()

                def v_tile(j, i):
                    for a in range(2):
                        hi, lo = half_ready(rings + i, 2 * j + a, J_V, parity + i * SLOTS + U_T)
                        for n in range(KC):
                            last = products(accT[:, n, :], hi, lo,
                                            [(slice(n * P, (n + 1) * P), (act_hi[a], act_lo[a]))], False, False)
                        last.then_inc(half_done, 1)

                with pe.Fori(0, U_T // SLOTS) as i:
                    for s in range(SLOTS):
                        v_tile(s, i)
                v_tile(U_T - 1, 0)
                close_acc(v_done)
                column_sum(stat0 + 3, YC, KC)
                column_sum(stat0 + 4, SQ2, KC)

        @block.scalar
        def _(act):
            A = nc.scalar.activation

            def tile_through(rings, j):
                act.wait_ge(slot_free[j % SLOTS], rings + j // SLOTS + 2)

            def high_part(rings, c, j0, number, arena_col=None):
                j = j0 + c // 2
                act.wait_ge(w_loaded[j % SLOTS], (rings + j // SLOTS + 1) * 16)
                act.wait_ge(half_done, number + c + 1)
                if arena_col is not None:
                    A(act_hi[c % 2].unsqueeze(1), arena[:, bass.ds(arena_col, 1), :], ACT.Copy)
                A(w_hi[c % 2][:, :], slot[j % SLOTS][:, (c % 2) * HALF:(c % 2 + 1) * HALF], ACT.Copy)\
                    .then_inc(hi_ready, 1)

            def halves_done(number):
                act.wait_ge(half_done, number + 2)

            def unit1(l, u):
                part = {14: 1, 15: 2, 16: 3, UN_CONV: 4, UN_CONV + 2: 5, UN_ROUT: 6}
                if u in part:
                    act.wait_ge(part_done, l * PARTS1 + part[u])
                elif u < UN_POOL:
                    tile_through(l * (TILES1 // SLOTS), J_IN + u)
                elif u < UN_CONV:
                    tile_through(l * (TILES1 // SLOTS), J_POOL)
                elif u < UN_OUT:
                    tile_through(l * (TILES1 // SLOTS), J_CONV + (u - UN_CONV) // 2)
                else:
                    tile_through(l * (TILES1 // SLOTS), J_OUT + u - UN_OUT)
                return lin[u % LB]

            def unit2(l, u):
                count = l * (TILES2 // SLOTS) + L * TILES1 // SLOTS
                if UN_SC <= u < UN_SC + 7:
                    act.wait_ge(part_done, l * PARTS2 + (L * PARTS1 + u - UN_SC + 1))
                elif u < UN_WO:
                    tile_through(count, u)
                elif u < UN_WQ:
                    tile_through(count, J_WO + u - UN_WO)
                elif u < UN_SC:
                    tile_through(count, J_WQ + u - UN_WQ)
                else:
                    tile_through(count, J_KEY)
                return lin[u % LB]

            def root(value, src, dst):
                act.wait_ge(var_ready, value)
                A(dst, src, ACT.Sqrt).then_inc(std_ready, 1)

            act.sem_inc(lin_free, LB)
            act.sem_inc(silu_done, 1)
            act.wait_ge(small_loaded, 16)
            A(c_act[:, :], par(cst, COLC, "c"), ACT.Silu).then_inc(c_ready, 1)

            with act.Fori(0, L) as l:
                units = l * UNITS1
                root(l * 3 + 1, VAR, RSTD)
                dsts = [UA[:, 0:2], SG[:, 0:2], UA[:, 2:4], SG[:, 2:4], UP[:, 0:2], UP[:, 2:4]]
                dsts += [GA[:, 2 * q:2 * q + 2] for q in range(4)] + [GB[:, 2 * q:2 * q + 2] for q in range(4)]
                for j, dst in enumerate(dsts):
                    func = ACT.Copy if j in (0, 2, 4, 5) else ACT.Sigmoid
                    A(dst, unit1(l, j)[:, :].rearrange("p (c t) -> p c t", c=2), func).then_inc(lin_free, 1)
                ps = par(par1, COL1, "pool_scale")
                for j in range(4):
                    bank = unit1(l, UN_POOL + j)
                    for n in range(2):
                        last = A(YB[:, 2 * j + n], bank[:, n * T:(n + 1) * T], ACT.Identity,
                                 scale=ps[:, 2 * j + n:2 * j + n + 1])
                    last.then_inc(lin_free, 1)
                root(l * 3 + 2, VAR, RSTD)
                act.wait_ge(cvn_ready, l + 1)
                g, b = par(par1, COL1, "ln_g"), par(par1, COL1, "ln_b")
                for k in range(CC):
                    last = A(CVS[:, k], CVN[:, k], ACT.Silu, scale=g[:, k:k + 1], bias=b[:, k:k + 1])
                last.then_inc(cvs_ready, 1)
                bo = par(par1, COL1, "b_out")
                for j in range(4):
                    bank = unit1(l, UN_CONV + j)
                    for n in range(2):
                        last = A(YA[:, 2 * j + n], bank[:, n * T:(n + 1) * T], ACT.Identity,
                                 bias=bo[:, 2 * j + n:2 * j + n + 1])
                    last.then_inc(lin_free, 1)
                for j in range(4):
                    bank = unit1(l, UN_OUT + j)
                    for n in range(2):
                        m = 2 * KC + 2 * j + n
                        last = A(TMP1[:, 2 * j + n], bank[:, n * T:(n + 1) * T], ACT.Identity,
                                 scale=mod[:, m:m + 1])
                    last.then_inc(lin_free, 1)
                root(l * 3 + 3, VAR, RSTD)
                A(RT[:, 0:TH * NR], unit1(l, UN_ROUT)[:, 0:TH * NR], ACT.Copy).then_inc(lin_free, 1)
                rings, number = l * (TILES1 // SLOTS), l * HALVES1
                high_part(rings, 0, J_MOE, number)
                high_part(rings, 1, J_MOE, number)
                act.wait_ge(rl_ready, l * 2 + 1)
                A(RT[:, 100:108], RT[:, 100:108], ACT.Exp).then_inc(re_ready, 1)
                act.wait_ge(rl_ready, l * 2 + 2)
                A(RT[:, 200:216], RT[:, 200:216], ACT.Exp).then_inc(re_ready, 1)

                def expert_silu(e, halves):
                    halves_done(halves)
                    act.wait_ge(eact_ready, l * NE + e + 1)
                    A(SGM, G_PS[:, :].rearrange("p (c t) -> p c t", c=2), ACT.Silu).then_inc(silu_done, 1)

                high_part(rings, 2, J_MOE, number)
                high_part(rings, 3, J_MOE, number)
                expert_silu(0, number + 2)
                high_part(rings, 4, J_MOE, number)
                with act.Fori(0, NE - 1) as i:
                    high_part(rings + i, 5, J_MOE, number + i * 6)
                    high_part(rings + i, 6, J_MOE, number + i * 6)
                    high_part(rings + i, 7, J_MOE, number + i * 6)
                    expert_silu(i + 1, number + i * 6 + 6)
                    high_part(rings + i, 8, J_MOE, number + i * 6)
                    high_part(rings + i, 9, J_MOE, number + i * 6)
                    high_part(rings + i, 10, J_MOE, number + i * 6)
                high_part(rings, HALVES1 - 1, J_MOE, number)
                act.wait_ge(moe_done, l + 1)
                for n in range(KC):
                    last = A(TMP1[:, n], accT[:, n, :], ACT.Identity, scale=mod[:, 5 * KC + n:5 * KC + n + 1])
                last.then_inc(moe_out, 1)

            root(L * 3 + 1, VAR, RSTD)

            with act.Fori(0, L) as l:
                units = l * UNITS2 + BASE2
                act.wait_ge(lam_in, l + 1)
                A(lamb[:, 2:4], lamb[:, 0:2], ACT.Exp).then_inc(lam_exp, 1)
                for j in range(IN2_T):
                    bank = unit2(l, j)[:, :].rearrange("p (c t) -> p c t", c=2)
                    which, half = divmod(j, 2)
                    if which in (2, 5):
                        dst = (DV if which == 2 else SV)[:, :, half * T:(half + 1) * T]
                    else:
                        dst = {0: DQ, 1: DK, 3: SQT, 4: SKT}[which][:, 2 * half:2 * half + 2]
                    A(dst, bank, ACT.Copy).then_inc(lin_free, 1)

                def soft(d):
                    b = d // DH
                    act.wait_ge(smax_ready, l * 8 + d + 1)
                    for m in range(2):
                        last = A(EXO[d % 2][:, m, 0:(b + 1) * P], SCO[d % 2][:, m, 0:(b + 1) * P], ACT.Exp,
                                 bias=rsm[:, 4 * (d % 2) + m:4 * (d % 2) + m + 1],
                                 accum_out=rsm[:, 4 * (d % 2) + 2 + m:4 * (d % 2) + 3 + m])
                    last.then_inc(e_ready, 1)

                def move(d):
                    b, h = divmod(d, DH)
                    act.wait_ge(tr_done, l * 8 + d + 1)
                    A(ATT_T[:, h, 0:b + 1, b * P:(b + 1) * P],
                      lin[d % 2][:, 0:(b + 1) * P].rearrange("p (k q) -> p k q", k=b + 1),
                      ACT.Copy).then_inc(tr_out, 1)

                soft(0)
                for d in range(8):
                    if d + 1 < 8:
                        soft(d + 1)
                    move(d)
                act.wait_ge(dpv_done, l + 1)
                A(DIFF, accT[:, 0:4, :], ACT.Copy).then_inc(dpv_out, 1)
                act.wait_ge(dvar_ready, l + 1)
                A(DRS, DRS, ACT.Sqrt).then_inc(dstd_ready, 1)
                for w4 in range(2):
                    v = l * 2 + w4 + 1
                    act.wait_ge(na_ready, v)
                    A(NA, NA, ACT.Exp)
                    act.drain()
                    A(L1, NA, ACT.Ln, bias=1.0).then_inc(l1_ready, 1)
                    act.wait_ge(wl_ready, v)
                    A(NA, ZS, ACT.Exp).then_inc(we_ready, 1)
                    act.wait_ge(spv_done, v)
                    A(MIXT[:, 4 + 2 * w4:6 + 2 * w4], stat[:, :].rearrange("p (c t) -> p c t", c=2),
                      ACT.Copy).then_inc(spv_out, 1)
                for j in range(WO_T):
                    A(TMP2[:, 2 * j:2 * j + 2], unit2(l, UN_WO + j)[:, :].rearrange("p (c t) -> p c t", c=2),
                      ACT.Copy).then_inc(lin_free, 1)
                root(L * 3 + 1 + l * 2 + 1, VAR2, RSTD2)
                for j in range(WQ_T):
                    A(QT[:, 2 * j:2 * j + 2], unit2(l, UN_WQ + j)[:, :].rearrange("p (c t) -> p c t", c=2),
                      ACT.Copy).then_inc(lin_free, 1)
                for s in range(8):
                    th, q = divmod(s, 4)
                    A(SC[th][:, 4 * q:4 * q + 4, :],
                      unit2(l, UN_SC + s)[:, :].rearrange("p (a n) -> p a n", a=4),
                      ACT.Copy).then_inc(lin_free, 1)

                rings = l * (TILES2 // SLOTS) + L * TILES1 // SLOTS
                number = l * HALVES2 + L * HALVES1

                def gelu(j, i):
                    halves_done(number + i * 6 + (2 * j + 2))
                    A(arena[:, bass.ds(i * 6 + 2 * j, 2), :],
                      lin[(UN_U + j) % LB][:, :].rearrange("p (c t) -> p c t", c=2), ACT.Gelu).then_inc(lin_free, 1)

                def u_steps(i):
                    for s in range(SLOTS):
                        high_part(rings + i, 2 * s + 1, J_U, number + i * 6)
                        high_part(rings + i, 2 * s + 2, J_U, number + i * 6)
                        gelu(s, i)

                high_part(rings, 0, J_U, number)
                with act.Fori(0, HEAD - 1) as i:
                    u_steps(i)
                act.wait_ge(bl_ready, l + 1)
                A(BE, BE, ACT.Exp).then_inc(be_ready, 1)
                with act.Fori(HEAD - 1, HEAD) as i:
                    u_steps(i)
                act.wait_ge(ptr_done, l + 1)
                A(picksT[:, 0:2, :], acc[:, 2, :].rearrange("p (q t) -> p q t", q=2), ACT.Copy)
                A(picksT[:, 2, :], acc[:, 3, 0:T], ACT.Copy).then_inc(ptr_out, 1)
                with act.Fori(HEAD, U_T // SLOTS) as i:
                    u_steps(i)
                high_part(rings, 2 * U_T - 1, J_U, number)
                gelu(U_T - 1, 0)

                def scale_group(g, i):
                    n = l * G4 + i * 6 + g
                    act.wait_ge(hot_ready, n + 1)
                    act.wait_ge(g_done, n + 1)
                    for t in range(4):
                        last = A(gated_hot[:, g % 2, t, :], hot[:, g % HOTS, 0, t, :], ACT.Identity,
                                 scale=picksT[:, 2, bass.ds(i * 24 + (4 * g + t), 1)])
                    last.then_inc(scaled_hot, 1)

                with act.Fori(0, G4 // 6) as i:
                    for g in range(6):
                        scale_group(g, i)
                for g in range(G4 // 6 * 6, G4):
                    scale_group(g, 0)
                act.wait_ge(gated, l + 1)
                with act.Fori(0, U_T // SLOTS) as i:
                    for c in range(2 * SLOTS):
                        high_part(rings + i, c, J_V, number + i * 6 + C_V, i * 6 + c)
                for c in range(U_T // SLOTS * 6, 2 * U_T):
                    high_part(rings, c, J_V, number + C_V, c)
                act.wait_ge(v_done, l + 1)
                A(TMP2, accT, ACT.Copy).then_inc(v_out, 1)
                root(L * 3 + 1 + l * 2 + 2, VAR2, RSTD2)
            act.wait_ge(final_ready, 1)
            act.dma_start(out[:, :, :], xT[:, :, :]).then_inc(stored, 16)
            act.wait_ge(stored, 16)

        @block.vector
        def _(dve):
            V = nc.vector
            TT, TS, STT = V.tensor_tensor, V.tensor_scalar, V.scalar_tensor_tensor

            def over(ap, n):
                return ap.to_broadcast([P, n, T])

            def rstd(sum_value, root_value, src_bank, n, eps, var, dst):
                dve.wait_ge(stat_out, sum_value)
                TS(var[:, 0, :], src_bank, 1.0 / n, eps, ALU.mult, ALU.add).then_inc(var_ready, 1)
                dve.wait_ge(std_ready, root_value)
                V.reciprocal(dst[:, 0, :], dst[:, 0, :])
                dve.drain()

            def squares(src, dst):
                TT(dst, src, src, ALU.mult).then_inc(stat_in, 1)

            def modulated(dst, gains, shifts):
                TT(dst, xT[:, :, :], over(RSTD, KC), ALU.mult)
                dve.drain()
                for k in range(KC):
                    if shifts is None:
                        TS(xT[:, k, :], dst[:, k, :], gains[:, k:k + 1], None, ALU.mult)
                    else:
                        TS(dst[:, k, :], dst[:, k, :], gains[:, k:k + 1], shifts[:, k:k + 1], ALU.mult, ALU.add)

            def low_part(c, j, number, arena_col=None):
                dve.wait_ge(hi_ready, number + c + 1)
                if arena_col is not None:
                    TT(act_lo[c % 2].unsqueeze(1), arena[:, bass.ds(arena_col, 1), :], act_hi[c % 2].bitcast(F32).unsqueeze(1),
                       ALU.subtract)
                TT(w_lo[c % 2][:, :], slot[j % SLOTS][:, (c % 2) * HALF:(c % 2 + 1) * HALF], w_hi[c % 2][:, :].bitcast(F32),
                   ALU.subtract).then_inc(slot_free[j % SLOTS] if c % 2 else split_ready, 1)

            dve.sem_inc(eact_ready, 1)
            dve.sem_inc(ada_free, ADA_BUFS)
            V.memset(zeros[:, :], 0.0).then_inc(zeros_made, 1)
            dve.wait_ge(small_loaded, 16)
            dve.wait_ge(x_loaded, 16)
            dve.wait_ge(inv_loaded, 16)
            dve.wait_ge(consts_made, 1)

            dve.wait_ge(c_ready, 1)
            with dve.Fori(0, ADA_GROUPS // 6) as i:
                for g in range(6):
                    dst = ADA_SUM[g % 2]
                    dve.wait_ge(ada_loaded[g % ADA_BUFS], (i * 2 + g // ADA_BUFS + 1) * (16 * ADA_G))
                    dve.wait_ge(sums_used, i * 6 + g + 1)
                    src = ADA_IN[g % ADA_BUFS]
                    TS(dst, src[:, :, 0, :], c_act[:, 0:1], None, ALU.mult)
                    dve.drain()
                    for k in range(1, KC):
                        STT(dst, src[:, :, k, :], c_act[:, k:k + 1], dst, ALU.mult, ALU.add)
                        if k < KC - 1:
                            dve.drain()
                    dve.drain().then_inc(part_sums, 1)
                    dve.sem_inc(ada_free, 1)
            dve.wait_ge(sums_used, ADA_GROUPS + 2)
            V.tensor_copy(mods[:, :], acc[:, 0, 0:L * 6 * KC])
            dve.drain().then_inc(layer_end1, 1)

            with dve.Fori(0, L) as l:
                units = l * UNITS1

                def moved(u):
                    dve.wait_ge(lin_free, units + u + 1 + LB)

                squares(xT[:, :, :], SQ)
                rstd(l * 4 + 1, l * 3 + 1, stat[:, 0:T], D, EPS1, VAR, RSTD)
                dve.wait_ge(par1_loaded, l * 16 + 16)
                TT(mod[:, :], mods[:, bass.ds(l * (6 * KC), 6 * KC)], par(par1, COL1, "b_ada"), ALU.add)
                dve.drain()
                for q, name in ((0, "norm_g"), (1, "ffn_g")):
                    s = (3 * q + 1) * KC
                    STT(gain[:, q * KC:(q + 1) * KC], mod[:, s:s + KC], 1.0, par(par1, COL1, name), ALU.add, ALU.mult)
                dve.drain()
                modulated(H, gain[:, 0:KC], mod[:, 0:KC])
                dve.drain().then_inc(h_ready, 1)
                dve.wait_ge(pads_made, l + 1)
                moved(3)
                TT(VPAD[:, :, CK - 1:], UA, SG, ALU.mult)
                moved(5)
                V.tensor_copy(PPAD[0][:, :, 16:], UP)
                dve.drain()
                for s in range(4):
                    a, w = PPAD[s % 2 * 2], 1 << s
                    src = PPAD[s]
                    c = slice(s, CC)
                    dst = PPAD[s + 1][:, c, 16:] if s < 3 else PLD[:, c, :]
                    TT(dst, src[:, c, 16:], src[:, c, 16 - w:16 + T - w], ALU.add)
                    dve.drain()
                for s in range(3):
                    TT(PLD[:, s, :], PPAD[s + 1][:, s, 16:], INVC[:, s, :], ALU.mult)
                TT(PLD[:, 3, :], PLD[:, 3, :], INVC[:, 3, :], ALU.mult)
                dve.drain()
                TT(PLD, PLD, UP, ALU.subtract).then_inc(pooled_ready, 1)
                cw = par(par1, COL1, "conv_w").rearrange("p (c k) -> p c k", c=CC)
                cb = par(par1, COL1, "conv_b")
                for c in range(CC):
                    TS(CV[:, c, :], VPAD[:, c, 0:T], cw[:, c, 0:1], cb[:, c:c + 1], ALU.mult, ALU.add)
                dve.drain()
                with dve.Fori(1, CK) as k:
                    for c in range(CC):
                        STT(CV[:, c, :], VPAD[:, c, bass.ds(k, T)], cw[:, c, bass.ds(k, 1)], CV[:, c, :],
                            ALU.mult, ALU.add)
                    dve.drain()
                dve.drain().then_inc(stat_in, 1)
                dve.wait_ge(stat_out, l * 4 + 2)
                TS(MEAN[:, 0, :], stat[:, 0:T], 1.0 / DCONV, None, ALU.mult)
                dve.drain()
                TT(CVN, CV, over(MEAN, CC), ALU.subtract)
                dve.drain()
                squares(CVN, SQ[:, 0:CC, :])
                rstd(l * 4 + 3, l * 3 + 2, stat[:, 0:T], DCONV, EPS1, VAR, RSTD)
                TT(CVN, CVN, over(RSTD, CC), ALU.mult).then_inc(cvn_ready, 1)
                for u in range(4):
                    c = slice(2 * u, 2 * u + 2)
                    if u == 0:
                        moved(UN_POOL + 3)
                    TT(YB[:, c], YB[:, c], GB[:, c], ALU.mult)
                    moved(UN_CONV + u)
                    TT(YA[:, c], YA[:, c], GA[:, c], ALU.mult)
                    dve.drain()
                    TT(MIX[:, c], YA[:, c], YB[:, c], ALU.add)
                dve.drain().then_inc(mixed_ready, 1)
                for u in range(4):
                    moved(UN_OUT + u)
                    c = slice(2 * u, 2 * u + 2)
                    TT(xT[:, c, :], xT[:, c, :], TMP1[:, c], ALU.add)
                dve.drain()
                squares(xT[:, :, :], SQ)
                rstd(l * 4 + 4, l * 3 + 3, stat[:, 0:T], D, EPS1, VAR, RSTD)
                modulated(H, gain[:, KC:2 * KC], mod[:, 3 * KC:4 * KC])
                dve.drain().then_inc(h2_ready, 1)
                V.tensor_copy(x_hi, H)
                dve.drain()
                TT(x_lo, H, x_hi.bitcast(F32), ALU.subtract).then_inc(h2_split, 1)
                number = l * HALVES1
                low_part(0, J_MOE, number)
                low_part(1, J_MOE, number)

                def r(a, *shape):
                    n = int(np.prod(shape))
                    v = RT[:, a:a + n]
                    if len(shape) == 2:
                        return v.rearrange("p (h n) -> p h n", h=shape[0])
                    if len(shape) == 3:
                        return v.rearrange("p (h g n) -> p h g n", h=shape[0], g=shape[1])
                    return v

                lg = r(0, TH, NR)
                eg, e8 = r(100, TH, NG), r(200, TH, EPG)
                gp8, g8, e8t = r(120, TH, 8), r(140, TH, 8), r(160, TH, 8)
                gi, ei = r(220, TH * 8).bitcast(U32), r(240, TH * 8).bitcast(U32)
                gmax, gsum = r(260, TH), r(264, TH)
                emax, esum, den = r(268, TH), r(272, TH), r(276, TH)
                gif, eif = r(280, TH, 8), r(300, TH, 8)
                og, sel8 = r(320, TH, NG), r(340, TH, EPG)
                prod = r(400, TH, NG, EPG)
                o1, o2, comb = r(500, TH, EPG), r(520, TH, EPG), r(540, TH, EPG)

                def wide(ap, n):
                    return ap.unsqueeze(2).to_broadcast([P, TH, n])

                moved(UN_ROUT)
                TT(lg, lg, par(par1, COL1, "router_b").unsqueeze(1).to_broadcast([P, TH, NR]), ALU.add)
                V.memset(gp8, -1.0)
                dve.drain()
                V.tensor_reduce(gmax, lg[:, :, 0:NG], AX.X, ALU.max)
                dve.drain()
                TT(eg, lg[:, :, 0:NG], wide(gmax, NG), ALU.subtract).then_inc(rl_ready, 1)
                dve.wait_ge(re_ready, l * 2 + 1)
                V.tensor_reduce(gsum, eg, AX.X, ALU.add)
                dve.drain()
                V.reciprocal(gsum, gsum)
                dve.drain()
                TT(gp8[:, :, 0:NG], eg, wide(gsum, NG), ALU.mult)
                dve.drain()
                for th in range(TH):
                    V.max(g8[:, th, :], gp8[:, th, :])
                dve.drain()
                for th in range(TH):
                    V.max_index(gi[:, th * 8:th * 8 + 8], g8[:, th, :], gp8[:, th, :])
                dve.drain()
                V.tensor_copy(gif, gi.rearrange("p (h n) -> p h n", h=TH))
                dve.drain()
                iot = iota[:, 0:8].unsqueeze(1).to_broadcast([P, TH, 8])
                TT(og, iot[:, :, 0:NG], gif[:, :, 0:1].to_broadcast([P, TH, NG]), ALU.is_equal)
                dve.drain()
                lge = lg[:, :, NG:NR].rearrange("p h (g n) -> p h g n", g=NG)
                TT(prod, lge, og.unsqueeze(3).to_broadcast([P, TH, NG, EPG]), ALU.mult)
                dve.drain()
                V.tensor_reduce(sel8, prod.rearrange("p h g n -> p h n g"), AX.X, ALU.add)
                dve.drain()
                V.tensor_reduce(emax, sel8, AX.X, ALU.max)
                dve.drain()
                TT(e8, sel8, wide(emax, EPG), ALU.subtract).then_inc(rl_ready, 1)
                dve.wait_ge(re_ready, l * 2 + 2)
                V.tensor_reduce(esum, e8, AX.X, ALU.add)
                dve.drain()
                V.reciprocal(esum, esum)
                dve.drain()
                TT(e8, e8, wide(esum, EPG), ALU.mult)
                dve.drain()
                for th in range(TH):
                    V.max(e8t[:, th, :], e8[:, th, :])
                dve.drain()
                for th in range(TH):
                    V.max_index(ei[:, th * 8:th * 8 + 8], e8t[:, th, :], e8[:, th, :])
                TT(den, e8t[:, :, 0], e8t[:, :, 1], ALU.add)
                dve.drain()
                V.tensor_copy(eif, ei.rearrange("p (h n) -> p h n", h=TH))
                V.reciprocal(den, den)
                dve.drain()
                TT(o1, iot, eif[:, :, 0:1].to_broadcast([P, TH, 8]), ALU.is_equal)
                TT(o2, iot, eif[:, :, 1:2].to_broadcast([P, TH, 8]), ALU.is_equal)
                TT(den, den, g8[:, :, 0], ALU.mult)
                dve.drain()
                TT(o1, o1, o2, ALU.add)
                TT(comb, e8, wide(den, EPG), ALU.mult)
                dve.drain()
                TT(comb, comb, o1, ALU.mult)
                dve.drain()
                cm = CMB.rearrange("p h (g n) -> p h g n", g=NG)
                for th in range(TH):
                    TT(cm[:, th], og[:, th].unsqueeze(2).to_broadcast([P, NG, EPG]),
                       comb[:, th].unsqueeze(1).to_broadcast([P, NG, EPG]), ALU.mult)
                dve.drain()
                def diagonal(e):
                    for th in range(TH):
                        last = TS(DIAG[:, th, :], ident[:, :], CMB[:, th, bass.ds(e, 1)], None, ALU.mult)
                    last.then_inc(diag_ready, 1)

                def expert_act(e):
                    dve.wait_ge(silu_done, l * NE + e + 2)
                    dve.wait_ge(up_done, l * NE + e + 1)
                    TT(GU, SGM, U_PS[:, :].rearrange("p (c t) -> p c t", c=2), ALU.mult)
                    dve.drain()
                    TT(GU, GU, C_PS[:, 0:T].unsqueeze(1).to_broadcast([P, 2, T]), ALU.mult)
                    dve.drain()
                    V.tensor_copy(eact[:, 0], GU)
                    dve.drain()
                    TT(eact[:, 1], GU, eact[:, 0].bitcast(F32), ALU.subtract).then_inc(eact_ready, 1)

                low_part(2, J_MOE + 1, number)
                low_part(3, J_MOE + 1, number)
                diagonal(0)
                low_part(4, J_MOE + 2, number)
                with dve.Fori(0, NE - 1) as i:
                    low_part(5, J_MOE + 2, number + i * 6)
                    expert_act(i)
                    low_part(6, J_MOE + 3, number + i * 6)
                    low_part(7, J_MOE + 3, number + i * 6)
                    diagonal(i + 1)
                    low_part(8, J_MOE + 4, number + i * 6)
                    low_part(9, J_MOE + 4, number + i * 6)
                    low_part(10, J_MOE + 5, number + i * 6)
                low_part(HALVES1 - 1, J_MOE + HALVES1 // 2 - 1, number)
                expert_act(NE - 1)
                dve.wait_ge(moe_out, l + 1)
                TT(xT[:, :, :], xT[:, :, :], TMP1, ALU.add)
                dve.drain().then_inc(layer_end1, 1)

            squares(xT[:, :, :], SQ)
            rstd(L * 4 + 1, L * 3 + 1, stat[:, 0:T], D, EPS1, VAR, RSTD)
            modulated(H, par(cst, COLC, "final_g"), None)
            dve.drain().then_inc(layer_end2, 1)
            dve.drain().then_inc(x2_ready, 1)

            def layer_norm(stat_value, root_value, tmp, g, b):
                STT(YC, xT[:, :, :], ALPHA, tmp, ALU.mult, ALU.add).then_inc(stat_in, 1)
                dve.wait_ge(stat_out, stat_value)
                TS(MEAN2[:, 0, :], stat[:, 0:T], 1.0 / D, None, ALU.mult)
                dve.drain()
                TT(YC, YC, over(MEAN2, KC), ALU.subtract)
                dve.drain()
                squares(YC, SQ2)
                rstd(stat_value + 1, root_value, stat[:, 0:T], D, EPS2, VAR2, RSTD2)
                TT(YC, YC, over(RSTD2, KC), ALU.mult)
                dve.drain()
                for k in range(KC):
                    TS(xT[:, k, :], YC[:, k, :], g[:, k:k + 1], b[:, k:k + 1], ALU.mult, ALU.add)
                dve.drain()

            with dve.Fori(0, L) as l:
                units = l * UNITS2 + BASE2
                stat0 = l * 4 + (L * 4 + 1)
                root0 = l * 2 + (L * 3 + 1)

                def moved2(u):
                    dve.wait_ge(lin_free, units + u + 1 + LB)

                dve.wait_ge(par2_loaded, l * 16 + 16)
                lq = par(par2, COL2, "lam_q")
                TT(rsm_wide(arena), lq, par(par2, COL2, "lam_k"), ALU.mult)
                dve.drain()
                V.tensor_reduce(lamb[:, 0:2], rsm_wide(arena).rearrange("p (q n) -> p q n", q=2), AX.X, ALU.add)\
                    .then_inc(lam_in, 1)
                dve.wait_ge(lam_exp, l + 1)
                TT(lamb[:, 4:5], lamb[:, 3:4], lamb[:, 2:3], ALU.subtract)
                dve.drain()
                TT(lamb[:, 5:6], lamb[:, 4:5], par(par2, COL2, "lambda_init"), ALU.subtract)
                dve.drain()
                dve.wait_ge(alibi_made, l + 1)

                def shifted(d):
                    b, h = divmod(d, DH)
                    kv = (b + 1) * P
                    s = SCO[d % 2]
                    dve.wait_ge(sc_done, l * 8 + d + 1)
                    STT(s[:, :, 0:kv], acc[:, 2 * (d % 2):2 * (d % 2) + 2, 0:kv], HD ** -0.5,
                        ALIBI[:, h, b, 0:kv].unsqueeze(1).to_broadcast([P, 2, kv]), ALU.mult, ALU.add)
                    dve.drain()
                    a = 4 * (d % 2)
                    V.tensor_reduce(rsm[:, a:a + 2], s[:, :, 0:kv], AX.X, ALU.max)
                    dve.drain()
                    TS(rsm[:, a:a + 2], rsm[:, a:a + 2], -1.0, None, ALU.mult).then_inc(smax_ready, 1)

                def combined(d):
                    b, h = divmod(d, DH)
                    kv = (b + 1) * P
                    a = 4 * (d % 2)
                    dve.wait_ge(e_ready, l * 8 + d + 1)
                    V.reciprocal(rsm[:, a + 2:a + 4], rsm[:, a + 2:a + 4])
                    dve.drain()
                    TT(rsm[:, a + 3:a + 4], rsm[:, a + 3:a + 4], lamb[:, 5:6], ALU.mult)
                    TS(EXO[d % 2][:, 0, 0:kv], EXO[d % 2][:, 0, 0:kv], rsm[:, a + 2:a + 3], None, ALU.mult)
                    dve.drain()
                    if d >= 2:
                        dve.wait_ge(tr_done, l * 8 + d - 1)
                    STT(ATT[d % 2][:, 0, 0:kv], EXO[d % 2][:, 1, 0:kv], rsm[:, a + 3:a + 4],
                        EXO[d % 2][:, 0, 0:kv], ALU.mult, ALU.add).then_inc(att_ready, 1)

                shifted(0)
                for d in range(8):
                    if d + 1 < 8:
                        shifted(d + 1)
                    combined(d)
                dve.wait_ge(dpv_out, l + 1)
                TT(DSQ, DIFF, DIFF, ALU.mult).then_inc(dsq_ready, 1)
                dve.wait_ge(dss_done, l + 1)
                TS(DRS, accT[:, 4:8, :], 1.0 / (2 * HD), EPS2, ALU.mult, ALU.add).then_inc(dvar_ready, 1)
                dve.wait_ge(dstd_ready, l + 1)
                V.reciprocal(DRS, DRS)
                dve.drain()
                TT(DIFF, DIFF, DRS, ALU.mult)
                dve.drain()
                TS(MIXT[:, 0:4], DIFF, par(par2, COL2, "subln_g"), par(par2, COL2, "keep"), ALU.mult, ALU.mult)\
                    .then_inc(mixt_ready, 1)
                mask4 = MASK.unsqueeze(1).to_broadcast([P, 4, SW])
                for w4 in range(2):
                    v = l * 2 + w4 + 1
                    dve.wait_ge(z_done, v)
                    TS(ZS, acc[:, :, 0:SW], HD ** -0.5, None, ALU.mult)
                    dve.drain()
                    STT(NA, ZS, -1.0, ZS, ALU.mult, ALU.min).then_inc(na_ready, 1)
                    dve.wait_ge(l1_ready, v)
                    STT(WW, ZS, 0.0, L1, ALU.min, ALU.subtract)
                    dve.drain()
                    TT(LF, WW, ZS, ALU.subtract)
                    dve.drain()
                    TT(LF, LF, mask4, ALU.mult).then_inc(lf_ready, 1)
                    dve.wait_ge(lat_done, v)
                    TT(ZS, WW, acc[:, :, 0:SW], ALU.add).then_inc(wl_ready, 1)
                    dve.wait_ge(we_ready, v)
                    TT(WW, NA, mask4, ALU.mult).then_inc(ww_ready, 1)
                moved2(UN_WO + 3)
                layer_norm(stat0 + 1, root0 + 1, TMP2, par(par2, COL2, "ln1_g"), par(par2, COL2, "ln1_b"))
                dve.drain().then_inc(x3_ready, 1)
                V.tensor_copy(x_hi, xT[:, :, :])
                dve.drain()
                TT(x_lo, xT[:, :, :], x_hi.bitcast(F32), ALU.subtract).then_inc(x3_split, 1)
                number = l * HALVES2 + L * HALVES1

                def top16(vals, work, n, topv, topi):
                    for s in range(n):
                        V.max(topv[:, s, 0:8], vals[:, s, :])
                        if s % 8 == 7:
                            yield
                    dve.drain()
                    for s in range(n):
                        V.max_index(topi[:, s, 0:8], topv[:, s, 0:8], vals[:, s, :])
                        V.match_replace(work[:, s, :], topv[:, s, 0:8], vals[:, s, :], -3.0e38)
                        if s % 4 == 3:
                            yield
                    dve.drain()
                    for s in range(n):
                        V.max(topv[:, s, 8:16], work[:, s, :])
                        if s % 8 == 7:
                            yield
                    dve.drain()
                    for s in range(n):
                        V.max_index(topi[:, s, 8:16], topv[:, s, 8:16], work[:, s, :])
                        if s % 8 == 7:
                            yield
                    dve.drain()

                def routing():
                    for th in range(TH):
                        yield from top16(SC[th], WORK, HP, TOPV, TOPI)
                        V.tensor_copy(TOPF.rearrange("p h q j -> p (h q) j"), TOPI)
                        tv = TOPV.rearrange("p (h q) j -> p h q j", q=2)
                        for h in range(PH):
                            TT(CAND[:, h, :].rearrange("p (a b) -> p a b", a=16),
                               tv[:, h, 0, :].unsqueeze(2).to_broadcast([P, 16, 16]),
                               tv[:, h, 1, :].unsqueeze(1).to_broadcast([P, 16, 16]), ALU.add)
                            if h % 4 == 3:
                                yield
                        dve.drain()
                        yield from top16(CAND, CWORK, PH, BV, BPH)
                        TT(BE[:, th], BV, BV[:, :, 0:1].to_broadcast([P, PH, PTOP]), ALU.subtract)
                        TS(BA, BP, 4, None, ALU.logical_shift_right)
                        TS(BB, BP, 15, None, ALU.bitwise_and)
                        dve.drain()
                        V.tensor_copy(BF[:, 0, :], BA)
                        V.tensor_copy(BF[:, 1, :], BB)
                        dve.drain()
                        yield
                        for q in range(2):
                            for h in range(PH):
                                TT(EQH[:, h], iota[:, 0:16].unsqueeze(1).to_broadcast([P, 16, 16]),
                                   BF[:, q, 16 * h:16 * h + 16].unsqueeze(2).to_broadcast([P, 16, 16]), ALU.is_equal)
                                if h % 4 == 3:
                                    yield
                            dve.drain()
                            for h in range(PH):
                                TT(EQH[:, h], EQH[:, h], TOPF[:, h, q, :].unsqueeze(1).to_broadcast([P, 16, 16]),
                                   ALU.mult)
                                if h % 4 == 3:
                                    yield
                            dve.drain()
                            for a in range(2):
                                r_ = slice(a * NSEL // 2, (a + 1) * NSEL // 2)
                                V.tensor_reduce(picks[:, q, th, r_], EQS[:, r_, :], AX.X, ALU.add)
                                yield
                            dve.drain()

                moved2(UN_SC + 7)
                V.memset(BS, 0.0)
                work = routing()
                HEAD_C = HEAD * 6 - 1
                for c in range(HEAD_C):
                    low_part(c, J_U + c // 2, number)
                    next(work, None)
                    if c == HEAD_C - 12:
                        for _ in work:
                            pass
                        dve.drain().then_inc(bl_ready, 1)
                dve.wait_ge(be_ready, l + 1)
                V.tensor_reduce(BS, BE, AX.X, ALU.add)
                dve.drain()
                V.reciprocal(BS, BS)
                dve.drain()
                for th in range(TH):
                    TT(picks[:, 2, th, :].rearrange("p (h j) -> p h j", h=PH), BE[:, th],
                       BS[:, th].unsqueeze(2).to_broadcast([P, PH, PTOP]), ALU.mult)
                dve.drain().then_inc(routed, 1)
                low_part(HEAD_C, J_U + HEAD_C // 2, number)
                with dve.Fori(HEAD, U_T // SLOTS) as i:
                    for c in range(2 * SLOTS):
                        low_part(c, J_U + c // 2, number + i * 6)
                for c in range(U_T // SLOTS * 6, 2 * U_T):
                    low_part(c, J_U + c // 2, number)

                def hot_rows(g, i):
                    at = bass.ds(i * 24 + 4 * g, 4)
                    TT(hot[:, g % HOTS], iota[:, :].unsqueeze(1).unsqueeze(1).to_broadcast([P, 2, 4, P]),
                       picksT[:, 0:2, at].unsqueeze(3).to_broadcast([P, 2, 4, P]), ALU.is_equal)\
                        .then_inc(hot_ready, 1)

                def apply_gates(g, i):
                    dve.wait_ge(g_done, l * G4 + i * 6 + g + 3)
                    a = arena[:, :, bass.ds(i * 24 + 4 * g, 4)]
                    TT(a, a, acc[:, g % HOTS, :].rearrange("p (t n) -> p n t", t=4), ALU.mult)

                dve.wait_ge(ptr_out, l + 1)
                dve.wait_ge(lin_free, units + UNITS2 + LB)
                V.memset(lamb[:, 8:9], 0.0)
                for g in range(HOTS):
                    hot_rows(g, 0)
                with dve.Fori(0, G4 // 6) as i:
                    for g in range(6):
                        apply_gates(g, i)
                        hot_rows(g + HOTS, i)
                for g in range(G4 // 6 * 6, G4):
                    apply_gates(g, 0)
                    if g + HOTS < G4:
                        hot_rows(g + HOTS, 0)
                dve.drain().then_inc(gated, 1)
                with dve.Fori(0, U_T // SLOTS) as i:
                    for c in range(2 * SLOTS):
                        low_part(c, J_V + c // 2, number + i * 6 + C_V, i * 6 + c)
                for c in range(U_T // SLOTS * 6, 2 * U_T):
                    low_part(c, J_V + c // 2, number + C_V, c)
                dve.wait_ge(v_out, l + 1)
                layer_norm(stat0 + 3, root0 + 2, TMP2, par(par2, COL2, "ln2_g"), par(par2, COL2, "ln2_b"))
                dve.drain().then_inc(layer_end2, 1)
                dve.drain().then_inc(x2_ready, 1)
            dve.drain().then_inc(final_ready, 1)


def rsm_wide(arena):
    return arena[:, 127, 0:2 * HD]


def kernel(**inputs):
    import concourse.bacc as _bacc
    from concourse.bass_utils import run_bass_kernel_spmd as _run

    f = {k: np.asarray(v) for k, v in inputs.items()}
    f32 = np.float32

    def cols(v):
        return v.reshape(-1, P).T

    def rows(v):
        return np.broadcast_to(v.reshape(1, -1), (P, v.size))

    def k_tiles(w, order=None):
        n = w.shape[1] // 256
        t = w.reshape(-1, P, n, 256).transpose(2, 1, 0, 3).reshape(n, P, -1)
        return t if order is None else t[order]

    stream = np.zeros((TILES, P, TILE), f32)
    at = 0

    def put(t):
        nonlocal at
        stream[at:at + t.shape[0], :, 0:t.shape[2]] = t
        at += t.shape[0]

    def halved(t):
        return t.reshape(-1, P, KC, 2, P).transpose(0, 1, 3, 2, 4).reshape(-1, P, TILE)

    for l in range(L):
        put(k_tiles(f["w_in"][l], [0, 2, 1, 3] + list(range(4, 14))))
        put(f["pool_w"][l].transpose(1, 0, 2).reshape(1, P, -1))
        put(f["w_conv_out"][l].reshape(CC, P, 2, 512).transpose(2, 1, 0, 3).reshape(2, P, -1))
        put(k_tiles(f["w_out"][l]))
        wg, wu, wd = f["w_expert_gate"][l], f["w_expert_up"][l], f["w_expert_down"][l]
        down = wd.reshape(NE, 2, P, 2, 512).transpose(0, 2, 3, 1, 4).reshape(NE, P, -1)
        put(halved(k_tiles(wg[0])))
        put(halved(k_tiles(wu[0])))
        for e in range(NE - 1):
            put(halved(k_tiles(wg[e + 1])))
            put(down[e:e + 1])
            put(halved(k_tiles(wu[e + 1])))
        put(down[NE - 1:NE])
    for l in range(L):
        put(k_tiles(f["w_in_2"][l]))
        put(k_tiles(f["w_o_2"][l]))
        put(k_tiles(f["w_query_2"][l]))
        put(f["sub_keys_2"][l].transpose(3, 0, 1, 2).reshape(1, P, -1))
        u = f["expert_u_2"][l].reshape(P, U_T, 2, KC, P)
        put(u.transpose(1, 4, 2, 3, 0).reshape(U_T, P, -1))
        v = f["expert_v_2"][l].reshape(P, U_T, 2 * D)
        put(v.transpose(1, 0, 2))
    assert at == TILES

    par1 = np.stack([np.concatenate([
        cols(f["mixer_norm_g"][l]), cols(f["b_ada"][l]),
        f["conv_w"][l].T.reshape(CC, P, CK).transpose(1, 0, 2).reshape(P, -1), cols(f["conv_b"][l]),
        cols(f["conv_ln_g"][l]), cols(f["conv_ln_b"][l]), cols(f["b_conv_out"][l]), cols(f["pool_scale"][l]),
        cols(f["ffn_norm_g"][l]),
        np.concatenate([f["w_router_group"][l], f["w_router_expert"][l]], axis=1)
        .reshape(KC, P, NR).transpose(1, 0, 2).reshape(P, -1),
        rows(np.concatenate([f["b_router_group"][l], f["b_router_expert"][l]]))], axis=1) for l in range(L)])
    lambda_init = [0.8 - 0.6 * math.exp(-0.3 * l) for l in range(L)]
    par2 = np.stack([np.concatenate([
        cols(f["subln_g_2"][l]), np.full((P, 1), 1.0 - lambda_init[l], f32), np.full((P, 1), lambda_init[l], f32),
        cols(f["ln1_g_2"][l]), cols(f["ln1_b_2"][l]), cols(f["ln2_g_2"][l]), cols(f["ln2_b_2"][l]),
        rows(np.concatenate([f["lam_q1_2"][l], f["lam_q2_2"][l]])),
        rows(np.concatenate([f["lam_k1_2"][l], f["lam_k2_2"][l]]))], axis=1) for l in range(L)])
    consts = np.concatenate([cols(f["final_norm_g"]), cols(f["c"][0])], axis=1)
    inv = np.stack([1.0 / np.minimum(np.arange(1, T + 1), 2 << g) for g in range(CC)]).astype(f32)
    arrays = {
        "w_ada": np.concatenate([k_tiles(f["w_ada"][l]) for l in range(L)]), "wstream": stream,
        "x_in": f["x"][0].T.reshape(KC, P, T).transpose(1, 0, 2),
        "params1": par1, "params2": par2, "consts": consts,
        "inv_count": np.broadcast_to(inv[None], (P, CC, T)),
    }
    nc = _bacc.Bacc("TRN2", target_bir_lowering=False, num_devices=1)
    aps = {}
    for name in arrays:
        arrays[name] = np.ascontiguousarray(arrays[name])
        aps[name] = nc.dram_tensor(name, arrays[name].shape, F32, kind="ExternalInput").ap()
    out = nc.dram_tensor("out", (P, KC, T), F32, kind="ExternalOutput").ap()
    program(nc, aps["w_ada"], aps["wstream"], aps["x_in"], aps["params1"], aps["params2"], aps["consts"], aps["inv_count"], out)
    r = _run(nc, [arrays], core_ids=[0])
    return r.results[0]["out"].transpose(1, 0, 2).reshape(D, T).T.reshape(1, T, D)
```

```python
import math
from contextlib import ExitStack

import concourse.bass as bass
import numpy as np
from concourse import mybir

F32 = mybir.dt.float32
BF16 = mybir.dt.bfloat16
F32R = mybir.dt.float32r
U32 = mybir.dt.uint32
ALU = mybir.AluOpType
ACT = mybir.ActivationFunctionType
AX = mybir.AxisListType

P = 128
D = 1024
T = 256
L = 2
KC = D // P
TH = T // P
CK = 31
DCONV = 512
CC = DCONV // P
NG, EPG = 4, 8
NE = NG * EPG
NR = NG + NE
EPS1, EPS2 = 1e-6, 1e-5
HD = 64
DH, SH = 4, 8
PH, PTOP, NK = 8, 16, 128
HP = PH * 2
NSEL = PH * PTOP
ALPHA = (2.0 * L) ** 0.25
NEG = -1.0e30

SLOTS = 3
TILE = 2048
HALF = TILE // 2
IN_T, POOL_T, CONV_T, OUT_T = 14, 1, 2, 4
J_IN = 0
J_POOL = J_IN + IN_T
J_CONV = J_POOL + POOL_T
J_OUT = J_CONV + CONV_T
J_MOE = J_OUT + OUT_T
TILES1 = J_MOE + 3 * NE
MEAN_AT, VAR_AT = 10, 12
IN2_T, WO_T, WQ_T, KEY_T, U_T = 12, 4, 8, 1, NK // 2
VALUE_TILES = (4, 5, 10, 11)
J_WO = IN2_T
J_WQ = J_WO + WO_T
J_KEY = J_WQ + WQ_T
J_U = J_KEY + KEY_T
J_V = J_U + U_T
TILES2 = J_V + U_T
TILES = L * (TILES1 + TILES2)
LIN2_T = IN2_T + WO_T + WQ_T
PAIRS1, PAIRS2 = 3 * NE, LIN2_T + 2 * U_T

ADA_G = 4
ADA_GROUPS = L * 6 * D // 256 // ADA_G
ADA_BUFS = 3
assert TILES1 % SLOTS == 0 and TILES2 % SLOTS == 0

HEAD = 13
G4 = T // 4

LB = 3
UN_POOL, UN_CONV, UN_OUT, UN_ROUT = 14, 18, 22, 26
UNITS1 = 27
UN_WO, UN_WQ, UN_SC, UN_U = 12, 16, 24, 32
UNITS2 = UN_U + U_T
BASE2 = L * UNITS1
PARTS1, PARTS2 = 6, 7
assert UNITS1 % LB == 0 and UNITS2 % LB == 0


def columns(parts):
    at, out = 0, {}
    for name, n in parts:
        out[name] = (at, at + n)
        at += n
    return out, at


COL1, NCOL1 = columns([("norm_g", KC), ("b_ada", 6 * KC), ("conv_w", CC * CK), ("conv_b", CC),
                       ("ln_g", CC), ("ln_b", CC), ("b_out", KC), ("pool_scale", KC), ("ffn_g", KC),
                       ("router_w", KC * NR), ("router_b", NR)])
COL2, NCOL2 = columns([("subln_g", 1), ("keep", 1), ("lambda_init", 1), ("ln1_g", KC), ("ln1_b", KC),
                       ("ln2_g", KC), ("ln2_b", KC), ("lam_q", 2 * HD), ("lam_k", 2 * HD)])
COLC, NCOLC = columns([("final_g", KC), ("c", KC)])


def program(nc, w_ada, wstream, x_in, params1, params2, consts, inv_count, out):
    ctx = ExitStack()
    with ctx:
        def sb(name, shape, dt=F32):
            return ctx.enter_context(nc.sbuf_tensor(name, shape, dt))

        def sem(name):
            return ctx.enter_context(nc.semaphore(name))

        slot = [sb(f"slot{i}", [P, TILE]) for i in range(SLOTS)]
        w_hi = [sb(f"w_hi{i}", [P, HALF], F32R) for i in range(2)]
        w_lo = [sb(f"w_lo{i}", [P, HALF], F32R) for i in range(2)]
        arena = sb("arena", [P, NK, T])
        xT = sb("xT", [P, KC, T])
        iota = sb("iota", [P, P])
        ident = sb("ident", [P, P])
        ones = sb("ones", [P, P])
        later = sb("later", [P, P])
        zeros = sb("zeros", [P, P], BF16)
        par1 = sb("par", [P, max(NCOL1, NCOL2)])
        par2 = par1
        cst = sb("cst", [P, NCOLC])
        c_act = sb("c_act", [P, KC])
        mods = sb("mods", [P, L * 6 * KC])
        mod = sb("mod", [P, 6 * KC])
        gain = sb("gain", [P, 2 * KC])
        picksT = sb("picksT", [P, 3, T])
        eact = sb("eact", [P, 2, 2, T], F32R)
        lamb = sb("lamb", [P, 16])
        rsm = sb("rsm", [P, 16])

        REGION = nc.sbuf_usable_end // 32 * 32 - 4 * 2 * KC * T
        assert nc.sbuf_base <= REGION
        x_parts = nc.alloc_sbuf_tensor_at("x_parts", [P, 2, KC, T], F32R, offset=REGION)
        HOTS = 3
        hot = nc.alloc_sbuf_tensor_at("hot", [P, HOTS, 2, 4, P], F32, offset=REGION)
        gated_hot = nc.alloc_sbuf_tensor_at("gated_hot", [P, 2, 4, P], F32, offset=REGION + 4 * HOTS * 8 * P)
        x_hi, x_lo = x_parts[:, 0], x_parts[:, 1]
        act_hi = [x_parts[:, 0, b, :] for b in range(2)]
        act_lo = [x_parts[:, 1, b, :] for b in range(2)]

        def par(t, cols, name):
            a, b = cols[name]
            return t[:, a:b]

        def area(at, n):
            return arena[:, at:at + n, :]

        def flat(at, n):
            return arena[:, at:at + n, :].rearrange("p a b -> p (a b)")

        ADA_IN = [flat(32 * b, 32).rearrange("p (j k n) -> p j k n", j=ADA_G, k=KC) for b in range(ADA_BUFS)]
        ADA_SUM = [area(105 + ADA_G * b, ADA_G) for b in range(2)]
        SQ, H = area(0, 8), area(8, 8)
        UA, SG = area(16, 4), area(20, 4)
        GA, GB = area(24, 8), area(32, 8)
        YA, YB, MIX = area(40, 8), area(48, 8), area(56, 8)
        VPAD = flat(64, 5)[:, 0:CC * (T + CK - 1)].rearrange("p (c t) -> p c t", c=CC)
        UP, CV = area(69, 4), area(73, 4)
        PPAD = [flat(77 + 5 * i, 5)[:, 0:CC * (T + 16)].rearrange("p (c t) -> p c t", c=CC) for i in range(4)]
        PLD, INVC, TMP1 = area(97, 4), area(101, 4), area(105, 8)
        MEAN, VAR, RSTD = area(113, 1), area(114, 1), area(115, 1)
        CVN, CVS = area(116, 4), area(120, 4)
        RT = flat(73, 4)
        SGM, EACT, GU = area(77, 2), area(79, 2), area(81, 2)
        DIAG = flat(83, 1).rearrange("p (h t) -> p h t", h=TH)
        CMB = flat(84, 1)[:, 0:TH * NE].rearrange("p (h e) -> p h e", h=TH)

        DQ, DK, SQT, SKT = area(0, 4), area(4, 4), area(8, 4), area(12, 4)
        DV = flat(16, 4).rearrange("p (h n) -> p h n", h=TH)
        SV = flat(20, 4).rearrange("p (h n) -> p h n", h=TH)
        ALIBI = area(24, 8).rearrange("p (h b) t -> p h b t", h=DH)
        SCO = [area(32 + 2 * i, 2) for i in range(2)]
        EXO = [area(36 + 2 * i, 2) for i in range(2)]
        ATT = [area(40 + i, 1) for i in range(2)]
        ATT_T = area(42, 8).rearrange("p (h b) t -> p h b t", h=DH)
        DIFF, DSQ, DRS = area(50, 4), area(54, 4), area(58, 4)
        MIXT = area(62, 8)
        SW = 384
        ZS, LS, WW = (flat(70 + 12 * i, 12).rearrange("p (g t) -> p g t", g=SH) for i in range(3))
        MASK = flat(106, 2)[:, 0:SW]
        LAM_PRODUCTS = arena[:, 127, 0:2 * HD]
        YC, SQ2, TMP2 = area(0, 8), area(8, 8), area(16, 8)
        MEAN2, VAR2, RSTD2 = area(24, 1), area(25, 1), area(26, 1)
        QT = area(28, 16)
        SC = [flat(112 + 8 * h, 8).rearrange("p (s n) -> p s n", s=HP) for h in range(TH)]
        CAND = area(80, 8)
        WORK = flat(88, 8).rearrange("p (s n) -> p s n", s=HP)
        CWORK = area(88, 8)
        EQS = flat(88, 8).rearrange("p (s a) -> p s a", a=16)
        EQH = flat(88, 8).rearrange("p (h j a) -> p h j a", h=PH, j=16)
        TOPV = flat(96, 1).rearrange("p (s j) -> p s j", s=HP)
        TOPI = flat(97, 1).bitcast(U32).rearrange("p (s j) -> p s j", s=HP)
        TOPF = flat(98, 1).rearrange("p (h q j) -> p h q j", h=PH, q=2)
        BV = flat(99, 1)[:, 0:NSEL].rearrange("p (h j) -> p h j", h=PH)
        BP = flat(100, 1)[:, 0:NSEL].bitcast(U32)
        BPH = BP.rearrange("p (h j) -> p h j", h=PH)
        BA = flat(101, 1)[:, 0:NSEL].bitcast(U32)
        BB = flat(102, 1)[:, 0:NSEL].bitcast(U32)
        BF = flat(103, 1).rearrange("p (q s) -> p q s", q=2)
        BE = flat(104, 1).rearrange("p (t h j) -> p t h j", t=TH, h=PH)
        BS = flat(105, 1)[:, 0:TH * PH].rearrange("p (t h) -> p t h", t=TH)
        picks = flat(106, 3).rearrange("p (q t s) -> p q t s", q=3, t=TH)

        acc = ctx.enter_context(nc.psum_tensor("acc", [P, 4, 512], F32))
        lin = [ctx.enter_context(nc.psum_tensor(f"lin{i}", [P, 512], F32)) for i in range(LB)]
        stat = ctx.enter_context(nc.psum_tensor("stat", [P, 512], F32))
        accT = acc[:, :, :].rearrange("p b (c t) -> p (b c) t", c=2)
        G_PS, U_PS, C_PS = lin[0], lin[1], lin[2]
        sb_bank = (lin[2], stat)

        w_loaded = [sem(f"w_loaded{i}") for i in range(SLOTS)]
        slot_free = [sem(f"slot_free{i}") for i in range(SLOTS)]
        hi_ready = sem("hi_ready")
        split_ready = sem("split_ready")
        act_lo_ready = sem("act_lo_ready")
        hi_used = sem("hi_used")
        half_done = sem("half_done")
        ada_loaded = [sem(f"ada_loaded{i}") for i in range(ADA_BUFS)]
        ada_free, part_sums, sums_used = sem("ada_free"), sem("part_sums"), sem("sums_used")
        small_loaded = sem("small_loaded")
        x_loaded = sem("x_loaded")
        par1_loaded, par2_loaded = sem("par1_loaded"), sem("par2_loaded")
        inv_loaded = sem("inv_loaded")
        consts_made = sem("consts_made")
        zeros_made = sem("zeros_made")
        pads_made = sem("pads_made")
        c_ready = sem("c_ready")
        part_done = sem("part_done")
        values_done = sem("values_done")
        lin_free = sem("lin_free")
        stat_in, stat_out = sem("stat_in"), sem("stat_out")
        var_ready, std_ready = sem("var_ready"), sem("std_ready")
        h_ready = sem("h_ready")
        pooled_ready, mixed_ready = sem("pooled_ready"), sem("mixed_ready")
        cvn_ready, cvs_ready = sem("cvn_ready"), sem("cvs_ready")
        h2_ready = sem("h2_ready")
        h2_split, mixt_split, x3_split = sem("h2_split"), sem("mixt_split"), sem("x3_split")
        rl_ready, re_ready = sem("rl_ready"), sem("re_ready")
        up_done = sem("up_done")
        silu_done, diag_ready, eact_ready = sem("silu_done"), sem("diag_ready"), sem("eact_ready")
        moe_done, moe_out = sem("moe_done"), sem("moe_out")
        layer_end1, layer_end2 = sem("layer_end1"), sem("layer_end2")
        x2_ready = sem("x2_ready")
        alibi_made = sem("alibi_made")
        lam_in, lam_exp = sem("lam_in"), sem("lam_exp")
        sc_done, smax_ready, e_ready = sem("sc_done"), sem("smax_ready"), sem("e_ready")
        att_ready, tr_done, tr_out = sem("att_ready"), sem("tr_done"), sem("tr_out")
        dpv_done, dpv_out, dsq_ready, dss_done = sem("dpv_done"), sem("dpv_out"), sem("dsq_ready"), sem("dss_done")
        dvar_ready, dstd_ready = sem("dvar_ready"), sem("dstd_ready")
        z_done, na_ready, l1_ready, lf_ready = sem("z_done"), sem("na_ready"), sem("l1_ready"), sem("lf_ready")
        lat_done, wl_ready, we_ready, ww_ready = sem("lat_done"), sem("wl_ready"), sem("we_ready"), sem("ww_ready")
        spv_done, spv_out = sem("spv_done"), sem("spv_out")
        bl_ready, be_ready = sem("bl_ready"), sem("be_ready")
        routed = sem("routed")
        ptr_done, ptr_out = sem("ptr_done"), sem("ptr_out")
        hot_ready, scaled_hot = sem("hot_ready"), sem("scaled_hot")
        g_done, gated = sem("g_done"), sem("gated")
        v_done, v_out = sem("v_done"), sem("v_out")
        final_ready, stored = sem("final_ready"), sem("stored")

        block = ctx.enter_context(nc.Block())

        @block.sync
        def _(sp):
            sp.dma_start(cst[:, :], consts[:, :]).then_inc(small_loaded, 16)
            with sp.Fori(0, ADA_GROUPS // ADA_BUFS) as i:
                for b in range(ADA_BUFS):
                    sp.wait_ge(ada_free, i * ADA_BUFS + b + 1)
                    for j in range(ADA_G):
                        sp.dma_start(flat(32 * b + KC * j, KC), w_ada[i * (ADA_BUFS * ADA_G) + (b * ADA_G + j)])\
                          .then_inc(ada_loaded[b], 16)
            with sp.Fori(0, TILES // SLOTS) as i:
                for s in range(SLOTS):
                    sp.wait_ge(slot_free[s], i + 1)
                    sp.dma_start(slot[s][:, :], wstream[i * SLOTS + s]).then_inc(w_loaded[s], 16)

        @block.gpsimd
        def _(pool):
            pool.dma_start(xT[:, :, :], x_in[:, :, :]).then_inc(x_loaded, 16)
            pool.dma_start(INVC, inv_count[:, :, :]).then_inc(inv_loaded, 16)
            nc.gpsimd.iota(iota[:, :], [[1, P]], base=0, channel_multiplier=0,
                           allow_small_or_imprecise_dtypes=True)
            nc.gpsimd.memset(ones[:, :], 1.0)
            pool.drain()
            nc.gpsimd.affine_select(out=ident[:, :], in_=ones[:, :], compare_op=ALU.is_equal, fill=0.0,
                                    base=0, pattern=[[-1, P]], channel_multiplier=1)
            nc.gpsimd.affine_select(out=later[:, :], in_=ones[:, :], compare_op=ALU.is_gt, fill=0.0,
                                    base=0, pattern=[[-1, P]], channel_multiplier=1)
            pool.drain().then_inc(consts_made, 1)
            with pool.Fori(0, L) as l:
                pool.wait_ge(layer_end1, l + 1)
                pool.dma_start(par1[:, 0:NCOL1], params1[l]).then_inc(par1_loaded, 16)
                nc.gpsimd.memset(VPAD[:, :, 0:CK - 1], 0.0)
                for q in PPAD:
                    nc.gpsimd.memset(q[:, :, 0:16], 0.0)
                pool.drain().then_inc(pads_made, 1)
            pool.wait_ge(layer_end1, L + 1)
            with pool.Fori(0, L) as l:
                pool.wait_ge(layer_end2, l + 1)
                pool.dma_start(par2[:, 0:NCOL2], params2[l]).then_inc(par2_loaded, 16)
                for b in range(TH):
                    for h in range(DH):
                        nc.gpsimd.iota(ALIBI[:, h, b, :], [[-1, T]], base=b * P, channel_multiplier=1,
                                       allow_small_or_imprecise_dtypes=True)
                pool.drain()
                for h in range(DH):
                    slope = 2.0 ** (-8.0 * (h + 1) / DH)
                    nc.gpsimd.tensor_scalar(ALIBI[:, h, :, :], ALIBI[:, h, :, :], -slope, None, ALU.mult)
                pool.drain()
                for b in range(TH):
                    for h in range(DH):
                        nc.gpsimd.affine_select(out=ALIBI[:, h, b, :], in_=ALIBI[:, h, b, :],
                                                compare_op=ALU.is_ge, fill=NEG, base=b * P,
                                                pattern=[[-1, T]], channel_multiplier=1)
                nc.gpsimd.memset(MASK, 1.0)
                pool.drain()
                for a in (0, 2 * P):
                    nc.gpsimd.affine_select(out=MASK[:, a:a + P], in_=MASK[:, a:a + P], compare_op=ALU.is_gt,
                                            fill=0.0, base=0, pattern=[[1, P]], channel_multiplier=-1)
                pool.drain().then_inc(alibi_made, 1)

        @block.tensor
        def _(pe):
            mm = nc.tensor.matmul

            def loaded(count, j):
                pe.wait_ge(w_loaded[j % SLOTS], (count + j // SLOTS + 1) * 16)
                return slot[j % SLOTS]

            def column_sum(value, src, n):
                for k in range(n):
                    if k % (n // 2) == 0:
                        pe.wait_ge(stat_in, value * 2 - 1 + k // (n // 2))
                    last = mm(stat[:, 0:T], ones[:, :], src[:, k, :], start=(k == 0), stop=(k == n - 1))
                last.then_inc(stat_out, 1)

            def linear(count, j, rhs, unit, base_unit):
                w = loaded(count, j)
                pe.wait_ge(lin_free, base_unit + unit + 1)
                bank = lin[unit % LB]
                wv = w[:, :].rearrange("p (k n) -> p k n", k=KC)
                for n in range(2):
                    for k in range(KC):
                        last = mm(bank[:, n * T:(n + 1) * T], wv[:, k, n * P:(n + 1) * P], rhs[:, k, :],
                                  start=(k == 0), stop=(k == KC - 1))
                last.then_inc(slot_free[j % SLOTS], 1)

            for s in range(SLOTS):
                pe.sem_inc(slot_free[s], 1)
            pe.sem_inc(half_done, 2)
            pe.sem_inc(hi_used, 2)
            pe.sem_inc(sums_used, 2)
            pe.sem_inc(g_done, 2)
            pe.wait_ge(consts_made, 1)
            pe.wait_ge(zeros_made, 1)
            pe.wait_ge(c_ready, 1)

            zero_row = zeros[:, 0:1].to_broadcast([P, 512])

            def open_acc():
                for b in range(4):
                    mm(acc[:, b, :], zeros[:, :], zero_row, start=True, stop=False)

            def close_acc(done):
                for b in range(4):
                    last = mm(acc[:, b, :], zeros[:, :], zero_row, start=False, stop=True)
                last.then_inc(done, 1)

            def half_tile(rings, c, j0, pairs, outs, closed, x_low=None, x_first=False):
                pe.wait_ge(hi_ready, pairs * 2 + c + 1)
                hi, lo = w_hi[c % 2], w_lo[c % 2]

                def add(out_, w, x, start, stop):
                    a, b = (x, w) if x_first else (w, x)
                    return mm(out_, a, b, start=start, stop=stop)

                for out_, terms in outs:
                    for i, (cols_, x) in enumerate(terms):
                        add(out_, hi[:, cols_], x[0], start=(closed and i == 0), stop=False)
                if x_low is not None:
                    pe.wait_ge(act_lo_ready, x_low)
                for out_, terms in outs:
                    for cols_, x in terms:
                        last = add(out_, hi[:, cols_], x[1], start=False, stop=False)
                last.then_inc(hi_used, 1)
                if c % 2 == 0:
                    pe.wait_ge(split_ready, pairs + c // 2 + 2)
                else:
                    j = j0 + c // 2
                    pe.wait_ge(slot_free[j % SLOTS], rings + j // SLOTS + 2)
                for out_, terms in outs:
                    for i, (cols_, x) in enumerate(terms):
                        last = add(out_, lo[:, cols_], x[0], start=False, stop=(closed and i == len(terms) - 1))
                last.then_inc(half_done, 1)

            def whole_x(k):
                return slice(k * P, (k + 1) * P), (x_hi[:, k, :], x_lo[:, k, :])

            with pe.Fori(0, ADA_GROUPS // 2) as i:
                for b in range(2):
                    pe.wait_ge(part_sums, i * 2 + b + 1)
                    for n in range(2 * ADA_G):
                        last = mm(acc[:, 0, bass.ds((i * 2 + b) * (2 * ADA_G) + n, 1)],
                                  ADA_SUM[b][:, n // 2, (n % 2) * P:(n % 2 + 1) * P], ones[:, 0:1],
                                  start=True, stop=True)
                    last.then_inc(sums_used, 1)

            with pe.Fori(0, L) as l:
                rings = l * (TILES1 // SLOTS)
                units = l * UNITS1
                column_sum(l * 4 + 1, SQ, KC)
                pe.wait_ge(h_ready, l + 1)
                for j in range(IN_T):
                    linear(rings, J_IN + j, H, j, units)
                    if j == MEAN_AT:
                        column_sum(l * 4 + 2, CV, CC)
                    elif j == VAR_AT:
                        column_sum(l * 4 + 3, SQ, CC)
                pe.wait_ge(pooled_ready, l + 1)
                w = loaded(rings, J_POOL)
                for g in range(CC):
                    pe.wait_ge(lin_free, units + UN_POOL + g + 1)
                    bank = lin[(UN_POOL + g) % LB]
                    for n in range(2):
                        last = mm(bank[:, n * T:(n + 1) * T], w[:, (2 * g + n) * P:(2 * g + n + 1) * P],
                                  PLD[:, g, :], start=True, stop=True)
                    last.then_inc(slot_free[J_POOL % SLOTS] if g == CC - 1 else part_done, 1)
                pe.wait_ge(cvs_ready, l + 1)
                for j in range(CONV_T):
                    w = loaded(rings, J_CONV + j)[:, :].rearrange("p (k n) -> p k n", k=CC)
                    for half in range(2):
                        u = UN_CONV + 2 * j + half
                        pe.wait_ge(lin_free, units + u + 1)
                        for n in range(2):
                            for k in range(CC):
                                m = (2 * half + n) * P
                                last = mm(lin[u % LB][:, n * T:(n + 1) * T], w[:, k, m:m + P], CVS[:, k, :],
                                          start=(k == 0), stop=(k == CC - 1))
                        last.then_inc(slot_free[(J_CONV + j) % SLOTS] if half else part_done, 1)
                pe.wait_ge(mixed_ready, l + 1)
                for j in range(OUT_T):
                    linear(rings, J_OUT + j, MIX, UN_OUT + j, units)
                column_sum(l * 4 + 4, SQ, KC)
                pe.wait_ge(h2_ready, l + 1)
                pe.wait_ge(lin_free, units + UN_ROUT + 1)
                rw = par(par1, COL1, "router_w").rearrange("p (k n) -> p k n", k=KC)
                for th in range(TH):
                    for k in range(KC):
                        last = mm(lin[UN_ROUT % LB][:, th * NR:(th + 1) * NR], H[:, k, th * P:(th + 1) * P],
                                  rw[:, k, :], start=(k == 0), stop=(k == KC - 1))
                last.then_inc(part_done, 1)
                pe.wait_ge(lin_free, units + UNITS1 + LB)
                open_acc()

                pairs = l * PAIRS1
                e0 = l * NE
                pe.wait_ge(h2_split, l + 1)

                def expert_in(c, i, e, bank, free):
                    pe.wait_ge(free, e + 1)
                    for n in range(2):
                        half_tile(rings + i, c + n, J_MOE, pairs + i * 3,
                                  [(bank[:, n * T:(n + 1) * T], [whole_x(k) for k in range(KC)])], True)

                def spread_weights(e):
                    pe.wait_ge(diag_ready, e + 1)
                    for th in range(TH):
                        last = mm(C_PS[:, th * P:(th + 1) * P], ones[:, :], DIAG[:, th, :], start=True, stop=True)
                    last.then_inc(up_done, 1)

                def expert_down(c, i, e):
                    pe.wait_ge(eact_ready, e + 2)
                    for half in range(2):
                        outs = [(accT[:, 4 * half + n, :],
                                 [(slice(k * 512 + n * P, k * 512 + (n + 1) * P), (eact[:, 0, k, :], eact[:, 1, k, :]))
                                  for k in range(2)]) for n in range(4)]
                        half_tile(rings + i, c + half, J_MOE, pairs + i * 3, outs, False)

                expert_in(0, 0, e0, G_PS, silu_done)
                expert_in(2, 0, e0, U_PS, eact_ready)
                spread_weights(e0)
                with pe.Fori(0, NE - 1) as i:
                    expert_in(4, i, e0 + i + 1, G_PS, silu_done)
                    expert_down(6, i, e0 + i)
                    expert_in(8, i, e0 + i + 1, U_PS, eact_ready)
                    spread_weights(e0 + i + 1)
                expert_down(2 * PAIRS1 - 2, 0, e0 + NE - 1)
                close_acc(moe_done)

            column_sum(L * 4 + 1, SQ, KC)

            with pe.Fori(0, L) as l:
                rings = l * (TILES2 // SLOTS) + L * TILES1 // SLOTS
                units = l * UNITS2 + BASE2
                stat0 = l * 4 + (L * 4 + 1)
                pairs = l * PAIRS2 + L * PAIRS1

                def split_linear(t):
                    for n in range(2):
                        half_tile(rings, 2 * t + n, 0, pairs,
                                  [(lin[t % LB][:, n * T:(n + 1) * T], [whole_x(k) for k in range(KC)])], True)

                def split_values(t):
                    bank = lin[t % LB]
                    mm(bank[:, :], zeros[:, :], zero_row, start=True, stop=False)
                    for a in range(2):
                        outs = [(bank[:, th * T:(th + 1) * T],
                                 [(slice(k * T, (k + 1) * T),
                                   [x_parts[:, q, 4 * a + k, th * P:(th + 1) * P] for q in range(2)])
                                  for k in range(KC // 2)]) for th in range(TH)]
                        half_tile(rings, 2 * t + a, 0, pairs, outs, False, x_first=True)
                    mm(bank[:, :], zeros[:, :], zero_row, start=False, stop=True).then_inc(values_done, 1)

                pe.wait_ge(x2_ready, l + 1)
                for j in range(IN2_T):
                    pe.wait_ge(lin_free, units + j + 1)
                    (split_values if j in VALUE_TILES else split_linear)(j)

                def scores(d):
                    b, h = divmod(d, DH)
                    if d >= 2:
                        pe.wait_ge(smax_ready, l * 8 + d - 1)
                    for m in range(2):
                        r = slice(m * HD, (m + 1) * HD)
                        last = mm(acc[:, 2 * (d % 2) + m, 0:(b + 1) * P], DQ[r, h, b * P:(b + 1) * P],
                                  DK[r, h, 0:(b + 1) * P], start=True, stop=True)
                    last.then_inc(sc_done, 1)

                def sb_rows(hh):
                    return slice((hh % 2) * HD, (hh % 2 + 1) * HD)

                def sb_scores(hh):
                    if hh >= 2:
                        pe.wait_ge(wl_ready, l * SH + hh - 1)
                    bank, r, c = sb_bank[hh % 2], sb_rows(hh), hh // 2
                    mm(bank[:, 0:T], SKT[r, c, 0:P], SQT[r, c, :], start=True, stop=True)
                    mm(bank[:, T:SW], SKT[r, c, P:T], SQT[r, c, P:T], start=True, stop=True).then_inc(z_done, 1)

                def sb_later(hh):
                    pe.wait_ge(lf_ready, l * SH + hh + 1)
                    bank = sb_bank[hh % 2]
                    mm(bank[:, 0:T], later[:, :], LS[:, hh, 0:T], start=True, stop=False)
                    mm(bank[:, P:T], ones[:, :], LS[:, hh, T:SW], start=False, stop=True)
                    mm(bank[:, T:SW], later[:, :], LS[:, hh, T:SW], start=True, stop=True).then_inc(lat_done, 1)

                pe.wait_ge(lin_free, units + IN2_T + LB)
                scores(0)
                scores(1)
                for d in range(8):
                    b, h = divmod(d, DH)
                    sb_scores(d)
                    if d >= 1:
                        sb_later(d - 1)
                    pe.wait_ge(att_ready, l * 8 + d + 1)
                    if d >= 2:
                        pe.wait_ge(tr_out, l * 8 + d - 1)
                    for kb in range(b + 1):
                        last = nc.tensor.transpose(lin[d % 2][:, kb * P:(kb + 1) * P],
                                                   ATT[d % 2][:, 0, kb * P:(kb + 1) * P], ident[:, :])
                    last.then_inc(tr_done, 1)
                    if d + 2 < 8:
                        scores(d + 2)
                sb_later(SH - 1)
                pe.wait_ge(tr_out, l * 8 + 8)
                for h in range(DH):
                    o = accT[:, h, :]
                    mm(o, DV[:, 0, h * P:(h + 1) * P], ATT_T[:, h, 0, :], start=True, stop=False)
                    last = mm(accT[:, h, P:T], DV[:, 1, h * P:(h + 1) * P], ATT_T[:, h, 1, P:T],
                              start=False, stop=True)
                last.then_inc(dpv_done, 1)
                pe.wait_ge(wl_ready, l * SH + SH)
                for w4 in range(2):
                    for hh in range(4 * w4, 4 * w4 + 4):
                        pe.wait_ge(ww_ready, l * SH + hh + 1)
                        o, c = sb_bank[w4][sb_rows(hh), :], hh // 2 % 2
                        mm(o[:, c * T:(c + 1) * T], SV[:, 0, hh * HD:(hh + 1) * HD], WW[:, hh, 0:T],
                           start=True, stop=False)
                        last = mm(o[:, c * T + P:(c + 1) * T], SV[:, 1, hh * HD:(hh + 1) * HD],
                                  WW[:, hh, T:SW], start=False, stop=True)
                    last.then_inc(spv_done, 1)
                pe.wait_ge(dsq_ready, l + 1)
                for q in range(2):
                    last = mm(acc[:, 2 + q, :], ones[:, :], DSQ[:, 2 * q:2 * q + 2, :], start=True, stop=True)
                last.then_inc(dss_done, 1)
                pe.wait_ge(mixt_split, l + 1)
                for t in range(J_WO, J_WO + WO_T):
                    pe.wait_ge(lin_free, units + t + 1)
                    split_linear(t)
                column_sum(stat0 + 1, YC, KC)
                column_sum(stat0 + 2, SQ2, KC)
                pe.wait_ge(x3_split, l + 1)
                for t in range(J_WQ, J_WQ + WQ_T):
                    pe.wait_ge(lin_free, units + t + 1)
                    split_linear(t)
                pe.wait_ge(lin_free, units + UN_SC + LB)
                w = loaded(rings, J_KEY)[:, :].rearrange("p (s n) -> p s n", s=HP)
                for s in range(8):
                    th, q = divmod(s, 4)
                    pe.wait_ge(lin_free, units + UN_SC + s + 1)
                    for a in range(4):
                        hp = 4 * q + a
                        last = mm(lin[(UN_SC + s) % LB][:, a * P:(a + 1) * P], QT[:, hp, th * P:(th + 1) * P],
                                  w[:, hp, :], start=True, stop=True)
                    last.then_inc(slot_free[J_KEY % SLOTS] if s == 7 else part_done, 1)

                pairs_u = pairs + LIN2_T

                def u_tile(j, i):
                    pe.wait_ge(lin_free, units + i * SLOTS + (UN_U + j + 1))
                    for a in range(2):
                        half_tile(rings + i, 2 * j + a, J_U, pairs_u + i * SLOTS,
                                  [(lin[(UN_U + j) % LB][:, a * T:(a + 1) * T], [whole_x(k) for k in range(KC)])], True)

                with pe.Fori(0, HEAD) as i:
                    for s in range(SLOTS):
                        u_tile(s, i)
                pe.wait_ge(routed, l + 1)
                for q in range(3):
                    for th in range(TH):
                        a = q * TH + th
                        last = nc.tensor.transpose(acc[:, 2 + a // 4, (a % 4) * P:(a % 4 + 1) * P],
                                                   picks[:, q, th, :], ident[:, :])
                last.then_inc(ptr_done, 1)
                with pe.Fori(HEAD, U_T // SLOTS) as i:
                    for s in range(SLOTS):
                        u_tile(s, i)
                u_tile(U_T - 1, 0)

                def gate_group(g, i):
                    n = l * G4 + i * 6 + g
                    pe.wait_ge(scaled_hot, n + 1)
                    for t in range(4):
                        last = mm(acc[:, g % HOTS, t * P:(t + 1) * P], gated_hot[:, g % 2, t, :],
                                  hot[:, g % HOTS, 1, t, :], start=True, stop=True)
                    last.then_inc(g_done, 1)

                with pe.Fori(0, G4 // 6) as i:
                    for g in range(6):
                        gate_group(g, i)
                for g in range(G4 // 6 * 6, G4):
                    gate_group(g, 0)
                pe.wait_ge(gated, l + 1)
                open_acc()

                def v_tile(j, i):
                    for a in range(2):
                        outs = [(accT[:, n, :], [(slice(n * P, (n + 1) * P), (act_hi[a], act_lo[a]))]) for n in range(KC)]
                        half_tile(rings + i, 2 * j + a, J_V, pairs_u + i * SLOTS + U_T, outs, False,
                                  l * (2 * U_T) + i * (2 * SLOTS) + (2 * j + a + 1))

                with pe.Fori(0, U_T // SLOTS) as i:
                    for s in range(SLOTS):
                        v_tile(s, i)
                v_tile(U_T - 1, 0)
                close_acc(v_done)
                column_sum(stat0 + 3, YC, KC)
                column_sum(stat0 + 4, SQ2, KC)

        @block.scalar
        def _(act):
            A = nc.scalar.activation

            def tile_through(rings, j):
                act.wait_ge(slot_free[j % SLOTS], rings + j // SLOTS + 2)

            def high_part(rings, c, j0, pairs, arena_col=None):
                j = j0 + c // 2
                number = pairs * 2
                act.wait_ge(w_loaded[j % SLOTS], (rings + j // SLOTS + 1) * 16)
                act.wait_ge(hi_used, number + c + 1)
                if c % 2 == 0:
                    act.wait_ge(split_ready, pairs + c // 2 + 1)
                else:
                    act.wait_ge(slot_free[(j - 1) % SLOTS], rings + (j - 1) // SLOTS + 2)
                last = A(w_hi[c % 2][:, :], slot[j % SLOTS][:, (c % 2) * HALF:(c % 2 + 1) * HALF], ACT.Copy)
                if arena_col is not None:
                    act.wait_ge(half_done, number + c + 1)
                    last = A(act_hi[c % 2].unsqueeze(1), arena[:, bass.ds(arena_col, 1), :], ACT.Copy)
                last.then_inc(hi_ready, 1)

            def halves_done(number):
                act.wait_ge(half_done, number + 2)

            def unit1(l, u):
                part = {14: 1, 15: 2, 16: 3, UN_CONV: 4, UN_CONV + 2: 5, UN_ROUT: 6}
                if u in part:
                    act.wait_ge(part_done, l * PARTS1 + part[u])
                elif u < UN_POOL:
                    tile_through(l * (TILES1 // SLOTS), J_IN + u)
                elif u < UN_CONV:
                    tile_through(l * (TILES1 // SLOTS), J_POOL)
                elif u < UN_OUT:
                    tile_through(l * (TILES1 // SLOTS), J_CONV + (u - UN_CONV) // 2)
                else:
                    tile_through(l * (TILES1 // SLOTS), J_OUT + u - UN_OUT)
                return lin[u % LB]

            def unit2(l, u):
                count = l * (TILES2 // SLOTS) + L * TILES1 // SLOTS
                if UN_SC <= u < UN_SC + 7:
                    act.wait_ge(part_done, l * PARTS2 + (L * PARTS1 + u - UN_SC + 1))
                elif u in VALUE_TILES:
                    act.wait_ge(values_done, l * len(VALUE_TILES) + VALUE_TILES.index(u) + 1)
                elif u < UN_SC:
                    halves_done(l * (2 * PAIRS2) + (L * 2 * PAIRS1 + 2 * u + 2))
                else:
                    tile_through(count, J_KEY)
                return lin[u % LB]

            def root(value, src, dst):
                act.wait_ge(var_ready, value)
                A(dst, src, ACT.Sqrt).then_inc(std_ready, 1)

            act.sem_inc(lin_free, LB)
            act.sem_inc(silu_done, 1)
            act.wait_ge(small_loaded, 16)
            A(c_act[:, :], par(cst, COLC, "c"), ACT.Silu).then_inc(c_ready, 1)

            with act.Fori(0, L) as l:
                units = l * UNITS1
                root(l * 3 + 1, VAR, RSTD)
                dsts = [UA[:, 0:2], SG[:, 0:2], UA[:, 2:4], SG[:, 2:4], UP[:, 0:2], UP[:, 2:4]]
                dsts += [GA[:, 2 * q:2 * q + 2] for q in range(4)] + [GB[:, 2 * q:2 * q + 2] for q in range(4)]
                for j, dst in enumerate(dsts):
                    func = ACT.Copy if j in (0, 2, 4, 5) else ACT.Sigmoid
                    A(dst, unit1(l, j)[:, :].rearrange("p (c t) -> p c t", c=2), func).then_inc(lin_free, 1)
                    if j == VAR_AT:
                        root(l * 3 + 2, VAR, RSTD)
                        act.wait_ge(cvn_ready, l + 1)
                        g, b = par(par1, COL1, "ln_g"), par(par1, COL1, "ln_b")
                        for k in range(CC):
                            last = A(CVS[:, k], CVN[:, k], ACT.Silu, scale=g[:, k:k + 1], bias=b[:, k:k + 1])
                        last.then_inc(cvs_ready, 1)
                ps = par(par1, COL1, "pool_scale")
                for j in range(4):
                    bank = unit1(l, UN_POOL + j)
                    for n in range(2):
                        last = A(YB[:, 2 * j + n], bank[:, n * T:(n + 1) * T], ACT.Identity,
                                 scale=ps[:, 2 * j + n:2 * j + n + 1])
                    last.then_inc(lin_free, 1)
                bo = par(par1, COL1, "b_out")
                for j in range(4):
                    bank = unit1(l, UN_CONV + j)
                    for n in range(2):
                        last = A(YA[:, 2 * j + n], bank[:, n * T:(n + 1) * T], ACT.Identity,
                                 bias=bo[:, 2 * j + n:2 * j + n + 1])
                    last.then_inc(lin_free, 1)
                for j in range(4):
                    bank = unit1(l, UN_OUT + j)
                    for n in range(2):
                        m = 2 * KC + 2 * j + n
                        last = A(TMP1[:, 2 * j + n], bank[:, n * T:(n + 1) * T], ACT.Identity,
                                 scale=mod[:, m:m + 1])
                    last.then_inc(lin_free, 1)
                root(l * 3 + 3, VAR, RSTD)
                A(RT[:, 0:TH * NR], unit1(l, UN_ROUT)[:, 0:TH * NR], ACT.Copy).then_inc(lin_free, 1)
                rings, pairs = l * (TILES1 // SLOTS), l * PAIRS1
                high_part(rings, 0, J_MOE, pairs)
                high_part(rings, 1, J_MOE, pairs)
                act.wait_ge(rl_ready, l * 2 + 1)
                A(RT[:, 100:108], RT[:, 100:108], ACT.Exp).then_inc(re_ready, 1)
                act.wait_ge(rl_ready, l * 2 + 2)
                A(RT[:, 200:216], RT[:, 200:216], ACT.Exp).then_inc(re_ready, 1)

                def expert_silu(e, halves):
                    halves_done(halves)
                    act.wait_ge(eact_ready, l * NE + e + 1)
                    A(SGM, G_PS[:, :].rearrange("p (c t) -> p c t", c=2), ACT.Silu).then_inc(silu_done, 1)

                high_part(rings, 2, J_MOE, pairs)
                high_part(rings, 3, J_MOE, pairs)
                expert_silu(0, pairs * 2 + 2)
                high_part(rings, 4, J_MOE, pairs)
                with act.Fori(0, NE - 1) as i:
                    high_part(rings + i, 5, J_MOE, pairs + i * 3)
                    high_part(rings + i, 6, J_MOE, pairs + i * 3)
                    high_part(rings + i, 7, J_MOE, pairs + i * 3)
                    expert_silu(i + 1, pairs * 2 + i * 6 + 6)
                    high_part(rings + i, 8, J_MOE, pairs + i * 3)
                    high_part(rings + i, 9, J_MOE, pairs + i * 3)
                    high_part(rings + i, 10, J_MOE, pairs + i * 3)
                high_part(rings, 2 * PAIRS1 - 1, J_MOE, pairs)
                act.wait_ge(moe_done, l + 1)
                for n in range(KC):
                    last = A(TMP1[:, n], accT[:, n, :], ACT.Identity, scale=mod[:, 5 * KC + n:5 * KC + n + 1])
                last.then_inc(moe_out, 1)

            root(L * 3 + 1, VAR, RSTD)

            with act.Fori(0, L) as l:
                units = l * UNITS2 + BASE2
                rings = l * (TILES2 // SLOTS) + L * TILES1 // SLOTS
                pairs = l * PAIRS2 + L * PAIRS1
                high_part(rings, 0, 0, pairs)
                high_part(rings, 1, 0, pairs)
                for j in range(IN2_T):
                    high_part(rings, 2 * j + 2, 0, pairs)
                    high_part(rings, 2 * j + 3, 0, pairs)
                    bank = unit2(l, j)[:, :].rearrange("p (c t) -> p c t", c=2)
                    which, half = divmod(j, 2)
                    if which in (2, 5):
                        dst = (DV if which == 2 else SV)[:, :, half * T:(half + 1) * T]
                    else:
                        dst = {0: DQ, 1: DK, 3: SQT, 4: SKT}[which][:, 2 * half:2 * half + 2]
                    A(dst, bank, ACT.Copy).then_inc(lin_free, 1)
                act.wait_ge(lam_in, l + 1)
                A(lamb[:, 2:4], lamb[:, 0:2], ACT.Exp).then_inc(lam_exp, 1)

                def soft(d):
                    b = d // DH
                    act.wait_ge(smax_ready, l * 8 + d + 1)
                    for m in range(2):
                        last = A(EXO[d % 2][:, m, 0:(b + 1) * P], SCO[d % 2][:, m, 0:(b + 1) * P], ACT.Exp,
                                 bias=rsm[:, 4 * (d % 2) + m:4 * (d % 2) + m + 1],
                                 accum_out=rsm[:, 4 * (d % 2) + 2 + m:4 * (d % 2) + 3 + m])
                    last.then_inc(e_ready, 1)

                def move(d):
                    b, h = divmod(d, DH)
                    act.wait_ge(tr_done, l * 8 + d + 1)
                    A(ATT_T[:, h, 0:b + 1, b * P:(b + 1) * P],
                      lin[d % 2][:, 0:(b + 1) * P].rearrange("p (k q) -> p k q", k=b + 1),
                      ACT.Copy).then_inc(tr_out, 1)

                def sb_softplus(hh):
                    act.wait_ge(na_ready, l * SH + hh + 1)
                    A(LS[:, hh], LS[:, hh], ACT.Exp)
                    act.drain()
                    A(LS[:, hh], LS[:, hh], ACT.Ln, bias=1.0).then_inc(l1_ready, 1)

                def sb_exp(hh):
                    act.wait_ge(wl_ready, l * SH + hh + 1)
                    A(WW[:, hh], WW[:, hh], ACT.Exp).then_inc(we_ready, 1)

                soft(0)
                for d in range(8):
                    sb_softplus(d)
                    if d + 1 < 8:
                        soft(d + 1)
                    if d >= 1:
                        sb_exp(d - 1)
                    move(d)
                sb_exp(SH - 1)
                act.wait_ge(dpv_done, l + 1)
                A(DIFF, accT[:, 0:4, :], ACT.Copy).then_inc(dpv_out, 1)
                for w4 in range(2):
                    act.wait_ge(spv_done, l * 2 + w4 + 1)
                    A(MIXT[:, 4 + 2 * w4:6 + 2 * w4], sb_bank[w4][:, :].rearrange("p (c t) -> p c t", c=2),
                      ACT.Copy).then_inc(spv_out, 1)
                act.wait_ge(dvar_ready, l + 1)
                A(DRS, DRS, ACT.Sqrt).then_inc(dstd_ready, 1)
                for j in range(WO_T):
                    high_part(rings, 2 * (J_WO + j) + 2, 0, pairs)
                    high_part(rings, 2 * (J_WO + j) + 3, 0, pairs)
                    A(TMP2[:, 2 * j:2 * j + 2], unit2(l, UN_WO + j)[:, :].rearrange("p (c t) -> p c t", c=2),
                      ACT.Copy).then_inc(lin_free, 1)
                root(L * 3 + 1 + l * 2 + 1, VAR2, RSTD2)
                for j in range(WQ_T):
                    if j < WQ_T - 1:
                        high_part(rings, 2 * (J_WQ + j) + 2, 0, pairs)
                        high_part(rings, 2 * (J_WQ + j) + 3, 0, pairs)
                    else:
                        high_part(rings, 0, J_U, pairs + LIN2_T)
                    A(QT[:, 2 * j:2 * j + 2], unit2(l, UN_WQ + j)[:, :].rearrange("p (c t) -> p c t", c=2),
                      ACT.Copy).then_inc(lin_free, 1)
                for s in range(8):
                    th, q = divmod(s, 4)
                    A(SC[th][:, 4 * q:4 * q + 4, :],
                      unit2(l, UN_SC + s)[:, :].rearrange("p (a n) -> p a n", a=4),
                      ACT.Copy).then_inc(lin_free, 1)

                pairs = l * PAIRS2 + (L * PAIRS1 + LIN2_T)

                def gelu(j, i):
                    halves_done(pairs * 2 + i * 6 + (2 * j + 2))
                    A(arena[:, bass.ds(i * 6 + 2 * j, 2), :],
                      lin[(UN_U + j) % LB][:, :].rearrange("p (c t) -> p c t", c=2), ACT.Gelu).then_inc(lin_free, 1)

                def u_steps(i):
                    for s in range(SLOTS):
                        high_part(rings + i, 2 * s + 1, J_U, pairs + i * 3)
                        high_part(rings + i, 2 * s + 2, J_U, pairs + i * 3)
                        gelu(s, i)

                def gelu_table():
                    A(lamb[:, 10:11], ones[:, 0:1], ACT.Gelu)

                gelu_table()
                with act.Fori(0, HEAD - 1) as i:
                    u_steps(i)
                act.wait_ge(bl_ready, l + 1)
                A(BE, BE, ACT.Exp).then_inc(be_ready, 1)
                gelu_table()
                with act.Fori(HEAD - 1, HEAD) as i:
                    u_steps(i)
                act.wait_ge(ptr_done, l + 1)
                A(picksT[:, 0:2, :], acc[:, 2, :].rearrange("p (q t) -> p q t", q=2), ACT.Copy)
                A(picksT[:, 2, :], acc[:, 3, 0:T], ACT.Copy).then_inc(ptr_out, 1)
                with act.Fori(HEAD, U_T // SLOTS) as i:
                    u_steps(i)
                high_part(rings, 2 * U_T - 1, J_U, pairs)
                gelu(U_T - 1, 0)

                def scale_group(g, i):
                    n = l * G4 + i * 6 + g
                    act.wait_ge(hot_ready, n + 1)
                    act.wait_ge(g_done, n + 1)
                    for t in range(4):
                        last = A(gated_hot[:, g % 2, t, :], hot[:, g % HOTS, 0, t, :], ACT.Identity,
                                 scale=picksT[:, 2, bass.ds(i * 24 + (4 * g + t), 1)])
                    last.then_inc(scaled_hot, 1)

                with act.Fori(0, G4 // 6) as i:
                    for g in range(6):
                        scale_group(g, i)
                for g in range(G4 // 6 * 6, G4):
                    scale_group(g, 0)
                act.wait_ge(gated, l + 1)
                with act.Fori(0, U_T // SLOTS) as i:
                    for c in range(2 * SLOTS):
                        high_part(rings + i, c, J_V, pairs + i * 3 + U_T, i * 6 + c)
                for c in range(U_T // SLOTS * 6, 2 * U_T):
                    high_part(rings, c, J_V, pairs + U_T, c)
                act.wait_ge(v_done, l + 1)
                A(TMP2, accT, ACT.Copy).then_inc(v_out, 1)
                root(L * 3 + 1 + l * 2 + 2, VAR2, RSTD2)
            act.wait_ge(final_ready, 1)
            act.dma_start(out[:, :, :], xT[:, :, :]).then_inc(stored, 16)
            act.wait_ge(stored, 16)

        @block.vector
        def _(dve):
            V = nc.vector
            TT, TS, STT = V.tensor_tensor, V.tensor_scalar, V.scalar_tensor_tensor

            def over(ap, n):
                return ap.to_broadcast([P, n, T])

            def rstd(sum_value, root_value, src_bank, n, eps, var, dst):
                dve.wait_ge(stat_out, sum_value)
                TS(var[:, 0, :], src_bank, 1.0 / n, eps, ALU.mult, ALU.add).then_inc(var_ready, 1)
                dve.wait_ge(std_ready, root_value)
                V.reciprocal(dst[:, 0, :], dst[:, 0, :])
                dve.drain()

            def halves_of(t):
                n = t.shape[1] // 2
                return slice(0, n), slice(n, 2 * n)

            def squares(src, dst):
                for c in halves_of(dst):
                    TT(dst[:, c], src[:, c], src[:, c], ALU.mult).then_inc(stat_in, 1)

            def modulated(dst, gains, shifts):
                TT(dst, xT[:, :, :], over(RSTD, KC), ALU.mult)
                dve.drain()
                for k in range(KC):
                    if shifts is None:
                        TS(xT[:, k, :], dst[:, k, :], gains[:, k:k + 1], None, ALU.mult)
                    else:
                        TS(dst[:, k, :], dst[:, k, :], gains[:, k:k + 1], shifts[:, k:k + 1], ALU.mult, ALU.add)

            def low_part(c, j, number, arena_col=None):
                dve.wait_ge(hi_ready, number + c + 1)
                if arena_col is not None:
                    TT(act_lo[c % 2].unsqueeze(1), arena[:, bass.ds(arena_col, 1), :], act_hi[c % 2].bitcast(F32).unsqueeze(1),
                       ALU.subtract).then_inc(act_lo_ready, 1)
                dve.wait_ge(half_done, number + c + 1)
                TT(w_lo[c % 2][:, :], slot[j % SLOTS][:, (c % 2) * HALF:(c % 2 + 1) * HALF], w_hi[c % 2][:, :].bitcast(F32),
                   ALU.subtract).then_inc(slot_free[j % SLOTS] if c % 2 else split_ready, 1)

            dve.sem_inc(eact_ready, 1)
            dve.sem_inc(split_ready, 1)
            dve.sem_inc(ada_free, ADA_BUFS)
            V.memset(zeros[:, :], 0.0).then_inc(zeros_made, 1)
            dve.wait_ge(small_loaded, 16)
            dve.wait_ge(x_loaded, 16)
            dve.wait_ge(inv_loaded, 16)
            dve.wait_ge(consts_made, 1)

            dve.wait_ge(c_ready, 1)
            with dve.Fori(0, ADA_GROUPS // 6) as i:
                for g in range(6):
                    dst = ADA_SUM[g % 2]
                    dve.wait_ge(ada_loaded[g % ADA_BUFS], (i * 2 + g // ADA_BUFS + 1) * (16 * ADA_G))
                    dve.wait_ge(sums_used, i * 6 + g + 1)
                    src = ADA_IN[g % ADA_BUFS]
                    TS(dst, src[:, :, 0, :], c_act[:, 0:1], None, ALU.mult)
                    dve.drain()
                    for k in range(1, KC):
                        STT(dst, src[:, :, k, :], c_act[:, k:k + 1], dst, ALU.mult, ALU.add)
                        if k < KC - 1:
                            dve.drain()
                    dve.drain().then_inc(part_sums, 1)
                    dve.sem_inc(ada_free, 1)
            dve.wait_ge(sums_used, ADA_GROUPS + 2)
            V.tensor_copy(mods[:, :], acc[:, 0, 0:L * 6 * KC])
            dve.drain().then_inc(layer_end1, 1)

            with dve.Fori(0, L) as l:
                units = l * UNITS1

                def moved(u):
                    dve.wait_ge(lin_free, units + u + 1 + LB)

                squares(xT[:, :, :], SQ)
                rstd(l * 4 + 1, l * 3 + 1, stat[:, 0:T], D, EPS1, VAR, RSTD)
                dve.wait_ge(par1_loaded, l * 16 + 16)
                TT(mod[:, :], mods[:, bass.ds(l * (6 * KC), 6 * KC)], par(par1, COL1, "b_ada"), ALU.add)
                dve.drain()
                for q, name in ((0, "norm_g"), (1, "ffn_g")):
                    s = (3 * q + 1) * KC
                    STT(gain[:, q * KC:(q + 1) * KC], mod[:, s:s + KC], 1.0, par(par1, COL1, name), ALU.add, ALU.mult)
                dve.drain()
                modulated(H, gain[:, 0:KC], mod[:, 0:KC])
                dve.drain().then_inc(h_ready, 1)
                dve.wait_ge(pads_made, l + 1)
                cw = par(par1, COL1, "conv_w").rearrange("p (c k) -> p c k", c=CC)
                cb = par(par1, COL1, "conv_b")

                def tap(dst, c, k):
                    STT(dst[:, c, :], VPAD[:, c, bass.ds(k, T)], cw[:, c, bass.ds(k, 1)], dst[:, c, :], ALU.mult, ALU.add)

                for half in range(2):
                    both = (2 * half, 2 * half + 1)
                    cs = slice(2 * half, 2 * half + 2)
                    moved(2 * half + 1)
                    TT(VPAD[:, cs, CK - 1:], UA[:, cs], SG[:, cs], ALU.mult)
                    dve.drain()
                    for c in both:
                        TS(CV[:, c, :], VPAD[:, c, 0:T], cw[:, c, 0:1], cb[:, c:c + 1], ALU.mult, ALU.add)
                        TS(CVN[:, c, :], VPAD[:, c, 1:1 + T], cw[:, c, 1:2], None, ALU.mult)
                    dve.drain()
                    with dve.Fori(0, (CK - 3) // 4) as k4:
                        for k in (2, 4):
                            for c in both:
                                tap(CV, c, k4 * 4 + k)
                                tap(CVN, c, k4 * 4 + (k + 1))
                            dve.drain()
                    for c in both:
                        tap(CV, c, CK - 1)
                    dve.drain()
                    TT(CV[:, cs], CV[:, cs], CVN[:, cs], ALU.add)
                dve.drain().then_inc(stat_in, 2)
                moved(5)
                V.tensor_copy(PPAD[0][:, :, 16:], UP)
                dve.drain()
                for s in range(4):
                    w = 1 << s
                    src = PPAD[s]
                    c = slice(s, CC)
                    dst = PPAD[s + 1][:, c, 16:] if s < 3 else PLD[:, c, :]
                    TT(dst, src[:, c, 16:], src[:, c, 16 - w:16 + T - w], ALU.add)
                    dve.drain()
                for s in range(3):
                    TT(PLD[:, s, :], PPAD[s + 1][:, s, 16:], INVC[:, s, :], ALU.mult)
                TT(PLD[:, 3, :], PLD[:, 3, :], INVC[:, 3, :], ALU.mult)
                dve.drain()
                TT(PLD, PLD, UP, ALU.subtract).then_inc(pooled_ready, 1)
                dve.wait_ge(stat_out, l * 4 + 2)
                TS(MEAN[:, 0, :], stat[:, 0:T], 1.0 / DCONV, None, ALU.mult)
                dve.drain()
                TT(CVN, CV, over(MEAN, CC), ALU.subtract)
                dve.drain()
                squares(CVN, SQ[:, 0:CC, :])
                rstd(l * 4 + 3, l * 3 + 2, stat[:, 0:T], DCONV, EPS1, VAR, RSTD)
                TT(CVN, CVN, over(RSTD, CC), ALU.mult).then_inc(cvn_ready, 1)
                for u in range(4):
                    c = slice(2 * u, 2 * u + 2)
                    if u == 0:
                        moved(UN_POOL + 3)
                    TT(YB[:, c], YB[:, c], GB[:, c], ALU.mult)
                    moved(UN_CONV + u)
                    TT(YA[:, c], YA[:, c], GA[:, c], ALU.mult)
                    dve.drain()
                    TT(MIX[:, c], YA[:, c], YB[:, c], ALU.add)
                dve.drain().then_inc(mixed_ready, 1)
                for u in range(4):
                    moved(UN_OUT + u)
                    c = slice(2 * u, 2 * u + 2)
                    TT(xT[:, c, :], xT[:, c, :], TMP1[:, c], ALU.add)
                dve.drain()
                squares(xT[:, :, :], SQ)
                rstd(l * 4 + 4, l * 3 + 3, stat[:, 0:T], D, EPS1, VAR, RSTD)
                modulated(H, gain[:, KC:2 * KC], mod[:, 3 * KC:4 * KC])
                dve.drain().then_inc(h2_ready, 1)
                V.tensor_copy(x_hi, H)
                dve.drain()
                TT(x_lo, H, x_hi.bitcast(F32), ALU.subtract).then_inc(h2_split, 1)
                number = l * (2 * PAIRS1)
                low_part(0, J_MOE, number)
                low_part(1, J_MOE, number)

                def r(a, *shape):
                    n = int(np.prod(shape))
                    v = RT[:, a:a + n]
                    if len(shape) == 2:
                        return v.rearrange("p (h n) -> p h n", h=shape[0])
                    if len(shape) == 3:
                        return v.rearrange("p (h g n) -> p h g n", h=shape[0], g=shape[1])
                    return v

                lg = r(0, TH, NR)
                eg, e8 = r(100, TH, NG), r(200, TH, EPG)
                gp8, g8, e8t = r(120, TH, 8), r(140, TH, 8), r(160, TH, 8)
                gi, ei = r(220, TH * 8).bitcast(U32), r(240, TH * 8).bitcast(U32)
                gmax, gsum = r(260, TH), r(264, TH)
                emax, esum, den = r(268, TH), r(272, TH), r(276, TH)
                gif, eif = r(280, TH, 8), r(300, TH, 8)
                og, sel8 = r(320, TH, NG), r(340, TH, EPG)
                prod = r(400, TH, NG, EPG)
                o1, o2, comb = r(500, TH, EPG), r(520, TH, EPG), r(540, TH, EPG)

                def wide(ap, n):
                    return ap.unsqueeze(2).to_broadcast([P, TH, n])

                moved(UN_ROUT)
                TT(lg, lg, par(par1, COL1, "router_b").unsqueeze(1).to_broadcast([P, TH, NR]), ALU.add)
                V.memset(gp8, -1.0)
                dve.drain()
                V.tensor_reduce(gmax, lg[:, :, 0:NG], AX.X, ALU.max)
                dve.drain()
                TT(eg, lg[:, :, 0:NG], wide(gmax, NG), ALU.subtract).then_inc(rl_ready, 1)
                dve.wait_ge(re_ready, l * 2 + 1)
                V.tensor_reduce(gsum, eg, AX.X, ALU.add)
                dve.drain()
                V.reciprocal(gsum, gsum)
                dve.drain()
                TT(gp8[:, :, 0:NG], eg, wide(gsum, NG), ALU.mult)
                dve.drain()
                for th in range(TH):
                    V.max(g8[:, th, :], gp8[:, th, :])
                dve.drain()
                for th in range(TH):
                    V.max_index(gi[:, th * 8:th * 8 + 8], g8[:, th, :], gp8[:, th, :])
                dve.drain()
                V.tensor_copy(gif, gi.rearrange("p (h n) -> p h n", h=TH))
                dve.drain()
                iot = iota[:, 0:8].unsqueeze(1).to_broadcast([P, TH, 8])
                TT(og, iot[:, :, 0:NG], gif[:, :, 0:1].to_broadcast([P, TH, NG]), ALU.is_equal)
                dve.drain()
                lge = lg[:, :, NG:NR].rearrange("p h (g n) -> p h g n", g=NG)
                TT(prod, lge, og.unsqueeze(3).to_broadcast([P, TH, NG, EPG]), ALU.mult)
                dve.drain()
                V.tensor_reduce(sel8, prod.rearrange("p h g n -> p h n g"), AX.X, ALU.add)
                dve.drain()
                V.tensor_reduce(emax, sel8, AX.X, ALU.max)
                dve.drain()
                TT(e8, sel8, wide(emax, EPG), ALU.subtract).then_inc(rl_ready, 1)
                dve.wait_ge(re_ready, l * 2 + 2)
                V.tensor_reduce(esum, e8, AX.X, ALU.add)
                dve.drain()
                V.reciprocal(esum, esum)
                dve.drain()
                TT(e8, e8, wide(esum, EPG), ALU.mult)
                dve.drain()
                for th in range(TH):
                    V.max(e8t[:, th, :], e8[:, th, :])
                dve.drain()
                for th in range(TH):
                    V.max_index(ei[:, th * 8:th * 8 + 8], e8t[:, th, :], e8[:, th, :])
                TT(den, e8t[:, :, 0], e8t[:, :, 1], ALU.add)
                dve.drain()
                V.tensor_copy(eif, ei.rearrange("p (h n) -> p h n", h=TH))
                V.reciprocal(den, den)
                dve.drain()
                TT(o1, iot, eif[:, :, 0:1].to_broadcast([P, TH, 8]), ALU.is_equal)
                TT(o2, iot, eif[:, :, 1:2].to_broadcast([P, TH, 8]), ALU.is_equal)
                TT(den, den, g8[:, :, 0], ALU.mult)
                dve.drain()
                TT(o1, o1, o2, ALU.add)
                TT(comb, e8, wide(den, EPG), ALU.mult)
                dve.drain()
                TT(comb, comb, o1, ALU.mult)
                dve.drain()
                cm = CMB.rearrange("p h (g n) -> p h g n", g=NG)
                for th in range(TH):
                    TT(cm[:, th], og[:, th].unsqueeze(2).to_broadcast([P, NG, EPG]),
                       comb[:, th].unsqueeze(1).to_broadcast([P, NG, EPG]), ALU.mult)
                dve.drain()
                def diagonal(e):
                    for th in range(TH):
                        last = TS(DIAG[:, th, :], ident[:, :], CMB[:, th, bass.ds(e, 1)], None, ALU.mult)
                    last.then_inc(diag_ready, 1)

                def expert_act(e):
                    dve.wait_ge(silu_done, l * NE + e + 2)
                    dve.wait_ge(up_done, l * NE + e + 1)
                    TT(GU, SGM, U_PS[:, :].rearrange("p (c t) -> p c t", c=2), ALU.mult)
                    dve.drain()
                    TT(GU, GU, C_PS[:, 0:T].unsqueeze(1).to_broadcast([P, 2, T]), ALU.mult)
                    dve.drain()
                    V.tensor_copy(eact[:, 0], GU)
                    dve.drain()
                    TT(eact[:, 1], GU, eact[:, 0].bitcast(F32), ALU.subtract).then_inc(eact_ready, 1)

                low_part(2, J_MOE + 1, number)
                low_part(3, J_MOE + 1, number)
                diagonal(0)
                low_part(4, J_MOE + 2, number)
                with dve.Fori(0, NE - 1) as i:
                    low_part(5, J_MOE + 2, number + i * 6)
                    expert_act(i)
                    low_part(6, J_MOE + 3, number + i * 6)
                    low_part(7, J_MOE + 3, number + i * 6)
                    diagonal(i + 1)
                    low_part(8, J_MOE + 4, number + i * 6)
                    low_part(9, J_MOE + 4, number + i * 6)
                    low_part(10, J_MOE + 5, number + i * 6)
                low_part(2 * PAIRS1 - 1, J_MOE + PAIRS1 - 1, number)
                expert_act(NE - 1)
                dve.wait_ge(moe_out, l + 1)
                TT(xT[:, :, :], xT[:, :, :], TMP1, ALU.add)
                dve.drain().then_inc(layer_end1, 1)

            squares(xT[:, :, :], SQ)
            rstd(L * 4 + 1, L * 3 + 1, stat[:, 0:T], D, EPS1, VAR, RSTD)
            modulated(H, par(cst, COLC, "final_g"), None)
            dve.drain().then_inc(layer_end2, 1)

            def split_x(src, chunks):
                V.tensor_copy(x_hi[:, chunks, :], src[:, chunks, :])
                dve.drain()
                return TT(x_lo[:, chunks, :], src[:, chunks, :], x_hi[:, chunks, :].bitcast(F32), ALU.subtract)

            split_x(xT, slice(0, KC)).then_inc(x2_ready, 1)

            def layer_norm(stat_value, root_value, tmp, g, b):
                for c in halves_of(YC):
                    STT(YC[:, c], xT[:, c], ALPHA, tmp[:, c], ALU.mult, ALU.add).then_inc(stat_in, 1)
                dve.wait_ge(stat_out, stat_value)
                TS(MEAN2[:, 0, :], stat[:, 0:T], 1.0 / D, None, ALU.mult)
                dve.drain()
                TT(YC, YC, over(MEAN2, KC), ALU.subtract)
                dve.drain()
                squares(YC, SQ2)
                rstd(stat_value + 1, root_value, stat[:, 0:T], D, EPS2, VAR2, RSTD2)
                TT(YC, YC, over(RSTD2, KC), ALU.mult)
                dve.drain()
                for k in range(KC):
                    TS(xT[:, k, :], YC[:, k, :], g[:, k:k + 1], b[:, k:k + 1], ALU.mult, ALU.add)
                dve.drain()

            with dve.Fori(0, L) as l:
                units = l * UNITS2 + BASE2
                stat0 = l * 4 + (L * 4 + 1)
                root0 = l * 2 + (L * 3 + 1)

                def moved2(u):
                    dve.wait_ge(lin_free, units + u + 1 + LB)

                number = l * (2 * PAIRS2) + L * 2 * PAIRS1
                for c in range(2 * IN2_T + 2):
                    low_part(c, c // 2, number)
                dve.wait_ge(par2_loaded, l * 16 + 16)
                lq = par(par2, COL2, "lam_q")
                TT(LAM_PRODUCTS, lq, par(par2, COL2, "lam_k"), ALU.mult)
                dve.drain()
                V.tensor_reduce(lamb[:, 0:2], LAM_PRODUCTS.rearrange("p (q n) -> p q n", q=2), AX.X, ALU.add)\
                    .then_inc(lam_in, 1)
                dve.wait_ge(lam_exp, l + 1)
                TT(lamb[:, 4:5], lamb[:, 3:4], lamb[:, 2:3], ALU.subtract)
                dve.drain()
                TT(lamb[:, 5:6], lamb[:, 4:5], par(par2, COL2, "lambda_init"), ALU.subtract)
                dve.drain()
                dve.wait_ge(alibi_made, l + 1)

                def shifted(d):
                    b, h = divmod(d, DH)
                    kv = (b + 1) * P
                    s = SCO[d % 2]
                    dve.wait_ge(sc_done, l * 8 + d + 1)
                    STT(s[:, :, 0:kv], acc[:, 2 * (d % 2):2 * (d % 2) + 2, 0:kv], HD ** -0.5,
                        ALIBI[:, h, b, 0:kv].unsqueeze(1).to_broadcast([P, 2, kv]), ALU.mult, ALU.add)
                    dve.drain()
                    a = 4 * (d % 2)
                    V.tensor_reduce(rsm[:, a:a + 2], s[:, :, 0:kv], AX.X, ALU.max)
                    dve.drain()
                    TS(rsm[:, a:a + 2], rsm[:, a:a + 2], -1.0, None, ALU.mult).then_inc(smax_ready, 1)

                def combined(d):
                    b, h = divmod(d, DH)
                    kv = (b + 1) * P
                    a = 4 * (d % 2)
                    dve.wait_ge(e_ready, l * 8 + d + 1)
                    V.reciprocal(rsm[:, a + 2:a + 4], rsm[:, a + 2:a + 4])
                    dve.drain()
                    TT(rsm[:, a + 3:a + 4], rsm[:, a + 3:a + 4], lamb[:, 5:6], ALU.mult)
                    TS(EXO[d % 2][:, 0, 0:kv], EXO[d % 2][:, 0, 0:kv], rsm[:, a + 2:a + 3], None, ALU.mult)
                    dve.drain()
                    if d >= 2:
                        dve.wait_ge(tr_done, l * 8 + d - 1)
                    STT(ATT[d % 2][:, 0, 0:kv], EXO[d % 2][:, 1, 0:kv], rsm[:, a + 3:a + 4],
                        EXO[d % 2][:, 0, 0:kv], ALU.mult, ALU.add).then_inc(att_ready, 1)

                def sb_scaled(hh):
                    dve.wait_ge(z_done, l * SH + hh + 1)
                    TS(ZS[:, hh], sb_bank[hh % 2][:, 0:SW], HD ** -0.5, None, ALU.mult)
                    dve.drain()
                    STT(LS[:, hh], ZS[:, hh], -1.0, ZS[:, hh], ALU.mult, ALU.min).then_inc(na_ready, 1)

                def sb_log_sigmoids(hh):
                    dve.wait_ge(l1_ready, l * SH + hh + 1)
                    STT(WW[:, hh], ZS[:, hh], 0.0, LS[:, hh], ALU.min, ALU.subtract)
                    dve.drain()
                    TT(LS[:, hh], WW[:, hh], ZS[:, hh], ALU.subtract)
                    dve.drain()
                    TT(LS[:, hh], LS[:, hh], MASK, ALU.mult).then_inc(lf_ready, 1)

                def sb_exponent(hh):
                    dve.wait_ge(lat_done, l * SH + hh + 1)
                    TT(WW[:, hh], WW[:, hh], sb_bank[hh % 2][:, 0:SW], ALU.add).then_inc(wl_ready, 1)

                def sb_masked(hh):
                    dve.wait_ge(we_ready, l * SH + hh + 1)
                    TT(WW[:, hh], WW[:, hh], MASK, ALU.mult).then_inc(ww_ready, 1)

                shifted(0)
                for d in range(8):
                    sb_scaled(d)
                    if d + 1 < 8:
                        shifted(d + 1)
                    if d >= 1:
                        sb_exponent(d - 1)
                    combined(d)
                    sb_log_sigmoids(d)
                    if d >= 1:
                        sb_masked(d - 1)
                sb_exponent(SH - 1)
                sb_masked(SH - 1)
                dve.wait_ge(dpv_out, l + 1)
                TT(DSQ, DIFF, DIFF, ALU.mult).then_inc(dsq_ready, 1)
                for w4 in range(2):
                    dve.wait_ge(spv_out, l * 2 + w4 + 1)
                    split_x(MIXT, slice(4 + 2 * w4, 6 + 2 * w4))
                dve.wait_ge(dss_done, l + 1)
                TS(DRS, accT[:, 4:8, :], 1.0 / (2 * HD), EPS2, ALU.mult, ALU.add).then_inc(dvar_ready, 1)
                dve.wait_ge(dstd_ready, l + 1)
                V.reciprocal(DRS, DRS)
                dve.drain()
                TT(DIFF, DIFF, DRS, ALU.mult)
                dve.drain()
                TS(MIXT[:, 0:4], DIFF, par(par2, COL2, "subln_g"), par(par2, COL2, "keep"), ALU.mult, ALU.mult)
                dve.drain()
                split_x(MIXT, slice(0, 4)).then_inc(mixt_split, 1)
                for c in range(2 * J_WO + 2, 2 * J_WQ + 2):
                    low_part(c, c // 2, number)
                moved2(UN_WO + 3)
                layer_norm(stat0 + 1, root0 + 1, TMP2, par(par2, COL2, "ln1_g"), par(par2, COL2, "ln1_b"))
                split_x(xT, slice(0, KC)).then_inc(x3_split, 1)
                for c in range(2 * J_WQ + 2, 2 * LIN2_T):
                    low_part(c, c // 2, number)
                number = l * (2 * PAIRS2) + 2 * (L * PAIRS1 + LIN2_T)

                def top16(vals, work, n, step, topv, topi):
                    for s in range(n):
                        V.max(topv[:, s, 0:8], vals[:, s, :])
                        if s % step == step - 1:
                            yield
                    dve.drain()
                    for s in range(n):
                        V.max_index(topi[:, s, 0:8], topv[:, s, 0:8], vals[:, s, :])
                        V.match_replace(work[:, s, :], topv[:, s, 0:8], vals[:, s, :], -3.0e38)
                        if s % (step // 2) == step // 2 - 1:
                            yield
                    dve.drain()
                    for s in range(n):
                        V.max(topv[:, s, 8:16], work[:, s, :])
                        if s % step == step - 1:
                            yield
                    dve.drain()
                    for s in range(n):
                        V.max_index(topi[:, s, 8:16], topv[:, s, 8:16], work[:, s, :])
                        if s % step == step - 1:
                            yield
                    dve.drain()

                def routing():
                    for th in range(TH):
                        yield from top16(SC[th], WORK, HP, 4, TOPV, TOPI)
                        V.tensor_copy(TOPF.rearrange("p h q j -> p (h q) j"), TOPI)
                        tv = TOPV.rearrange("p (h q) j -> p h q j", q=2)
                        for h in range(PH):
                            TT(CAND[:, h, :].rearrange("p (a b) -> p a b", a=16),
                               tv[:, h, 0, :].unsqueeze(2).to_broadcast([P, 16, 16]),
                               tv[:, h, 1, :].unsqueeze(1).to_broadcast([P, 16, 16]), ALU.add)
                            if h % 2 == 1:
                                yield
                        dve.drain()
                        yield from top16(CAND, CWORK, PH, 2, BV, BPH)
                        TT(BE[:, th], BV, BV[:, :, 0:1].to_broadcast([P, PH, PTOP]), ALU.subtract)
                        TS(BA, BP, 4, None, ALU.logical_shift_right)
                        TS(BB, BP, 15, None, ALU.bitwise_and)
                        dve.drain()
                        V.tensor_copy(BF[:, 0, :], BA)
                        V.tensor_copy(BF[:, 1, :], BB)
                        dve.drain()
                        yield
                        for q in range(2):
                            for h in range(PH):
                                TT(EQH[:, h], iota[:, 0:16].unsqueeze(1).to_broadcast([P, 16, 16]),
                                   BF[:, q, 16 * h:16 * h + 16].unsqueeze(2).to_broadcast([P, 16, 16]), ALU.is_equal)
                                if h % 2 == 1:
                                    yield
                            dve.drain()
                            for h in range(PH):
                                TT(EQH[:, h], EQH[:, h], TOPF[:, h, q, :].unsqueeze(1).to_broadcast([P, 16, 16]),
                                   ALU.mult)
                                if h % 2 == 1:
                                    yield
                            dve.drain()
                            for a in range(4):
                                r_ = slice(a * NSEL // 4, (a + 1) * NSEL // 4)
                                V.tensor_reduce(picks[:, q, th, r_], EQS[:, r_, :], AX.X, ALU.add)
                                yield
                            dve.drain()

                moved2(UN_SC + 7)
                V.memset(BS, 0.0)
                work = routing()
                HEAD_C = HEAD * 6 - 1
                for c in range(HEAD_C):
                    low_part(c, J_U + c // 2, number)
                    next(work, None)
                    next(work, None)
                    if c == HEAD_C - 6:
                        assert next(work, "done") == "done"
                        dve.drain().then_inc(bl_ready, 1)
                dve.wait_ge(be_ready, l + 1)
                V.tensor_reduce(BS, BE, AX.X, ALU.add)
                dve.drain()
                V.reciprocal(BS, BS)
                dve.drain()
                for th in range(TH):
                    TT(picks[:, 2, th, :].rearrange("p (h j) -> p h j", h=PH), BE[:, th],
                       BS[:, th].unsqueeze(2).to_broadcast([P, PH, PTOP]), ALU.mult)
                dve.drain().then_inc(routed, 1)
                low_part(HEAD_C, J_U + HEAD_C // 2, number)
                with dve.Fori(HEAD, U_T // SLOTS) as i:
                    for c in range(2 * SLOTS):
                        low_part(c, J_U + c // 2, number + i * 6)
                for c in range(U_T // SLOTS * 6, 2 * U_T):
                    low_part(c, J_U + c // 2, number)

                def hot_rows(g, i):
                    at = bass.ds(i * 24 + 4 * g, 4)
                    TT(hot[:, g % HOTS], iota[:, :].unsqueeze(1).unsqueeze(1).to_broadcast([P, 2, 4, P]),
                       picksT[:, 0:2, at].unsqueeze(3).to_broadcast([P, 2, 4, P]), ALU.is_equal)\
                        .then_inc(hot_ready, 1)

                def apply_gates(g, i):
                    dve.wait_ge(g_done, l * G4 + i * 6 + g + 3)
                    a = arena[:, :, bass.ds(i * 24 + 4 * g, 4)]
                    TT(a, a, acc[:, g % HOTS, :].rearrange("p (t n) -> p n t", t=4), ALU.mult)

                dve.wait_ge(ptr_out, l + 1)
                dve.wait_ge(lin_free, units + UNITS2 + LB)
                V.memset(lamb[:, 8:9], 0.0)
                for g in range(HOTS):
                    hot_rows(g, 0)
                with dve.Fori(0, G4 // 6) as i:
                    for g in range(6):
                        apply_gates(g, i)
                        hot_rows(g + HOTS, i)
                for g in range(G4 // 6 * 6, G4):
                    apply_gates(g, 0)
                    if g + HOTS < G4:
                        hot_rows(g + HOTS, 0)
                dve.drain().then_inc(gated, 1)
                with dve.Fori(0, U_T // SLOTS) as i:
                    for c in range(2 * SLOTS):
                        low_part(c, J_V + c // 2, number + i * 6 + 2 * U_T, i * 6 + c)
                for c in range(U_T // SLOTS * 6, 2 * U_T):
                    low_part(c, J_V + c // 2, number + 2 * U_T, c)
                dve.wait_ge(v_out, l + 1)
                layer_norm(stat0 + 3, root0 + 2, TMP2, par(par2, COL2, "ln2_g"), par(par2, COL2, "ln2_b"))
                dve.drain().then_inc(layer_end2, 1)
                split_x(xT, slice(0, KC)).then_inc(x2_ready, 1)
            dve.drain().then_inc(final_ready, 1)


def kernel(**inputs):
    import concourse.bacc as _bacc
    from concourse.bass_utils import run_bass_kernel_spmd as _run

    f = {k: np.asarray(v) for k, v in inputs.items()}
    f32 = np.float32

    def cols(v):
        return v.reshape(-1, P).T

    def rows(v):
        return np.broadcast_to(v.reshape(1, -1), (P, v.size))

    def k_tiles(w, order=None):
        n = w.shape[1] // 256
        t = w.reshape(-1, P, n, 256).transpose(2, 1, 0, 3).reshape(n, P, -1)
        return t if order is None else t[order]

    stream = np.zeros((TILES, P, TILE), f32)
    at = 0

    def put(t):
        nonlocal at
        stream[at:at + t.shape[0], :, 0:t.shape[2]] = t
        at += t.shape[0]

    def halved(t):
        return t.reshape(-1, P, KC, 2, P).transpose(0, 1, 3, 2, 4).reshape(-1, P, TILE)

    for l in range(L):
        put(k_tiles(f["w_in"][l], [0, 2, 1, 3] + list(range(4, 14))))
        put(f["pool_w"][l].transpose(1, 0, 2).reshape(1, P, -1))
        put(f["w_conv_out"][l].reshape(CC, P, 2, 512).transpose(2, 1, 0, 3).reshape(2, P, -1))
        put(k_tiles(f["w_out"][l]))
        wg, wu, wd = f["w_expert_gate"][l], f["w_expert_up"][l], f["w_expert_down"][l]
        down = wd.reshape(NE, 2, P, 2, 512).transpose(0, 2, 3, 1, 4).reshape(NE, P, -1)
        put(halved(k_tiles(wg[0])))
        put(halved(k_tiles(wu[0])))
        for e in range(NE - 1):
            put(halved(k_tiles(wg[e + 1])))
            put(down[e:e + 1])
            put(halved(k_tiles(wu[e + 1])))
        put(down[NE - 1:NE])
    for l in range(L):
        t = k_tiles(f["w_in_2"][l])
        put(np.stack([t[j] if j in VALUE_TILES else halved(t[j])[0] for j in range(IN2_T)]))
        put(halved(k_tiles(f["w_o_2"][l])))
        put(halved(k_tiles(f["w_query_2"][l])))
        put(f["sub_keys_2"][l].transpose(3, 0, 1, 2).reshape(1, P, -1))
        u = f["expert_u_2"][l].reshape(P, U_T, 2, KC, P)
        put(u.transpose(1, 4, 2, 3, 0).reshape(U_T, P, -1))
        v = f["expert_v_2"][l].reshape(P, U_T, 2 * D)
        put(v.transpose(1, 0, 2))
    assert at == TILES

    par1 = np.stack([np.concatenate([
        cols(f["mixer_norm_g"][l]), cols(f["b_ada"][l]),
        f["conv_w"][l].T.reshape(CC, P, CK).transpose(1, 0, 2).reshape(P, -1), cols(f["conv_b"][l]),
        cols(f["conv_ln_g"][l]), cols(f["conv_ln_b"][l]), cols(f["b_conv_out"][l]), cols(f["pool_scale"][l]),
        cols(f["ffn_norm_g"][l]),
        np.concatenate([f["w_router_group"][l], f["w_router_expert"][l]], axis=1)
        .reshape(KC, P, NR).transpose(1, 0, 2).reshape(P, -1),
        rows(np.concatenate([f["b_router_group"][l], f["b_router_expert"][l]]))], axis=1) for l in range(L)])
    lambda_init = [0.8 - 0.6 * math.exp(-0.3 * l) for l in range(L)]
    par2 = np.stack([np.concatenate([
        cols(f["subln_g_2"][l]), np.full((P, 1), 1.0 - lambda_init[l], f32), np.full((P, 1), lambda_init[l], f32),
        cols(f["ln1_g_2"][l]), cols(f["ln1_b_2"][l]), cols(f["ln2_g_2"][l]), cols(f["ln2_b_2"][l]),
        rows(np.concatenate([f["lam_q1_2"][l], f["lam_q2_2"][l]])),
        rows(np.concatenate([f["lam_k1_2"][l], f["lam_k2_2"][l]]))], axis=1) for l in range(L)])
    consts = np.concatenate([cols(f["final_norm_g"]), cols(f["c"][0])], axis=1)
    inv = np.stack([1.0 / np.minimum(np.arange(1, T + 1), 2 << g) for g in range(CC)]).astype(f32)
    arrays = {
        "w_ada": np.concatenate([k_tiles(f["w_ada"][l]) for l in range(L)]), "wstream": stream,
        "x_in": f["x"][0].T.reshape(KC, P, T).transpose(1, 0, 2),
        "params1": par1, "params2": par2, "consts": consts,
        "inv_count": np.broadcast_to(inv[None], (P, CC, T)),
    }
    nc = _bacc.Bacc("TRN2", target_bir_lowering=False, num_devices=1)
    aps = {}
    for name in arrays:
        arrays[name] = np.ascontiguousarray(arrays[name])
        aps[name] = nc.dram_tensor(name, arrays[name].shape, F32, kind="ExternalInput").ap()
    out = nc.dram_tensor("out", (P, KC, T), F32, kind="ExternalOutput").ap()
    program(nc, aps["w_ada"], aps["wstream"], aps["x_in"], aps["params1"], aps["params2"], aps["consts"], aps["inv_count"], out)
    r = _run(nc, [arrays], core_ids=[0])
    return r.results[0]["out"].transpose(1, 0, 2).reshape(D, T).T.reshape(1, T, D)
```
